# Optimizing a Trainium2 kernel written in Bass

```python
import math
import jax
import jax.numpy as jnp
from jax import lax
import numpy as np
import jax, jax.numpy as jnp

D_MODEL = 1024
BATCH = 1
SEQ = 256
DEPTH = 4

N_MIXERS = 3
ROPE_THETA = 500000.0
EPS = 1e-6
Q_BLOCK = 128
MASK_VALUE = -1e30

A_HEADS = 8
A_HEAD_DIM = D_MODEL // A_HEADS // 2
A_V_DIM = 2 * A_HEAD_DIM
A_ROT = A_HEAD_DIM // 4

B_HEADS = 16
B_Q_RANK = 384
B_KV_RANK = 256
B_NOPE = 64
B_ROPE = 32
B_V = 64

C_GROUPS = ((128, 1), (512, 4), (2048, 16))
C_HEADS = 16
C_HEAD_DIM = 64
C_ROT = C_HEAD_DIM // 4
C_BLOCK = 64

FFN_DIM = -(-8 * D_MODEL // (3 * 256)) * 256

N_A = (DEPTH + 2) // 3
N_B = (DEPTH + 1) // 3
N_C = DEPTH // 3


def rms_norm(x, g):
    xf = x.astype(jnp.float32)
    y = xf * lax.rsqrt(jnp.mean(xf * xf, axis=-1, keepdims=True) + EPS) * g.astype(jnp.float32)
    return y.astype(x.dtype)

def rope_tables(seq_len, rot_dim):
    pos = jnp.arange(seq_len, dtype=jnp.float32)
    inv = ROPE_THETA ** (-jnp.arange(0, rot_dim, 2, dtype=jnp.float32) / rot_dim)
    ang = pos[:, None] * inv[None, :]
    return jnp.cos(ang), jnp.sin(ang)

def apply_rope(x, cos, sin):
    r = cos.shape[-1]
    shape = (x.shape[1],) + (1,) * (x.ndim - 3) + (r,)
    c = cos.reshape(shape)
    s = sin.reshape(shape)
    xf = x[..., :2 * r].astype(jnp.float32)
    x1, x2 = xf[..., :r], xf[..., r:]
    rot = jnp.concatenate([x1 * c - x2 * s, x2 * c + x1 * s], axis=-1).astype(x.dtype)
    return jnp.concatenate([rot, x[..., 2 * r:]], axis=-1)

def _to_blocks(t):
    b, h, s, d = t.shape
    return t.reshape(b, h, s // Q_BLOCK, Q_BLOCK, d).transpose(2, 0, 1, 3, 4)

def _from_blocks(t):
    nb, b, h, q, d = t.shape
    return t.transpose(1, 2, 0, 3, 4).reshape(b, h, nb * q, d)

def diff_attention(h, w_qkv, lam_q1, lam_k1, lam_q2, lam_k2, subln, w_o, lambda_init, cos, sin):
    B, S, _ = h.shape
    qk_w = 2 * A_HEADS * A_HEAD_DIM
    qkv = h @ w_qkv
    q = qkv[..., :qk_w].reshape(B, S, 2 * A_HEADS, A_HEAD_DIM)
    k = qkv[..., qk_w:2 * qk_w].reshape(B, S, 2 * A_HEADS, A_HEAD_DIM)
    v = qkv[..., 2 * qk_w:].reshape(B, S, A_HEADS, A_V_DIM)
    q = (apply_rope(q, cos, sin) * (A_HEAD_DIM ** -0.5)).transpose(0, 2, 1, 3)
    k = apply_rope(k, cos, sin).transpose(0, 2, 1, 3)
    v = v.transpose(0, 2, 1, 3)
    lam = (jnp.exp(jnp.sum(lam_q1.astype(jnp.float32) * lam_k1.astype(jnp.float32)))
           - jnp.exp(jnp.sum(lam_q2.astype(jnp.float32) * lam_k2.astype(jnp.float32)))
           + lambda_init)

    def block(qb):
        s = jnp.einsum('bhqd,bhkd->bhqk', qb, k).astype(jnp.float32)
        p = jax.nn.softmax(s, axis=-1).reshape(B, A_HEADS, 2, qb.shape[2], S)
        a = p[:, :, 0] - lam * p[:, :, 1]
        return jnp.einsum('bhqk,bhkd->bhqd', a.astype(v.dtype), v)

    o = _from_blocks(lax.map(block, _to_blocks(q)))
    o = rms_norm(o, subln) * (1.0 - lambda_init)
    o = o.transpose(0, 2, 1, 3).reshape(B, S, A_HEADS * A_V_DIM)
    return o @ w_o

def latent_attention(h, w_a, q_norm, kv_norm, w_qb, w_kvb, w_o, cos, sin):
    B, S, _ = h.shape
    a = h @ w_a
    q_lat = rms_norm(a[..., :B_Q_RANK], q_norm)
    kv_lat = rms_norm(a[..., B_Q_RANK:B_Q_RANK + B_KV_RANK], kv_norm)
    k_rope = apply_rope(a[..., B_Q_RANK + B_KV_RANK:], cos, sin)
    scale = (B_NOPE + B_ROPE) ** -0.5
    q = (q_lat @ w_qb).reshape(B, S, B_HEADS, B_NOPE + B_ROPE)
    q_nope = (q[..., :B_NOPE] * scale).transpose(0, 2, 1, 3)
    q_rope = (apply_rope(q[..., B_NOPE:], cos, sin) * scale).transpose(0, 2, 1, 3)
    kv = (kv_lat @ w_kvb).reshape(B, S, B_HEADS, B_NOPE + B_V)
    k_nope = kv[..., :B_NOPE].transpose(0, 2, 1, 3)
    v = kv[..., B_NOPE:].transpose(0, 2, 1, 3)

    def block(qs):
        qn, qr = qs
        s = (jnp.einsum('bhqd,bhkd->bhqk', qn, k_nope)
             + jnp.einsum('bhqr,bkr->bhqk', qr, k_rope)).astype(jnp.float32)
        p = jax.nn.softmax(s, axis=-1)
        return jnp.einsum('bhqk,bhkd->bhqd', p.astype(v.dtype), v)

    o = _from_blocks(lax.map(block, (_to_blocks(q_nope), _to_blocks(q_rope))))
    o = o.transpose(0, 2, 1, 3).reshape(B, S, B_HEADS * B_V)
    return o @ w_o

def _dilated_group(q, k, v, window, dilation):
    B, S, H, hd = q.shape
    radius = (window // 2) // dilation
    L = S // dilation
    nb = -(-L // C_BLOCK)
    Lp = nb * C_BLOCK

    def phase(t):
        t = t.reshape(B, L, dilation, H, hd).transpose(0, 2, 3, 1, 4)
        return jnp.pad(t, ((0, 0), (0, 0), (0, 0), (0, Lp - L), (0, 0)))

    def band(t):
        t = jnp.pad(phase(t), ((0, 0), (0, 0), (0, 0), (C_BLOCK, C_BLOCK), (0, 0)))
        t = t.reshape(B, dilation, H, nb + 2, C_BLOCK, hd)
        return jnp.concatenate([t[:, :, :, :-2], t[:, :, :, 1:-1], t[:, :, :, 2:]], axis=-2)

    qb = phase(q).reshape(B, dilation, H, nb, C_BLOCK, hd)
    kb, vb = band(k), band(v)
    blk = jnp.arange(nb)[:, None]
    qpos = blk * C_BLOCK + jnp.arange(C_BLOCK)[None, :]
    kpos = (blk - 1) * C_BLOCK + jnp.arange(3 * C_BLOCK)[None, :]
    mask = ((jnp.abs(qpos[:, :, None] - kpos[:, None, :]) <= radius)
            & (kpos[:, None, :] >= 0) & (kpos[:, None, :] < L))
    s = jnp.einsum('bphnqd,bphnkd->bphnqk', qb, kb).astype(jnp.float32)
    s = jnp.where(mask, s, MASK_VALUE)
    lse = jax.nn.logsumexp(s, axis=-1, keepdims=True)
    p = jnp.exp(s - lse)
    o = jnp.einsum('bphnqk,bphnkd->bphnqd', p.astype(v.dtype), vb)
    o = o.reshape(B, dilation, H, Lp, hd)[:, :, :, :L].transpose(0, 3, 1, 2, 4).reshape(B, S, H, hd)
    lse = lse[..., 0].reshape(B, dilation, H, Lp)[..., :L].transpose(0, 3, 1, 2).reshape(B, S, H)
    return o, lse

def dilated_attention(h, w_qkv, w_o, cos, sin):
    B, S, _ = h.shape
    G = len(C_GROUPS)
    qkv = (h @ w_qkv).reshape(B, S, G, 3, C_HEADS, C_HEAD_DIM)
    q = apply_rope(qkv[:, :, :, 0], cos, sin) * (C_HEAD_DIM ** -0.5)
    k = apply_rope(qkv[:, :, :, 1], cos, sin)
    v = qkv[:, :, :, 2]
    outs, lses = [], []
    for g, (window, dilation) in enumerate(C_GROUPS):
        o_g, l_g = _dilated_group(q[:, :, g], k[:, :, g], v[:, :, g], window, dilation)
        outs.append(o_g)
        lses.append(l_g)
    wts = jax.nn.softmax(jnp.stack(lses, axis=0), axis=0)
    o = jnp.sum(wts[..., None].astype(v.dtype) * jnp.stack(outs, axis=0), axis=0)
    return o.reshape(B, S, C_HEADS * C_HEAD_DIM) @ w_o

def swiglu(h, w_gu, w_out):
    gu = h @ w_gu
    return (jax.nn.silu(gu[..., :FFN_DIM]) * gu[..., FFN_DIM:]) @ w_out

def _w(k, shape, fan_in):
    return jax.random.normal(k, shape, jnp.float32) * (fan_in ** -0.5)

def _gain(k, shape):
    return 1.0 + 0.02 * jax.random.normal(k, shape, jnp.float32)

def first_inputs(seed: int = 0) -> dict:
    key = jax.random.key(seed)
    ks = jax.random.split(key, 21)
    D = D_MODEL
    a_qkv = 2 * 2 * A_HEADS * A_HEAD_DIM + A_HEADS * A_V_DIM
    c_qkv = len(C_GROUPS) * 3 * C_HEADS * C_HEAD_DIM
    return {
        'x': jax.random.normal(ks[0], (BATCH, SEQ, D), jnp.float32),
        'attn_norm': _gain(ks[1], (DEPTH, D)),
        'ffn_norm': _gain(ks[2], (DEPTH, D)),
        'final_norm': _gain(ks[3], (D,)),
        'a_w_qkv': _w(ks[4], (N_A, D, a_qkv), D),
        'a_lambda_q1': 0.1 * jax.random.normal(ks[5], (N_A, A_HEAD_DIM), jnp.float32),
        'a_lambda_k1': 0.1 * jax.random.normal(ks[6], (N_A, A_HEAD_DIM), jnp.float32),
        'a_lambda_q2': 0.1 * jax.random.normal(ks[7], (N_A, A_HEAD_DIM), jnp.float32),
        'a_lambda_k2': 0.1 * jax.random.normal(ks[8], (N_A, A_HEAD_DIM), jnp.float32),
        'a_subln': _gain(ks[9], (N_A, A_V_DIM)),
        'a_w_o': _w(ks[10], (N_A, A_HEADS * A_V_DIM, D), A_HEADS * A_V_DIM),
        'b_w_a': _w(ks[11], (N_B, D, B_Q_RANK + B_KV_RANK + B_ROPE), D),
        'b_q_norm': _gain(ks[12], (N_B, B_Q_RANK)),
        'b_kv_norm': _gain(ks[13], (N_B, B_KV_RANK)),
        'b_w_qb': _w(ks[14], (N_B, B_Q_RANK, B_HEADS * (B_NOPE + B_ROPE)), B_Q_RANK),
        'b_w_kvb': _w(ks[15], (N_B, B_KV_RANK, B_HEADS * (B_NOPE + B_V)), B_KV_RANK),
        'b_w_o': _w(ks[16], (N_B, B_HEADS * B_V, D), B_HEADS * B_V),
        'c_w_qkv': _w(ks[17], (N_C, D, c_qkv), D),
        'c_w_o': _w(ks[18], (N_C, C_HEADS * C_HEAD_DIM, D), C_HEADS * C_HEAD_DIM),
        'f_w_gu': _w(ks[19], (DEPTH, D, 2 * FFN_DIM), D),
        'f_w_out': _w(ks[20], (DEPTH, FFN_DIM, D), FFN_DIM),
    }

def first_block(x, attn_norm, ffn_norm, final_norm, a_w_qkv, a_lambda_q1, a_lambda_k1, a_lambda_q2,
              a_lambda_k2, a_subln, a_w_o, b_w_a, b_q_norm, b_kv_norm, b_w_qb, b_w_kvb, b_w_o,
              c_w_qkv, c_w_o, f_w_gu, f_w_out):
    S = x.shape[1]
    cos_p, sin_p = rope_tables(S, A_ROT)
    cos_b, sin_b = rope_tables(S, B_ROPE)
    for i in range(DEPTH):
        m, j = i % N_MIXERS, i // N_MIXERS
        h = rms_norm(x, attn_norm[i])
        if m == 0:
            lambda_init = 0.8 - 0.6 * math.exp(-0.3 * i)
            mix = diff_attention(h, a_w_qkv[j], a_lambda_q1[j], a_lambda_k1[j], a_lambda_q2[j],
                                 a_lambda_k2[j], a_subln[j], a_w_o[j], lambda_init, cos_p, sin_p)
        elif m == 1:
            mix = latent_attention(h, b_w_a[j], b_q_norm[j], b_kv_norm[j], b_w_qb[j], b_w_kvb[j],
                                   b_w_o[j], cos_b, sin_b)
        else:
            mix = dilated_attention(h, c_w_qkv[j], c_w_o[j], cos_p, sin_p)
        x = x + mix
        x = x + swiglu(rms_norm(x, ffn_norm[i]), f_w_gu[i], f_w_out[i])
    return rms_norm(x, final_norm)


DEPTH_2 = 2

POOL_GROUPS = 4
POOL_GROUP_DIM = 64
POOL_WINDOWS = (2, 4, 8, 16)
D_POOL = POOL_GROUPS * POOL_GROUP_DIM
D_CONV = 256
CONV_WIDTH = 31
N_HEADS = 8
N_KV_HEADS = 2
HEAD_DIM = 64
D_ATTN = N_HEADS * HEAD_DIM
D_KV = N_KV_HEADS * HEAD_DIM
IDX_HEADS = 8
IDX_DIM = 64
TOPK_MAX = 256
ROPE_THETA_2 = 10000.0
N_BRANCH = 3
IN_SIZES = (D_POOL, 2 * D_CONV, D_ATTN, D_KV, D_KV, IDX_HEADS * IDX_DIM, IDX_DIM, IDX_HEADS, N_BRANCH * D_MODEL)
D_IN = sum(IN_SIZES)
D_FF = 2816
FFN_CONV_WIDTH = 3
LN_EPS = 1e-5
DEEPNORM_ALPHA = (2 * DEPTH_2) ** 0.25
DEEPNORM_BETA = (8 * DEPTH_2) ** -0.25


def layer_norm(x, g, b):
    xf = x.astype(jnp.float32)
    mu = jnp.mean(xf, axis=-1, keepdims=True)
    var = jnp.mean(jnp.square(xf - mu), axis=-1, keepdims=True)
    y = (xf - mu) * lax.rsqrt(var + LN_EPS) * g.astype(jnp.float32) + b.astype(jnp.float32)
    return y.astype(x.dtype)

def rope(x, positions):
    half = x.shape[-1] // 2
    inv_freq = ROPE_THETA_2 ** (-jnp.arange(half, dtype=jnp.float32) / half)
    ang = positions.astype(jnp.float32)[..., None] * inv_freq
    cos = jnp.cos(ang)[:, :, None, :]
    sin = jnp.sin(ang)[:, :, None, :]
    xf = x.astype(jnp.float32)
    x1, x2 = xf[..., :half], xf[..., half:]
    return jnp.concatenate([x1 * cos - x2 * sin, x2 * cos + x1 * sin], axis=-1).astype(x.dtype)

def causal_dwconv(x, w, b):
    k, c = w.shape
    y = lax.conv_general_dilated(
        x, w[:, None, :].astype(x.dtype), window_strides=(1,), padding=[(k - 1, 0)],
        dimension_numbers=('NWC', 'WIO', 'NWC'), feature_group_count=c)
    return y + b

def split_cols(z, sizes):
    out, off = [], 0
    for s in sizes:
        out.append(z[..., off:off + s])
        off += s
    return out

def pool_mixer(u, pool_w, pool_scale):
    B, L, _ = u.shape
    uf = u.astype(jnp.float32).reshape(B, L, POOL_GROUPS, POOL_GROUP_DIM)
    cs0 = jnp.pad(jnp.cumsum(uf, axis=1), ((0, 0), (1, 0), (0, 0), (0, 0)))
    t = jnp.arange(L)
    pooled = []
    for g, win in enumerate(POOL_WINDOWS):
        start = jnp.maximum(t + 1 - win, 0)
        s = cs0[:, 1:, g] - cs0[:, start, g]
        cnt = (t + 1 - start).astype(jnp.float32)[None, :, None]
        pooled.append(s / cnt)
    mixed = jnp.stack(pooled, axis=2) - uf
    y = jnp.einsum('blgc,gcd->blgd', mixed, pool_w.astype(jnp.float32))
    return (y.reshape(B, L, D_POOL) * pool_scale.astype(jnp.float32)).astype(u.dtype)

def conformer_conv(u, dw_w, dw_b, ln_g, ln_b, w_pw):
    a, gate = jnp.split(u, 2, axis=-1)
    h = a * jax.nn.sigmoid(gate)
    h = causal_dwconv(h, dw_w, dw_b)
    h = jax.nn.silu(layer_norm(h, ln_g, ln_b))
    return h @ w_pw

def dsa_attention(q, k, v, q_idx, k_idx, w_idx):
    B, L = q.shape[0], q.shape[1]
    topk = min(TOPK_MAX, L // 4)
    n_blk = L // Q_BLOCK
    group = N_HEADS // N_KV_HEADS
    key_pos = jnp.arange(L)
    k_idx_f = k_idx.astype(jnp.float32)

    def block(i):
        q0 = i * Q_BLOCK
        qpos = q0 + jnp.arange(Q_BLOCK)
        qb = lax.dynamic_slice_in_dim(q, q0, Q_BLOCK, axis=1)
        qib = lax.dynamic_slice_in_dim(q_idx, q0, Q_BLOCK, axis=1).astype(jnp.float32)
        wib = lax.dynamic_slice_in_dim(w_idx, q0, Q_BLOCK, axis=1).astype(jnp.float32)
        logits = jnp.einsum('bqhd,bsd->bqsh', qib, k_idx_f)
        score = jnp.einsum('bqsh,bqh->bqs', jax.nn.relu(logits), wib)
        causal = key_pos[None, :] <= qpos[:, None]
        score = jnp.where(causal[None], score, -jnp.inf)
        _, idx = lax.top_k(score, topk)
        valid = idx <= qpos[None, :, None]
        k_sel = jax.vmap(lambda kk, ii: kk[ii])(k, idx)
        v_sel = jax.vmap(lambda vv, ii: vv[ii])(v, idx)
        qg = qb.reshape(B, Q_BLOCK, N_KV_HEADS, group, HEAD_DIM).astype(jnp.float32)
        s = jnp.einsum('bqngd,bqknd->bngqk', qg, k_sel.astype(jnp.float32)) * (HEAD_DIM ** -0.5)
        s = jnp.where(valid[:, None, None], s, -jnp.inf)
        p = jax.nn.softmax(s, axis=-1)
        o = jnp.einsum('bngqk,bqknd->bqngd', p, v_sel.astype(jnp.float32))
        return o.reshape(B, Q_BLOCK, D_ATTN).astype(q.dtype)

    out = lax.map(block, jnp.arange(n_blk))
    return out.transpose(1, 0, 2, 3).reshape(B, L, D_ATTN)

def token_mix(h, positions, w_in, b_in, pool_w, pool_scale, w_pool_out, conv_dw_w, conv_dw_b,
              conv_ln_g, conv_ln_b, w_conv_out, w_attn_out, w_o):
    B, L, _ = h.shape
    z = h @ w_in + b_in
    u_pool, u_conv, q, k, v, qi, ki, wi, gates = split_cols(z, IN_SIZES)
    q = rope(q.reshape(B, L, N_HEADS, HEAD_DIM), positions)
    k = rope(k.reshape(B, L, N_KV_HEADS, HEAD_DIM), positions)
    v = v.reshape(B, L, N_KV_HEADS, HEAD_DIM)
    qi = rope(qi.reshape(B, L, IDX_HEADS, IDX_DIM), positions) * (IDX_DIM ** -0.5)
    ki = rope(ki[:, :, None, :], positions)[:, :, 0, :]
    wi = wi * (IDX_HEADS ** -0.5)
    y_pool = pool_mixer(u_pool, pool_w, pool_scale) @ w_pool_out
    y_conv = conformer_conv(u_conv, conv_dw_w, conv_dw_b, conv_ln_g, conv_ln_b, w_conv_out)
    y_attn = dsa_attention(q, k, v, qi, ki, wi) @ w_attn_out
    g = jax.nn.sigmoid(gates.astype(jnp.float32)).reshape(B, L, N_BRANCH, D_MODEL).astype(h.dtype)
    merged = g[:, :, 0] * y_pool + g[:, :, 1] * y_conv + g[:, :, 2] * y_attn
    return merged @ w_o

def conv_ffn(h, w_up, ffn_dw_w, ffn_dw_b, w_down):
    u = causal_dwconv(h @ w_up, ffn_dw_w, ffn_dw_b)
    gate, val = jnp.split(u, 2, axis=-1)
    return (jax.nn.silu(gate) * val) @ w_down

def second_inputs(seed: int = 0) -> dict:
    key = jax.random.key(seed)
    ks = jax.random.split(key, 24)
    f32 = jnp.float32

    def nrm(k, shape, scale):
        return jax.random.normal(k, shape, f32) * scale

    return {
        "x": nrm(ks[0], (BATCH, SEQ, D_MODEL), 1.0),
        "positions": jnp.broadcast_to(jnp.arange(SEQ, dtype=jnp.int32), (BATCH, SEQ)),
        "ln_in_g": 1.0 + nrm(ks[1], (D_MODEL,), 0.02),
        "ln_in_b": nrm(ks[2], (D_MODEL,), 0.02),
        "w_in": nrm(ks[3], (DEPTH_2, D_MODEL, D_IN), D_MODEL ** -0.5),
        "b_in": nrm(ks[4], (DEPTH_2, D_IN), 0.02),
        "pool_w": nrm(ks[5], (DEPTH_2, POOL_GROUPS, POOL_GROUP_DIM, POOL_GROUP_DIM), POOL_GROUP_DIM ** -0.5),
        "pool_scale": 1.0 + nrm(ks[6], (DEPTH_2, D_POOL), 0.1),
        "w_pool_out": nrm(ks[7], (DEPTH_2, D_POOL, D_MODEL), D_POOL ** -0.5),
        "conv_dw_w": nrm(ks[8], (DEPTH_2, CONV_WIDTH, D_CONV), CONV_WIDTH ** -0.5),
        "conv_dw_b": nrm(ks[9], (DEPTH_2, D_CONV), 0.02),
        "conv_ln_g": 1.0 + nrm(ks[10], (DEPTH_2, D_CONV), 0.02),
        "conv_ln_b": nrm(ks[11], (DEPTH_2, D_CONV), 0.02),
        "w_conv_out": nrm(ks[12], (DEPTH_2, D_CONV, D_MODEL), D_CONV ** -0.5),
        "w_attn_out": nrm(ks[13], (DEPTH_2, D_ATTN, D_MODEL), D_ATTN ** -0.5),
        "w_o": nrm(ks[14], (DEPTH_2, D_MODEL, D_MODEL), DEEPNORM_BETA * D_MODEL ** -0.5),
        "ln1_g": 1.0 + nrm(ks[15], (DEPTH_2, D_MODEL), 0.02),
        "ln1_b": nrm(ks[16], (DEPTH_2, D_MODEL), 0.02),
        "w_up": nrm(ks[17], (DEPTH_2, D_MODEL, 2 * D_FF), D_MODEL ** -0.5),
        "ffn_dw_w": nrm(ks[18], (DEPTH_2, FFN_CONV_WIDTH, 2 * D_FF), FFN_CONV_WIDTH ** -0.5),
        "ffn_dw_b": nrm(ks[19], (DEPTH_2, 2 * D_FF), 0.02),
        "w_down": nrm(ks[20], (DEPTH_2, D_FF, D_MODEL), DEEPNORM_BETA * D_FF ** -0.5),
        "ln2_g": 1.0 + nrm(ks[21], (DEPTH_2, D_MODEL), 0.02),
        "ln2_b": nrm(ks[22], (DEPTH_2, D_MODEL), 0.02),
    }

def second_block(x, positions, ln_in_g, ln_in_b, w_in, b_in, pool_w, pool_scale, w_pool_out,
              conv_dw_w, conv_dw_b, conv_ln_g, conv_ln_b, w_conv_out, w_attn_out, w_o,
              ln1_g, ln1_b, w_up, ffn_dw_w, ffn_dw_b, w_down, ln2_g, ln2_b):
    h = layer_norm(x, ln_in_g, ln_in_b)
    for l in range(DEPTH_2):
        mix = token_mix(h, positions, w_in[l], b_in[l], pool_w[l], pool_scale[l], w_pool_out[l],
                        conv_dw_w[l], conv_dw_b[l], conv_ln_g[l], conv_ln_b[l], w_conv_out[l],
                        w_attn_out[l], w_o[l])
        h = layer_norm(DEEPNORM_ALPHA * h + mix, ln1_g[l], ln1_b[l])
        ffn = conv_ffn(h, w_up[l], ffn_dw_w[l], ffn_dw_b[l], w_down[l])
        h = layer_norm(DEEPNORM_ALPHA * h + ffn, ln2_g[l], ln2_b[l])
    return h


def setup_inputs(seed=0):
    out = dict(first_inputs(seed))
    for name, value in second_inputs(seed + 1).items():
        if name != "x":
            out[name + "_2"] = value
    return out


def reference(
    x, attn_norm, ffn_norm, final_norm, a_w_qkv, a_lambda_q1, a_lambda_k1, a_lambda_q2,
    a_lambda_k2, a_subln, a_w_o, b_w_a, b_q_norm, b_kv_norm, b_w_qb, b_w_kvb, b_w_o, c_w_qkv,
    c_w_o, f_w_gu, f_w_out, positions_2, ln_in_g_2, ln_in_b_2, w_in_2, b_in_2, pool_w_2,
    pool_scale_2, w_pool_out_2, conv_dw_w_2, conv_dw_b_2, conv_ln_g_2, conv_ln_b_2,
    w_conv_out_2, w_attn_out_2, w_o_2, ln1_g_2, ln1_b_2, w_up_2, ffn_dw_w_2, ffn_dw_b_2,
    w_down_2, ln2_g_2, ln2_b_2,
):
    x = first_block(
        x, attn_norm, ffn_norm, final_norm, a_w_qkv, a_lambda_q1, a_lambda_k1, a_lambda_q2,
        a_lambda_k2, a_subln, a_w_o, b_w_a, b_q_norm, b_kv_norm, b_w_qb, b_w_kvb, b_w_o,
        c_w_qkv, c_w_o, f_w_gu, f_w_out,
    )
    return second_block(
        x, positions_2, ln_in_g_2, ln_in_b_2, w_in_2, b_in_2, pool_w_2, pool_scale_2,
        w_pool_out_2, conv_dw_w_2, conv_dw_b_2, conv_ln_g_2, conv_ln_b_2, w_conv_out_2,
        w_attn_out_2, w_o_2, ln1_g_2, ln1_b_2, w_up_2, ffn_dw_w_2, ffn_dw_b_2, w_down_2,
        ln2_g_2, ln2_b_2,
    )


_drawn_inputs = setup_inputs


def setup_inputs(seed=0):
    import zlib

    import numpy as np

    out = dict(_drawn_inputs(seed))
    spreads = {}
    factors = {'final_norm': 2.731,
     'a_subln': 2.762,
     'b_q_norm': 8.0,
     'b_kv_norm': 7.553,
     'b_in_2': 5.649,
     'conv_dw_b_2': 8.0,
     'conv_ln_g_2': 8.0,
     'conv_ln_b_2': 21.382,
     'ffn_dw_b_2': 6.285,
     'pool_scale_2': 4.004}
    for name, (base, spread) in spreads.items():
        noise = np.random.default_rng([zlib.crc32(name.encode()), seed]).standard_normal(out[name].shape)
        drawn = base * np.exp(spread * noise) if base else spread * noise
        out[name] = jnp.asarray(drawn.astype(out[name].dtype))
    for name, factor in factors.items():
        out[name] = (out[name] * factor).astype(out[name].dtype)
    return out
```

```python
import math
from contextlib import ExitStack

import numpy as np
import concourse.bass as bass
from concourse import mybir

F32 = mybir.dt.float32
I32 = mybir.dt.int32
ALU = mybir.AluOpType
ACT = mybir.ActivationFunctionType
AX = mybir.AxisListType

P = 128
T = 256
NT = T // P
D = 1024
KT = D // P
FFN = 2816
FT = FFN // P
DEPTH, DEPTH_2 = 4, 2
EPS, LN_EPS = 1e-6, 1e-5
ALPHA = (2 * DEPTH_2) ** 0.25
A_HEADS = 8
B_HEADS, B_QR, B_KVR, B_NOPE, B_ROPE, B_V = 16, 384, 256, 64, 32, 64
C_HEADS, C_GROUPS = 16, 3
HD = 64
N_HEADS, N_KV, IDX_HEADS, TOPK = 8, 2, 8, 64
CONV_W, FCW = 31, 3
FF_2 = 2816
POOL_WINDOWS = (2, 4, 8, 16)
FILL, TAKEN, NEG = -3.0e38, float(np.float32(-3.3e38)), -1.0e30

SLOTS = 3
BANKS = 8

ROWS = [("attn_norm", 32), ("ffn_norm", 32), ("final_norm", 8), ("a_subln", 2), ("b_q_norm", 3),
        ("b_kv_norm", 2), ("ln_in_g_2", 8), ("ln_in_b_2", 8), ("ln1_g_2", 16), ("ln1_b_2", 16),
        ("ln2_g_2", 16), ("ln2_b_2", 16), ("pool_scale_2", 4), ("conv_dw_w_2", 2 * CONV_W * 2),
        ("conv_dw_b_2", 4), ("conv_ln_g_2", 4), ("conv_ln_b_2", 4), ("ffn_dw_w_2", 2 * FCW * 44),
        ("ffn_dw_b_2", 88)]
Z_POOL, Z_CONV, Z_Q, Z_K, Z_V, Z_QI, Z_KI, Z_WI, Z_GATE = 0, 256, 768, 1280, 1408, 1536, 2048, 2112, 2120
B_ROWS = ([(Z_POOL + P * i, P) for i in range(10)] + [(Z_K, HD), (Z_K + HD, HD)]
          + [(Z_QI + P * i, P) for i in range(4)] + [(Z_KI, HD)] + [(Z_GATE + P * i, P) for i in range(24)])
B_POOL, B_CONV, B_Q, B_K, B_QI, B_KI, B_GATE = 0, 2, 6, 10, 12, 16, 17


def row_starts():
    at, n = {}, 0
    for name, rows in ROWS:
        at[name] = n
        n += rows
    for l in range(DEPTH_2):
        at["b_in", l] = n
        n += len(B_ROWS)
    return at, n


ROW, N_ROWS = row_starts()
ROW_TILES = -(-N_ROWS // P)


class Item:

    def __init__(self, bank, free):
        self.bank, self.free, self.done, self.step_done, self.step_free = bank, free, 0, 0, 0


class Chunk:

    def __init__(self, loads, slot, landed):
        self.loads, self.slot, self.landed = loads, slot, landed
        self.done, self.step_done, self.step_landed = 0, 0, 0
        self.round, self.rounds, self.group = 0, 1, None


def build(nc, t, stages=99):
    with ExitStack() as ctx:
        def sb(name, shape, dt=F32):
            return ctx.enter_context(nc.sbuf_tensor(name, shape, dt))

        def sem(name):
            return ctx.enter_context(nc.semaphore(name))

        wring = [sb(f"wring{s}", [P, 4096]) for s in range(SLOTS)]
        xT = sb("xT", [P, KT, T])
        hT = sb("hT", [P, KT, T])
        sq = sb("sq", [P, KT, T])
        Q = sb("Q", [P, 6144])
        K = sb("K", [P, 6144])
        V = sb("V", [P, 6144])
        expo = [sb(f"expo{i}", [P, 1536]) for i in range(2)]
        expoT = [sb(f"expoT{i}", [P, 1536]) for i in range(2)]
        pre = [sb(f"pre{i}", [P, 2 * T]) for i in range(3)]
        rot = [sb(f"rot{i}", [P, 2 * T]) for i in range(2)]
        cmask = sb("cmask", [P, 1536])
        tab = sb("tab", [P, 6, T])
        tabk = sb("tabk", [P, 2, T])
        tabd = sb("tabd", [P, 4, T])
        rotm = sb("rotm", [P, 3, P])
        ident = sb("ident", [P, P])
        ones = sb("ones", [P, P])
        pcol = sb("pcol", [P, ROW_TILES * P])
        brow = sb("brow", [1, DEPTH_2, 136])
        inv_cnt = sb("inv_cnt", [P, 2, T])
        eps = sb("eps", [P, 4])
        std = sb("std", [P, 16])
        rs = sb("rs", [P, 16])
        negmax = [sb(f"negmax{i}", [P, 2]) for i in range(4)]
        esum = [sb(f"esum{i}", [P, 2]) for i in range(4)]
        erec = [sb(f"erec{i}", [P, 2]) for i in range(4)]
        lams = sb("lams", [P, 4])
        lame = sb("lame", [P, 4])
        neglam = sb("neglam", [P, 2])
        subg = sb("subg", [P, 2])
        invf = sb("invf", [P, 1])
        wi = sb("wi", [P, 2, 8])
        m8 = sb("m8", [P, 8])
        banks = [ctx.enter_context(nc.psum_tensor(f"bank{b}", [P, 512], F32)) for b in range(BANKS)]

        xrows = K[:, 0:2048].rearrange("p (t n) -> p t n", t=NT)
        prow = V[:, 0:ROW_TILES * P].rearrange("p (r n) -> p r n", n=P)
        hidden = Q[:, 0:FT * T].rearrange("p (m n) -> p m n", n=T)
        qT = Q[:].rearrange("p (m n) -> p m n", n=T)
        kT = K[:].rearrange("p (m n) -> p m n", n=T)
        vA = V[:, 0:2048].rearrange("p (t n) -> p t n", t=NT)
        vC = V[:].rearrange("p (t n) -> p t n", t=NT)
        kidT, kdT, qiT = qT[:, 4], qT[:, 5:7], qT[:, 7:11]
        vD = Q[:, 11 * T:11 * T + 256].rearrange("p (t n) -> p t n", t=NT)
        gates = V[:].rearrange("p (m n) -> p m n", n=T)
        PADW = 32
        pool_u = K[:, 0:2 * (T + PADW)].rearrange("p (m n) -> p m n", m=2)
        pool_w2 = K[:, 576:1152].rearrange("p (m n) -> p m n", m=2)
        conv_a = K[:, 1152:1664].rearrange("p (m n) -> p m n", m=2)
        conv_h = K[:, 1664:2240].rearrange("p (m n) -> p m n", m=2)
        conv_y = K[:, 2240:2752].rearrange("p (m n) -> p m n", m=2)
        mixed = K[:, 2752:3264].rearrange("p (m n) -> p m n", m=2)
        poolT = K[:, 3264:3776].rearrange("p (m n) -> p m n", m=2)
        convT = K[:, 3776:4288].rearrange("p (m n) -> p m n", m=2)
        score = K[:, 4288:4800].rearrange("p (t n) -> p t n", t=NT)
        work = K[:, 4800:5312].rearrange("p (t n) -> p t n", t=NT)
        pool_w4 = K[:, 5312:5888].rearrange("p (m n) -> p m n", m=2)
        relu = [expo[0][:, 0:512], expo[1][:, 0:512]]
        uval = [expoT[0][:, 512 * j:512 * (j + 1)] for j in range(3)]
        poolw = sb("poolw", [P, DEPTH_2, 2, P])
        oT = hT
        latT = V[:, 4096:4096 + 5 * T].rearrange("p (m n) -> p m n", n=T)
        kr = sq[:, 7, :]
        attnT = Q[:, 3072:4096].rearrange("p (m n) -> p m n", n=T)
        lamv = sq[:, 0:2, :].rearrange("p m n -> p (m n)").rearrange("p (v d) -> p v d", d=HD)
        lamp = sq[:, 2:3, :].rearrange("p m n -> p (m n)").rearrange("p (v d) -> p v d", d=HD)
        pos_i = hT[:, 0, :].bitcast(I32)

        pe_done = sem("pe_done")
        bank_free = [sem(f"bank_free{b}") for b in range(BANKS)]
        landed = [sem(f"weights_landed{s}") for s in range(SLOTS)]
        x_landed = sem("x_landed")
        consts_landed = sem("consts_landed")
        rows_landed = sem("rows_landed")
        lam_landed = sem("lam_landed")
        pos_landed = sem("pos_landed")
        poolw_zeroed = sem("poolw_zeroed")
        poolw_ready = sem("poolw_ready")
        out_stored = sem("out_stored")
        ident_ready = sem("ident_ready")
        eps_ready = sem("eps_ready")
        lam_sums = sem("lam_sums")
        lam_exps = sem("lam_exps")
        angles_ready = sem("angles_ready")
        sines_ready = sem("sines_ready")
        squares_ready = sem("squares_ready")
        rs_ready = sem("rs_ready")
        h_ready = sem("h_ready")
        centred = sem("centred")
        ln_ready = sem("ln_ready")
        y_ready = sem("y_ready")
        rot_ready = sem("rot_ready")
        kr_ready = sem("kr_ready")
        kr_spread = sem("kr_spread")
        negmax_ready = sem("negmax_ready")
        exp_ready = sem("exp_ready")
        probs_ready = sem("probs_ready")
        dve_step = sem("dve_step")
        hidden_ready = sem("hidden_ready")
        taps_started = sem("taps_started")
        gate_ready = sem("gate_ready")
        score_step = sem("score_step")
        score_masked = sem("score_masked")
        picked = sem("picked")
        keep_ready = sem("keep_ready")
        conv_out = sem("conv_out")
        mixed_ready = sem("mixed_ready")
        merged_ready = sem("merged_ready")

        def row_loads():
            out = []

            def add(at, src, c0=0, c1=P):
                n = src.shape[0]
                done = 0
                while done < n:
                    r = at + done
                    m = min(n - done, P - r % P)
                    out.append((prow[r % P:r % P + m, r // P, c0:c1], src[done:done + m, :]))
                    done += m

            for name, rows in ROWS:
                a = t[name]
                if len(a.shape) == 1:
                    a = a.rearrange("(r n) -> r n", n=P)
                elif len(a.shape) == 2:
                    a = a.rearrange("l (r n) -> (l r) n", n=P)
                else:
                    a = a.rearrange("l c (r n) -> (l c r) n", n=P)
                assert a.shape[0] == rows
                add(ROW[name], a)
            for l in range(DEPTH_2):
                b, at = t["b_in_2"][l], ROW["b_in", l]
                for first, n, col in ((B_POOL, 10, Z_POOL), (B_QI, 4, Z_QI), (B_GATE, 24, Z_GATE)):
                    add(at + first, b[col:col + n * P].rearrange("(r n) -> r n", n=P))
                for half in range(2):
                    add(at + B_K, b[Z_K:Z_K + 2 * HD].rearrange("(r n) -> r n", n=HD), HD * half, HD * half + HD)
                    add(at + B_KI, b[Z_KI:Z_KI + HD].rearrange("(r n) -> r n", n=HD), HD * half, HD * half + HD)
            return out

        block = ctx.enter_context(nc.Block())
        chunks, items = [], {}

        def phases():
            yield "start", 0
            n = 0
            for i in range(DEPTH):
                kind = "ABC"[i % 3]
                yield "rms", (i, "attn_norm", KT * i)
                yield kind, i
                yield "rms", (i, "ffn_norm", KT * i)
                yield "ffn", i
                n += 1
                if n >= stages:
                    break
            if n >= stages:
                yield "end", 0
                return
            yield "final", 0
            yield "ln", ("ln_in_g_2", "ln_in_b_2", 0)
            for l in range(DEPTH_2):
                yield "mix", l
                yield "ln", ("ln1_g_2", "ln1_b_2", KT * l)
                yield "ffn2", l
                yield "ln", ("ln2_g_2", "ln2_b_2", KT * l)
                n += 1
                if n >= stages:
                    break
            yield "end", 0

        def kxn(name, l, k0, k1, n0, n1):
            w = t[name] if l is None else t[name][l]
            return w.rearrange("(k p) n -> p k n", p=P)[:, k0:k1, n0:n1]

        def kxn_at(name, l, k0, k1, n0, width):
            w = t[name] if l is None else t[name][l]
            return w.rearrange("(k p) n -> p k n", p=P)[:, k0:k1, bass.ds(n0, width)]

        @block.tensor
        def _(pe):
            n_done = [0]
            uses = [0] * BANKS
            slot_loads = [0] * SLOTS
            tally = {}

            def count(s, n=1):
                tally[s.name] = tally.get(s.name, 0) + n
                return tally[s.name]

            def open_item(bank, released=True):
                if uses[bank]:
                    pe.wait_ge(bank_free[bank], uses[bank])
                uses[bank] += released
                return Item(bank, uses[bank])

            def close(ins, *what):
                n_done[0] += 1
                ins.then_inc(pe_done, 1)
                for w in what:
                    w.done = n_done[0]

            def new_chunk(loads):
                slot = len(chunks) % SLOTS
                slot_loads[slot] += len(loads)
                c = Chunk(loads, slot, 16 * slot_loads[slot])
                chunks.append(c)
                return c

            def wait_chunk(c):
                pe.wait_ge(landed[c.slot], c.landed)

            def wslot(c, k):
                return wring[c.slot][:, 0:k * (4096 // k)].rearrange("p (k n) -> p k n", k=k)

            def wtile(c, k, width):
                return wring[c.slot][:, 0:k * width].rearrange("p (k n) -> p k n", k=k)

            def product(bank, pairs, fresh=True):
                n = len(pairs)
                for i, (lhsT, rhs) in enumerate(pairs):
                    mm = nc.tensor.matmul(bank, lhsT, rhs, start=(fresh and i == 0), stop=(i == n - 1))
                return mm

            def linear(c, out, cols, src, k=KT, width=512, M=P, part=0):
                w = wtile(c, k, width)
                return product(out, [(w[:, j, cols:cols + M], src[:, j, :]) for j in range(k)])

            def stats(bank, col, src, tiles):
                for tt in range(NT):
                    mm = product(banks[bank][:, col + tt:col + tt + 1],
                                 [(src[:, j, tt * P:(tt + 1) * P], ones[:, 0:1]) for j in tiles])
                return mm

            def spread(bank, at, col):
                for tt in range(NT):
                    mm = nc.tensor.matmul(banks[bank][:, at + tt * P:at + (tt + 1) * P],
                                          rs[:, col + tt:col + tt + 1].to_broadcast([P, P]), ident[:],
                                          start=True, stop=True)
                return mm

            def h_wait():
                pe.wait_ge(h_ready, count(h_ready, KT))

            def start():
                it = {"x": [], "rows": []}
                pe.wait_ge(ident_ready, 3)
                pe.wait_ge(x_landed, 16)
                for j in range(4):
                    x = open_item(j)
                    for kk in range(2):
                        for tt in range(NT):
                            mm = nc.tensor.transpose(banks[j][:, kk * T + tt * P:kk * T + (tt + 1) * P],
                                                     xrows[:, tt, (2 * j + kk) * P:(2 * j + kk + 1) * P], ident[:])
                    close(mm, x)
                    it["x"].append(x)
                pe.wait_ge(rows_landed, 16 * n_row_loads)
                for j in range(0, ROW_TILES, 4):
                    r = open_item(4 + (j // 4) % 4)
                    for jj in range(j, min(j + 4, ROW_TILES)):
                        n = min(P, N_ROWS - jj * P)
                        mm = nc.tensor.transpose(banks[r.bank][:, (jj - j) * P:(jj - j) * P + n], prow[0:n, jj, :],
                                                 ident[0:n, 0:n])
                    close(mm, r)
                    it["rows"].append(r)
                items["start"] = it

            def rms(tag, tiles=range(KT), parts=4):
                pe.wait_ge(squares_ready, count(squares_ready, parts))
                s = open_item(6)
                close(stats(6, 0, sq, tiles), s)
                pe.wait_ge(rs_ready, count(rs_ready))
                b = open_item(7, released=False)
                close(spread(7, 0, 0), b)
                items[tag] = s, b
                return s, b

            def rotation(r, x, m, n=2 * T, lo=0, hi=P):
                pe.wait_ge(bank_free[x.bank], x.free)
                close(nc.tensor.matmul(banks[r.bank][lo:hi, 0:n], rotm[lo:hi, m, lo:hi],
                                       pre[x.pre][lo:hi, 0:n], start=True, stop=True), r)

            def residual_product(name, l, k, src, tag, bank0=0, width=512, first_wait=None):
                out = []
                groups = [(a, min(a + KT, k)) for a in range(0, k, KT)]
                for half in range(2):
                    pair = None
                    for gi, (k0, k1) in enumerate(groups):
                        c = new_chunk([((k1 - k0, 512, 0, 512), kxn(name, l, k0, k1, half * 512, half * 512 + 512))])
                        wait_chunk(c)
                        if pair is None:
                            pair = [open_item(bank0 + 2 * half), open_item(bank0 + 2 * half + 1)]
                        w = wtile(c, k1 - k0, 512)
                        for m in range(4):
                            o = banks[pair[m // 2].bank][:, (m % 2) * T:(m % 2 + 1) * T]
                            for j in range(k1 - k0):
                                mm = nc.tensor.matmul(o, w[:, j, m * P:(m + 1) * P], src[:, k0 + j, :],
                                                      start=(gi == 0 and j == 0 and m % 2 == 0),
                                                      stop=(gi == len(groups) - 1 and j == k1 - k0 - 1),
                                                      skip_group_check=True)
                            if gi == len(groups) - 1 and m % 2 == 1:
                                close(mm, pair[m // 2], *([c] if m == 3 else []))
                            elif m == 3:
                                close(mm, c)
                    out += pair
                items[tag] = out

            def ffn(name_up, name_down, l, tag):
                h_ok = h_wait if name_up == "f_w_gu" else y_wait
                h_ok()
                src = hT if name_up == "f_w_gu" else xT
                gbank, ubank = (0, 2, 4), (1, 3, 5)

                def step(c, g, u):
                    w = wtile(c, KT, 512)
                    for it, col in ((g, 0), (u, 256)):
                        for m in range(2):
                            mm = product(banks[it.bank][:, m * T:(m + 1) * T],
                                         [(w[:, j, col + m * P:col + (m + 1) * P], src[:, j, :]) for j in range(KT)])
                        close(mm, it, *([c] if it is u else []))

                def loads(i, j):
                    if isinstance(i, int):
                        a = (3 * i + j) * 256
                        return [((KT, 512, 0, 256), kxn(name_up, l, 0, KT, a, a + 256)),
                                ((KT, 512, 256, 256), kxn(name_up, l, 0, KT, FFN + a, FFN + a + 256))]
                    return [((KT, 512, 0, 256), kxn_at(name_up, l, 0, KT, i * 768 + j * 256, 256)),
                            ((KT, 512, 256, 256), kxn_at(name_up, l, 0, KT, i * 768 + FFN + j * 256, 256))]

                body = []
                done0, uses0 = n_done[0], list(uses)
                loads0 = list(slot_loads)
                rounds, per = 3, 6
                with pe.Fori(0, rounds) as i:
                    for j in range(3):
                        slot = len(chunks) % SLOTS
                        c = Chunk(loads, slot, 16 * (loads0[slot] + 2))
                        c.group, c.round, c.rounds, c.step_done, c.step_landed = done0, j, rounds, per, 32
                        chunks.append(c)
                        pe.wait_ge(landed[slot], i * 32 + c.landed)
                        pair = []
                        for b in (gbank[j], ubank[j]):
                            pe.wait_ge(bank_free[b], i + uses0[b])
                            x = Item(b, uses0[b] + 1)
                            x.step_done, x.step_free = per, 1
                            pair.append(x)
                        step(c, *pair)
                        body.append(pair)
                assert n_done[0] == done0 + per
                n_done[0] = done0 + per * rounds
                for j in range(3):
                    slot_loads[(chunks[-1].slot + 1 + j) % SLOTS] += 2 * rounds
                    uses[gbank[j]] += rounds
                    uses[ubank[j]] += rounds
                tail = []
                for j in range(2):
                    c = new_chunk(loads(3, j))
                    wait_chunk(c)
                    pair = [open_item(gbank[j]), open_item(ubank[j])]
                    step(c, *pair)
                    tail.append(pair)
                items[tag, "up"] = body, tail
                if name_up == "f_w_gu":
                    for b in ubank:
                        pe.wait_ge(bank_free[b], uses[b])
                else:
                    pe.wait_ge(hidden_ready, 3 + count(hidden_ready, 11))
                residual_product(name_down, l, FT, hidden, (tag, "down"))

            def y_wait():
                pe.wait_ge(y_ready, count(y_ready, KT))

            def attn_a(i):
                l = i // 3
                h_wait()
                xs, rr, vs = [], [], []
                pending = None
                for q in range(4):
                    c = new_chunk([((KT, 512, 0, 512), kxn("a_w_qkv", l, 0, KT, q * 512, q * 512 + 512))])
                    wait_chunk(c)
                    for m in range(2):
                        n = 2 * q + m
                        x = open_item(n % 3)
                        x.pre = n % 3
                        linear(c, banks[x.bank][:, 0:T], m * 256, hT)
                        mm = linear(c, banks[x.bank][:, T:2 * T], m * 256 + P, hT)
                        close(mm, x, *([c] if m == 1 else []))
                        xs.append(x)
                        if pending is not None:
                            r = open_item(3 + (n - 1) % 2)
                            rotation(r, pending, 0)
                            rr.append(r)
                        pending = x
                for q in range(2):
                    c = new_chunk([((KT, 512, 0, 512), kxn("a_w_qkv", l, 0, KT, 2048 + q * 512, 2048 + q * 512 + 512))])
                    wait_chunk(c)
                    w = wtile(c, KT, 512)
                    for tt in range(NT):
                        v = open_item(5 + tt)
                        mm = product(banks[v.bank][:], [(hT[:, j, tt * P:(tt + 1) * P], w[:, j, :]) for j in range(KT)])
                        close(mm, v, *([c] if tt == 1 else []))
                        vs.append(v)
                    if q == 0:
                        r = open_item(3 + 7 % 2)
                        rotation(r, pending, 0)
                        rr.append(r)
                items[i, "qk"], items[i, "rot"], items[i, "v"] = xs, rr, vs
                pe.wait_ge(rot_ready, count(rot_ready, 8))
                for v in vs[-2:]:
                    pe.wait_ge(bank_free[v.bank], v.free)
                S, TT, O = [], [], []
                for h in range(A_HEADS + 2):
                    if h < A_HEADS:
                        for sub in range(2):
                            s = open_item((2 * h + sub) % 4)
                            a = HD * sub
                            for tt in range(NT):
                                mm = nc.tensor.matmul(banks[s.bank][:, tt * T:(tt + 1) * T],
                                                      qT[a:a + HD, h, tt * P:(tt + 1) * P],
                                                      qT[a:a + HD, KT + h, :], start=True, stop=True)
                            close(mm, s)
                            S.append(s)
                    if 1 <= h <= A_HEADS:
                        TT.append(transposes(h - 1, NT, lambda tt, kt: expo[(h - 1) % 2][:, T * tt + kt * P:T * tt + (kt + 1) * P], 2, waits=1))
                    if h >= 2:
                        g = h - 2
                        if g % 2 == 0:
                            o = open_item(6 + (g // 2) % 2)
                            O.append(o)
                        pe.wait_ge(bank_free[TT[g][0].bank], TT[g][0].free)
                        for kt in range(NT):
                            mm = nc.tensor.matmul(banks[o.bank][:, (g % 2) * T:(g % 2 + 1) * T],
                                                  vA[:, kt, g * P:(g + 1) * P],
                                                  expoT[g % 2][:, kt * T:(kt + 1) * T],
                                                  start=(kt == 0), stop=(kt == NT - 1))
                        close(mm, o)
                        TT[g][0].used = n_done[0]
                items[i, "S"], items[i, "T"], items[i, "O"] = S, TT, O
                pe.wait_ge(squares_ready, count(squares_ready, 4))
                s = open_item(5)
                for h in range(A_HEADS):
                    mm = stats(5, 2 * h, sq, [h])
                close(mm, s)
                pe.wait_ge(rs_ready, count(rs_ready))
                sp_items = []
                for g in range(4):
                    b = open_item(g)
                    for hh in range(2):
                        mm = spread(g, hh * T, 2 * (2 * g + hh))
                    close(mm, b)
                    sp_items.append(b)
                items[i, "subln"] = s, sp_items
                for b in sp_items:
                    pe.wait_ge(bank_free[b.bank], b.free)
                residual_product("a_w_o", l, KT, oT, (i, "wo"))

            def transposes(h, nq, src, nk, waits=2):
                pe.wait_ge(probs_ready, count(probs_ready, waits))
                out = []
                for g in range(nk // 2):
                    it = open_item(4 + (h * (nk // 2) + g) % 2)
                    for kk in range(2):
                        for tt in range(nq):
                            mm = nc.tensor.transpose(banks[it.bank][:, kk * T + tt * P:kk * T + (tt + 1) * P],
                                                     src(tt, 2 * g + kk), ident[:])
                    close(mm, it)
                    out.append(it)
                return out

            def attn_64(i, heads, q_of, k_of, v_of, groups=1, tag=None):
                S, TT, O = [], [], []
                for h in range(heads + 2):
                    if h < heads:
                        mine = []
                        if groups == 1:
                            s = open_item(h % 4)
                            for tt in range(NT):
                                mm = nc.tensor.matmul(banks[s.bank][:, tt * T:(tt + 1) * T], q_of(h, 0, tt), k_of(h, 0),
                                                      start=True, stop=True)
                            close(mm, s)
                            mine.append(s)
                        else:
                            for n, parts in enumerate((((0, 0), (0, 1)), ((0, 2), (1, 2)), ((1, 0), (1, 1)))):
                                s = open_item((3 * h + n) % 4)
                                for y, (tt, g) in enumerate(parts):
                                    mm = nc.tensor.matmul(banks[s.bank][:, y * T:(y + 1) * T], q_of(h, g, tt), k_of(h, g),
                                                          start=True, stop=True)
                                close(mm, s)
                                mine.append(s)
                        S.append(mine)
                    if 1 <= h <= heads:
                        TT.append(transposes(h - 1, NT,
                                             lambda tt, kt: expo[(h - 1) % 2][:, T * groups * tt + kt * P:T * groups * tt + (kt + 1) * P],
                                             2 * groups, waits=1))
                    if h >= 2:
                        g = h - 2
                        if g % 4 == 0:
                            o = open_item(6 + (g // 4) % 2)
                            O.append(o)
                        for it in TT[g]:
                            pe.wait_ge(bank_free[it.bank], it.free)
                        a = HD * (g % 2)
                        for kt in range(2 * groups):
                            mm = nc.tensor.matmul(banks[o.bank][a:a + HD, (g // 2 % 2) * T:(g // 2 % 2 + 1) * T],
                                                  v_of(g, kt), expoT[g % 2][:, kt * T:(kt + 1) * T],
                                                  start=(kt == 0), stop=(kt == 2 * groups - 1))
                        close(mm, o)
                        for it in TT[g]:
                            it.used = n_done[0]
                items[tag, "S"], items[tag, "T"], items[tag, "O"] = S, TT, O
                for o in O[-2:]:
                    pe.wait_ge(bank_free[o.bank], o.free)

            def attn_b(i):
                h_wait()
                c = new_chunk([((KT, 512, 0, 512), kxn("b_w_a", 0, 0, KT, 0, 512))])
                wait_chunk(c)
                raw = [open_item(b) for b in range(3)]
                linear(c, banks[0][:, 0:T], 0, hT)
                close(linear(c, banks[0][:, T:2 * T], P, hT), raw[0])
                linear(c, banks[1][:, 0:T], 2 * P, hT)
                close(linear(c, banks[1][:, T:2 * T], 3 * P, hT), raw[1], c)
                c = new_chunk([((KT, 160, 0, 160), kxn("b_w_a", 0, 0, KT, 512, 672))])
                wait_chunk(c)
                linear(c, banks[2][:, 0:T], 0, hT, width=160)
                w = wtile(c, KT, 160)
                mm = product(banks[2][64:96, T:2 * T], [(w[:, j, P:160], hT[:, j, :]) for j in range(KT)])
                close(mm, raw[2], c)
                raw[2].pre = 2
                pe.wait_ge(squares_ready, count(squares_ready, 3))
                s = open_item(6)
                stats(6, 0, sq, range(3))
                close(stats(6, 2, sq, range(3, 5)), s)
                r = open_item(3)
                rotation(r, raw[2], 1, n=T, lo=64, hi=96)
                pe.wait_ge(rs_ready, count(rs_ready))
                b = open_item(7, released=False)
                spread(7, 0, 0)
                close(spread(7, T, 2), b)
                items[i, "raw"], items[i, "stat"], items[i, "krot"] = raw, (s, b), r
                pe.wait_ge(h_ready, count(h_ready, 5))
                xs, rr, ks, vs = [], [], [], []
                pending = None
                for q in range(2):
                    c = new_chunk([((3, 768, 0, 768), kxn("b_w_qb", 0, 0, 3, q * 768, q * 768 + 768))])
                    wait_chunk(c)
                    w = wtile(c, 3, 768)
                    for m in range(4):
                        n = 4 * q + m
                        x = open_item(n % 3)
                        x.pre = n % 3
                        for hh in range(2):
                            col = (2 * m + hh) * 96
                            mm = product(banks[x.bank][0:96, hh * T:(hh + 1) * T],
                                         [(w[:, j, col:col + 96], hT[:, j, :]) for j in range(3)])
                        close(mm, x, *([c] if m == 3 else []))
                        xs.append(x)
                        if pending is not None:
                            r = open_item(3 + (n - 1) % 2)
                            rotation(r, pending, 1, hi=96)
                            rr.append(r)
                        pending = x
                c = new_chunk([((2, 2048, 0, 2048), kxn("b_w_kvb", 0, 0, 2, 0, 2048))])
                wait_chunk(c)
                w = wtile(c, 2, 2048)
                for m in range(8):
                    x = open_item(5 + m % 2)
                    for hh in range(2):
                        col = (2 * m + hh) * P
                        mm = product(banks[x.bank][0:HD, hh * T:(hh + 1) * T],
                                     [(w[:, j, col:col + HD], hT[:, 3 + j, :]) for j in range(2)])
                    close(mm, x)
                    ks.append(x)
                    if m == 0:
                        r = open_item(3 + 7 % 2)
                        rotation(r, pending, 1, hi=96)
                        rr.append(r)
                for half in range(2):
                    for tt in range(NT):
                        v = open_item(half * 2 + tt)
                        mm = product(banks[v.bank][:].rearrange("p (h d) -> p h d", d=HD),
                                     [(hT[:, 3 + j, tt * P:(tt + 1) * P],
                                       w[:, j, half * 1024:half * 1024 + 1024].rearrange("p (h d) -> p h d", d=P)[:, :, HD:P])
                                      for j in range(2)])
                        close(mm, v, *([c] if half and tt else []))
                        vs.append(v)
                items[i, "qk"], items[i, "rot"], items[i, "k"], items[i, "v"] = xs, rr, ks, vs
                pe.wait_ge(rot_ready, count(rot_ready, 8))
                pe.wait_ge(kr_spread, count(kr_spread))
                for v in ks[-2:] + vs:
                    pe.wait_ge(bank_free[v.bank], v.free)
                attn_64(i, B_HEADS, lambda h, g, tt: qT[0:96, h, tt * P:(tt + 1) * P], lambda h, g: kT[0:96, h, :],
                        lambda h, kt: vA[:, kt, h * HD:(h + 1) * HD], tag=i)
                residual_product("b_w_o", 0, KT, oT, (i, "wo"))

            def attn_c(i):
                h_wait()
                done0, uses0, loads0 = n_done[0], list(uses), list(slot_loads)
                per = 20

                def take(bank, nth, i_):
                    n = per_bank[bank]
                    pe.wait_ge(bank_free[bank], i_ * n + (uses0[bank] + nth))
                    x = Item(bank, uses0[bank] + nth + 1)
                    x.step_done, x.step_free = per, n
                    return x

                per_bank = {0: 4, 1: 4, 2: 4, 3: 4, 4: 4}
                order = [n % 2 for n in range(8)]
                seen = {b: 0 for b in range(5)}
                xs, rr, vs = [], [], []
                with pe.Fori(0, C_GROUPS) as g:
                    pending = None

                    def tk(bank):
                        x = take(bank, seen[bank], g)
                        seen[bank] += 1
                        return x

                    for q in range(6):
                        slot = len(chunks) % SLOTS
                        nth = q // SLOTS

                        def loads(gi, j, q=q):
                            return [((KT, 512, 0, 512), kxn_at("c_w_qkv", 0, 0, KT, gi * 3072 + q * 512, 512))]

                        c = Chunk(loads, slot, 16 * (loads0[slot] + nth + 1))
                        c.group, c.round, c.rounds, c.step_done, c.step_landed = done0, q, C_GROUPS, per, 32
                        chunks.append(c)
                        pe.wait_ge(landed[slot], g * 32 + c.landed)
                        w = wtile(c, KT, 512)
                        if q < 4:
                            for m in range(2):
                                n = 2 * q + m
                                x = tk(n % 2)
                                x.pre = n % 2
                                linear(c, banks[x.bank][:, 0:T], m * 256, hT)
                                mm = linear(c, banks[x.bank][:, T:2 * T], m * 256 + P, hT)
                                close(mm, x, *([c] if m == 1 else []))
                                xs.append(x)
                                if pending is not None:
                                    r = tk(2 + (n - 1) % 2)
                                    pe.wait_ge(bank_free[pending.bank], g * pending.step_free + pending.free)
                                    close(nc.tensor.matmul(banks[r.bank][:], rotm[:, 0, :], pre[pending.pre][:],
                                                           start=True, stop=True), r)
                                    rr.append(r)
                                pending = x
                        else:
                            for tt in range(NT):
                                v = tk(4)
                                mm = product(banks[v.bank][:], [(hT[:, j, tt * P:(tt + 1) * P], w[:, j, :]) for j in range(KT)])
                                close(mm, v, *([c] if tt == 1 else []))
                                vs.append(v)
                            if q == 4:
                                r = tk(3)
                                pe.wait_ge(bank_free[pending.bank], g * pending.step_free + pending.free)
                                close(nc.tensor.matmul(banks[r.bank][:], rotm[:, 0, :], pre[pending.pre][:],
                                                       start=True, stop=True), r)
                                rr.append(r)
                assert n_done[0] == done0 + per and all(seen[b] == 4 for b in seen)
                n_done[0] = done0 + per * C_GROUPS
                for b in range(5):
                    uses[b] += 4 * C_GROUPS
                for s_ in range(SLOTS):
                    slot_loads[s_] += 2 * C_GROUPS
                items[i, "qk"], items[i, "rot"], items[i, "v"] = xs, rr, vs
                pe.wait_ge(rot_ready, count(rot_ready, 8 * C_GROUPS))
                pe.wait_ge(bank_free[4], uses[4])
                attn_64(i, C_HEADS,
                        lambda h, g, tt: qT[HD * (h % 2):HD * (h % 2) + HD, 8 * g + h // 2, tt * P:(tt + 1) * P],
                        lambda h, g: kT[HD * (h % 2):HD * (h % 2) + HD, 8 * g + h // 2, :],
                        lambda h, kt: vC[:, kt % 2, (kt // 2) * 1024 + h * HD:(kt // 2) * 1024 + (h + 1) * HD],
                        groups=C_GROUPS, tag=i)
                residual_product("c_w_o", 0, KT, oT, (i, "wo"))

            def final():
                rms("final")

            def ln(tag, n=KT, x_items=None):
                s = open_item(6)
                close(stats(6, 0, xT, range(KT)), s)
                pe.wait_ge(bank_free[6], s.free)
                m = open_item(5, released=False)
                close(spread(5, 0, 0), m)
                pe.wait_ge(squares_ready, count(squares_ready, 4))
                v = open_item(6)
                close(stats(6, 0, sq, range(KT)), v)
                pe.wait_ge(rs_ready, count(rs_ready))
                b = open_item(7, released=False)
                close(spread(7, 0, 0), b)
                count(ln_ready, KT)
                items[tag] = s, m, v, b

            def mix(l):
                y_wait()
                it = {}
                src = xT

                def two(c, bank, cols, width=512):
                    x = open_item(bank)
                    linear(c, banks[bank][:, 0:T], cols[0], src, width=width)
                    mm = linear(c, banks[bank][:, T:2 * T], cols[1], src, width=width)
                    return x, mm

                c = new_chunk([((KT, 512, 0, 512), kxn("w_in_2", l, 0, KT, 0, 512))])
                wait_chunk(c)
                it["pool"], mm = two(c, 0, (0, 128))
                close(mm, it["pool"])
                it["conv_a"], mm = two(c, 1, (256, 384))
                close(mm, it["conv_a"], c)
                c = new_chunk([((KT, 512, 0, 512), kxn("w_in_2", l, 0, KT, 512, 1024))])
                wait_chunk(c)
                it["conv_g"], mm = two(c, 2, (0, 128))
                close(mm, it["conv_g"])
                xs, rr = [], []
                x, mm = two(c, 3, (256, 384))
                close(mm, x, c)
                x.pre = 0
                xs.append(x)
                ld = [((KT, 512, 0, 256), kxn("w_in_2", l, 0, KT, Z_Q + 256, Z_Q + 512))]
                for g in range(2):
                    for z in range(2):
                        ld.append(((KT, 512, 256 + g * P + z * HD, HD), kxn("w_in_2", l, 0, KT, Z_K + g * HD, Z_K + (g + 1) * HD)))
                c = new_chunk(ld)
                wait_chunk(c)
                x, mm = two(c, 0, (0, 128))
                close(mm, x)
                x.pre = 1
                xs.append(x)
                r = open_item(4)
                rotation(r, xs[0], 2)
                rr.append(r)
                x, mm = two(c, 1, (256, 384))
                close(mm, x, c)
                x.pre = 2
                xs.append(x)
                r = open_item(5)
                rotation(r, xs[1], 2)
                rr.append(r)
                c = new_chunk([((KT, 512, 0, 512), kxn("w_in_2", l, 0, KT, Z_QI, Z_QI + 512))])
                wait_chunk(c)
                for m in range(2):
                    x, mm = two(c, 2 + m, (m * 256, m * 256 + 128))
                    close(mm, x, *([c] if m else []))
                    x.pre = m
                    xs.append(x)
                    r = open_item(4 + m)
                    rotation(r, xs[2 + m], 2)
                    rr.append(r)
                c = new_chunk([((KT, 264, 0, 128), kxn("w_in_2", l, 0, KT, Z_V, Z_V + 128)),
                               ((KT, 264, 128, 64), kxn("w_in_2", l, 0, KT, Z_KI, Z_KI + 64)),
                               ((KT, 264, 192, 64), kxn("w_in_2", l, 0, KT, Z_KI, Z_KI + 64)),
                               ((KT, 264, 256, 8), kxn("w_in_2", l, 0, KT, Z_WI, Z_WI + 8))])
                wait_chunk(c)
                w = wtile(c, KT, 264)
                x = open_item(0)
                mm = linear(c, banks[0][:, 0:T], 128, src, width=264)
                close(mm, x)
                x.pre = 2
                xs.append(x)
                r = open_item(4)
                rotation(r, xs[4], 2)
                rr.append(r)
                v = open_item(1)
                for tt in range(NT):
                    for (a, b, col, bc) in ((0, 128, 0, 0), (256, 264, 128, 128)):
                        o = banks[1][:, tt * 136 + bc:tt * 136 + bc + b - a]
                        for j in range(KT):
                            nc.tensor.matmul(o, src[:, j, tt * P:(tt + 1) * P], w[:, j, a:b], start=(j == 0), stop=False)
                        mm = nc.tensor.matmul(o, ones[0:1, :], brow[0:1, l, bc:bc + b - a], start=False, stop=True)
                close(mm, v, c)
                it["v"] = v
                r = open_item(5)
                rotation(r, xs[5], 2, n=T)
                rr.append(r)
                it["qk"], it["rot"] = xs, rr
                pe.wait_ge(rot_ready, count(rot_ready, 6))
                it["idx"] = []
                for h in range(IDX_HEADS):
                    s = open_item([0, 2, 3, 6][h % 4])
                    a = HD * (h % 2)
                    for tt in range(NT):
                        mm = nc.tensor.matmul(banks[s.bank][:, tt * T:(tt + 1) * T],
                                              qiT[a:a + HD, h // 2, tt * P:(tt + 1) * P], kidT[a:a + HD, :],
                                              start=True, stop=True)
                    close(mm, s)
                    it["idx"].append(s)
                done0, uses0, loads0 = n_done[0], list(uses), list(slot_loads)
                per, rounds = 6, 2
                body = []
                gb = (1, 4, 5, 7)
                order = [1, 4, 5, 1, 4, 5]
                seen = {b: 0 for b in order}
                with pe.Fori(0, rounds) as i_:
                    for j in range(3):
                        slot = len(chunks) % SLOTS

                        def loads(gi, jj, j=j):
                            return [((KT, 512, 0, 512), kxn_at("w_in_2", l, 0, KT, gi * 1536 + (Z_GATE + j * 512), 512))]

                        c = Chunk(loads, slot, 16 * (loads0[slot] + 1))
                        c.group, c.round, c.rounds, c.step_done, c.step_landed = done0, j, rounds, per, 16
                        chunks.append(c)
                        pe.wait_ge(landed[slot], i_ * 16 + c.landed)
                        for m in range(2):
                            b = order[2 * j + m]
                            pe.wait_ge(bank_free[b], i_ * 2 + (uses0[b] + seen[b]))
                            x = Item(b, uses0[b] + seen[b] + 1)
                            x.step_done, x.step_free = per, 2
                            seen[b] += 1
                            linear(c, banks[b][:, 0:T], m * 256, src)
                            mm = linear(c, banks[b][:, T:2 * T], m * 256 + P, src)
                            close(mm, x, *([c] if m else []))
                            body.append(x)
                assert n_done[0] == done0 + per
                n_done[0] = done0 + per * rounds
                for b in (1, 4, 5):
                    uses[b] += 2 * rounds
                for s_ in range(SLOTS):
                    slot_loads[s_] += rounds
                it["gates"] = body
                pe.wait_ge(mixed_ready, count(mixed_ready))
                if l == 0:
                    pe.wait_ge(poolw_ready, 32 * DEPTH_2 * 2)
                x = open_item(7)
                for m in range(2):
                    mm = nc.tensor.matmul(banks[7][:, m * T:(m + 1) * T], poolw[:, l, m, :], mixed[:, m, :],
                                          start=True, stop=True)
                close(mm, x)
                it["poolmix"] = x
                pe.wait_ge(conv_out, count(conv_out))
                s = open_item(6)
                close(stats(6, 0, conv_y, range(2)), s)
                pe.wait_ge(bank_free[6], s.free)
                m_ = open_item(5, released=False)
                close(spread(5, 0, 0), m_)
                pe.wait_ge(squares_ready, count(squares_ready))
                v = open_item(6)
                close(stats(6, 0, sq, range(2)), v)
                pe.wait_ge(rs_ready, count(rs_ready))
                b = open_item(7, released=False)
                close(spread(7, 0, 0), b)
                it["cln"] = s, m_, v, b
                pe.wait_ge(ln_ready, count(ln_ready, 2))
                attn_64(("m", l), N_HEADS,
                        lambda h, g, tt: qT[HD * (h % 2):HD * (h % 2) + HD, h // 2, tt * P:(tt + 1) * P],
                        lambda h, g: kdT[HD * (h % 2):HD * (h % 2) + HD, h // 4, :],
                        lambda h, kt: vD[:, kt, (h // 4) * HD:(h // 4 + 1) * HD], tag=("m", l))
                c = new_chunk([((2, 1024, 0, 1024), kxn("w_pool_out_2", l, 0, 2, 0, 1024)),
                               ((2, 1024, 0, 1024, 2048), kxn("w_conv_out_2", l, 0, 2, 0, 1024))])
                wait_chunk(c)
                pe.wait_ge(bank_free[it["poolmix"].bank], it["poolmix"].free)
                it["branch"] = []
                n = 0
                for br in range(2):
                    w = wring[c.slot][:, br * 2048:(br + 1) * 2048].rearrange("p (k n) -> p k n", k=2)
                    s_ = (poolT, convT)[br]
                    if br == 1:
                        pe.wait_ge(y_ready, count(y_ready, 2))
                    for m in range(4):
                        x = open_item(n % 4)
                        n += 1
                        for z in range(2):
                            col = (2 * m + z) * P
                            mm = product(banks[x.bank][:, z * T:(z + 1) * T], [(w[:, j, col:col + P], s_[:, j, :]) for j in range(2)])
                        close(mm, x, *([c] if br and m == 3 else []))
                        it["branch"].append(x)
                c = new_chunk([((4, 1024, 0, 1024), kxn("w_attn_out_2", l, 0, 4, 0, 1024))])
                wait_chunk(c)
                w = wtile(c, 4, 1024)
                for m in range(4):
                    x = open_item(n % 4)
                    n += 1
                    for z in range(2):
                        col = (2 * m + z) * P
                        mm = product(banks[x.bank][:, z * T:(z + 1) * T], [(w[:, j, col:col + P], attnT[:, j, :]) for j in range(4)])
                    close(mm, x, *([c] if m == 3 else []))
                    it["branch"].append(x)
                pe.wait_ge(merged_ready, count(merged_ready, 4))
                residual_product("w_o_2", l, KT, hT, (("m", l), "wo"), bank0=4)
                items["m", l] = it

            def end():
                if stages >= 5:
                    y_wait()
                else:
                    for x in items[last_add[0]]:
                        pe.wait_ge(bank_free[x.bank], x.free)
                out = []
                for tt in range(NT):
                    for g in range(2):
                        x = open_item(2 * tt + g)
                        for kk in range(4):
                            mm = nc.tensor.transpose(banks[x.bank][:, kk * P:(kk + 1) * P],
                                                     xT[:, 4 * g + kk, tt * P:(tt + 1) * P], ident[:])
                        close(mm, x)
                        out.append(x)
                items["end"] = out

            last_add = [None]
            n_row_loads = len(row_loads())
            for kind, arg in phases():
                if kind == "start":
                    start()
                elif kind == "rms":
                    rms((arg[0], arg[1]))
                elif kind == "A":
                    attn_a(arg)
                elif kind == "B":
                    attn_b(arg)
                elif kind == "C":
                    attn_c(arg)
                elif kind == "ffn":
                    ffn("f_w_gu", "f_w_out", arg, ("ffn", arg))
                    last_add[0] = (("ffn", arg), "down")
                elif kind == "final":
                    final()
                elif kind == "ln":
                    if arg[0] == "ln_in_g_2":
                        pe.wait_ge(h_ready, count(h_ready, KT))
                    else:
                        for x in items[last_add[0]]:
                            pe.wait_ge(bank_free[x.bank], x.free)
                    ln(arg)
                elif kind == "mix":
                    mix(arg)
                    last_add[0] = (("m", arg), "wo")
                elif kind == "ffn2":
                    ffn("w_up_2", "w_down_2", arg, ("ffn2", arg))
                    last_add[0] = (("ffn2", arg), "down")
                elif kind == "end":
                    end()

        @block.sync
        def _(sp):
            sp.dma_start(xrows[:], t["x"][0].rearrange("(t p) n -> p t n", p=P)).then_inc(x_landed, 16)

            def issue(c, loads):
                for shape, src in loads:
                    k, width, c0, n = shape[:4]
                    base = shape[4] if len(shape) > 4 else 0
                    dst = wring[c.slot][:, base:base + k * width].rearrange("p (k n) -> p k n", k=k)[:, :, c0:c0 + n]
                    sp.dma_start(dst, src).then_inc(landed[c.slot], 16)

            n = 0
            while n < len(chunks):
                c = chunks[n]
                if not callable(c.loads):
                    if n >= SLOTS:
                        sp.wait_ge(pe_done, last_read(chunks[n - SLOTS]))
                    issue(c, c.loads)
                    n += 1
                    continue
                body = [chunks[m] for m in range(n, len(chunks)) if callable(chunks[m].loads)
                        and chunks[m].group == c.group]
                for j, b in enumerate(body):
                    before = chunks[n + j - SLOTS]
                    sp.wait_ge(pe_done, before.done if before in body else last_read(before))
                    issue(b, b.loads(0, b.round))
                with sp.Fori(1, c.rounds) as i:
                    for j, b in enumerate(body):
                        if j >= SLOTS:
                            sp.wait_ge(pe_done, i * b.step_done + body[j - SLOTS].done)
                        else:
                            before = body[len(body) - SLOTS + j]
                            sp.wait_ge(pe_done, i * b.step_done + (before.done - before.step_done))
                        issue(b, b.loads(i, b.round))
                n += len(body)
            for x in items["end"]:
                sp.wait_ge(bank_free[x.bank], x.free)
            sp.dma_start(t["out"][0].rearrange("(t p) n -> p t n", p=P), xrows[:]).then_inc(out_stored, 16)
            sp.wait_ge(out_stored, 16)
            sp.wait_ge(poolw_ready, 16 * 4 * DEPTH_2)

        @block.gpsimd
        def _(pool):
            nc.gpsimd.memset(ones[:], 1.0).then_inc(ident_ready, 1)
            nc.gpsimd.memset(ident[:], 0.0).then_inc(ident_ready, 1)
            nc.gpsimd.memset(poolw[:], 0.0).then_inc(poolw_zeroed, 1)
            pool.wait_ge(ident_ready, 2)
            nc.gpsimd.affine_select(out=ident[:], in_=ident[:], compare_op=ALU.not_equal, fill=1.0, base=0,
                                    pattern=[[-1, P]], channel_multiplier=1).then_inc(ident_ready, 1)
            seen_b, seen_m = 0, 0
            for kind, arg in phases():
                if kind == "B":
                    seen_b += 1
                    pool.wait_ge(kr_ready, seen_b)
                    nc.gpsimd.tensor_copy(kT[64:96, 0:B_HEADS, :],
                                          kr[64:96, :].unsqueeze(1).to_broadcast([32, B_HEADS, T])).then_inc(kr_spread, 1)
                if kind == "mix":
                    for tt in range(NT):
                        pool.wait_ge(score_step, IDX_HEADS * NT * seen_m + NT * (IDX_HEADS - 1) + tt + 1)
                        nc.gpsimd.affine_select(out=score[:, tt, :], in_=score[:, tt, :], compare_op=ALU.is_ge,
                                                fill=FILL, base=tt * P, pattern=[[-1, T]],
                                                channel_multiplier=1).then_inc(score_masked, 1)
                    for tt in range(NT):
                        pool.wait_ge(picked, NT * seen_m + tt + 1)
                        nc.gpsimd.affine_select(out=work[:, tt, :], in_=work[:, tt, :], compare_op=ALU.is_ge,
                                                fill=NEG, base=tt * P, pattern=[[-1, T]],
                                                channel_multiplier=1).then_inc(keep_ready, 1)
                    seen_m += 1

        @block.scalar
        def _(act):
            tally = {}

            def count(s, n=1):
                tally[s.name] = tally.get(s.name, 0) + n
                return tally[s.name]

            def done(x, i=None):
                act.wait_ge(pe_done, x.done if i is None else i * x.step_done + x.done)

            def freed(x):
                act.wait_ge(bank_free[x.bank], x.free)

            def free(ins, x):
                ins.then_inc(bank_free[x.bank], 1)

            fn = nc.scalar.activation
            act.dma_start(pos_i[:], t["positions_2"].to_broadcast([P, T])).then_inc(pos_landed, 16)
            act.dma_start(invf[:], t["c_invf"]).then_inc(pos_landed, 16)
            for n, name in enumerate(("a_lambda_q1", "a_lambda_k1", "a_lambda_q2", "a_lambda_k2")):
                for l in range(2):
                    act.dma_start(lamv[:, 2 * n + l, :], t[name][l:l + 1, :].to_broadcast([P, HD])).then_inc(lam_landed, 16)
            for dst, src in row_loads():
                act.dma_start(dst, src).then_inc(rows_landed, 16)
            for dst, name in ((tab, "c_tab"), (tabk, "c_tabk"), (rotm, "c_rotm"), (cmask, "c_cmask"),
                              (inv_cnt, "c_inv_cnt")):
                act.dma_start(dst[:], t[name]).then_inc(consts_landed, 16)
            for (a, b, col) in ((0, P, Z_V), (P, P + 8, Z_WI)):
                act.dma_start(brow[0:1, :, a:b], t["b_in_2"][:, col:col + b - a].unsqueeze(0)).then_inc(consts_landed, 16)
            act.wait_ge(poolw_zeroed, 1)
            for l in range(DEPTH_2):
                for g in range(4):
                    a = HD * (g % 2)
                    act.dma_start(poolw[a:a + HD, l, g // 2, a:a + HD], t["pool_w_2"][l, g]).then_inc(poolw_ready, 16)

            def start():
                act.wait_ge(lam_sums, 1)
                fn(lame[:], lams[:], ACT.Exp).then_inc(lam_exps, 1)
                act.wait_ge(angles_ready, 2)
                fn(tabd[:, 3, :], expo[0][:, 0:T], ACT.Sin)
                fn(tabd[:, 2, :], expo[0][:, T:2 * T], ACT.Sin, scale=-1.0, bias=eps[:, 2:3]).then_inc(sines_ready, 1)

            def norm_squares(source, tiles=2):
                for j, x in enumerate(source):
                    freed(x)
                    fn(sq[:, 2 * j:2 * j + 2, :], xT[:, 2 * j:2 * j + 2, :], ACT.Square).then_inc(squares_ready, 1)

            def deviation(s, spans, e=0):
                done(s)
                for a, b, n in spans:
                    ins = fn(std[:, a:b], banks[s.bank][:, a:b], ACT.Sqrt, scale=1.0 / n, bias=eps[:, e:e + 1])
                free(ins, s)

            def pre_copies(xs, rr, before=(), rows=P):
                for n, x in enumerate(xs):
                    done(x)
                    if n >= 3:
                        freed(rr[n - 3])
                    free(nc.scalar.copy(pre[x.pre][0:rows, :], banks[x.bank][0:rows, :]), x)

            def attn_a(i):
                pre_copies(items[i, "qk"], items[i, "rot"])
                for n, v in enumerate(items[i, "v"]):
                    done(v)
                    free(nc.scalar.copy(vA[:, n % 2, (n // 2) * 512:(n // 2 + 1) * 512], banks[v.bank][:]), v)
                S, TT, O = items[i, "S"], items[i, "T"], items[i, "O"]
                for h in range(A_HEADS + 2):
                    if h < A_HEADS:
                        if h >= 2:
                            done(TT[h - 2][0])
                        for sub in range(2):
                            n = 2 * h + sub
                            act.wait_ge(negmax_ready, count(negmax_ready))
                            for tt in range(NT):
                                ins = fn(expo[h % 2][:, 512 * sub + tt * T:512 * sub + (tt + 1) * T],
                                         banks[S[n].bank][:, tt * T:(tt + 1) * T], ACT.Exp,
                                         bias=negmax[n % 4][:, tt:tt + 1], accum_out=esum[n % 4][:, tt:tt + 1])
                            free(ins, S[n])
                    if 1 <= h <= A_HEADS:
                        probs_t(h - 1, TT, 1)
                    if h >= 2 and (h - 2) % 2 == 1:
                        g = (h - 2) // 2
                        done(O[g])
                        fn(sq[:, 2 * g:2 * g + 2, :], banks[O[g].bank][:].rearrange("p (m n) -> p m n", m=2),
                           ACT.Square).then_inc(squares_ready, 1)
                        free(nc.scalar.copy(oT[:, 2 * g:2 * g + 2, :],
                                            banks[O[g].bank][:].rearrange("p (m n) -> p m n", m=2)), O[g])
                deviation(items[i, "subln"][0], ((0, 16, P),))

            def probs_t(h, TT, n):
                if h >= 2:
                    act.wait_ge(pe_done, TT[h - 2][-1].used)
                for g in range(n):
                    it = TT[h][g]
                    done(it)
                    free(nc.scalar.copy(expoT[h % 2][:, 512 * g:512 * (g + 1)], banks[it.bank][:]), it)

            def attn_64(tag, heads, masked, groups=1, dst=oT):
                S, TT, O = items[tag, "S"], items[tag, "T"], items[tag, "O"]
                w = T * groups
                for h in range(heads + 2):
                    if h < heads:
                        act.wait_ge(negmax_ready, count(negmax_ready))
                        if not masked and h >= 2:
                            for it in TT[h - 2]:
                                done(it)
                        for tt in range(NT):
                            e = expo[h % 2][:, w * tt:w * (tt + 1)]
                            ins = fn(e, e if masked else banks[S[h][0].bank][:, tt * T:(tt + 1) * T], ACT.Exp,
                                     bias=negmax[h % 4][:, tt:tt + 1], accum_out=esum[h % 4][:, tt:tt + 1])
                        if masked:
                            ins.then_inc(exp_ready, 1)
                        else:
                            free(ins, S[h][0])
                    if 1 <= h <= heads:
                        probs_t(h - 1, TT, groups)
                    if h >= 2 and (h - 2) % 4 == 3:
                        g = (h - 2) // 4
                        done(O[g])
                        free(nc.scalar.copy(dst[:, 2 * g:2 * g + 2, :],
                                            banks[O[g].bank][:].rearrange("p (m n) -> p m n", m=2)), O[g])

            def attn_b(i):
                raw = items[i, "raw"]
                for n in range(2):
                    done(raw[n])
                    b = banks[raw[n].bank][:].rearrange("p (m n) -> p m n", m=2)
                    fn(sq[:, 2 * n:2 * n + 2, :], b, ACT.Square).then_inc(squares_ready, 1)
                    free(nc.scalar.copy(latT[:, 2 * n:2 * n + 2, :], b), raw[n])
                done(raw[2])
                fn(sq[:, 4, :], banks[2][:, 0:T], ACT.Square).then_inc(squares_ready, 1)
                nc.scalar.copy(latT[:, 4, :], banks[2][:, 0:T])
                free(nc.scalar.copy(pre[2][64:96, 0:T], banks[2][64:96, T:2 * T]), raw[2])
                deviation(items[i, "stat"][0], ((0, 2, B_QR), (2, 4, B_KVR)))
                for n, x in enumerate(items[i, "qk"]):
                    done(x)
                    if n == 2:
                        freed(items[i, "krot"])
                    if n >= 3:
                        freed(items[i, "rot"][n - 3])
                    free(nc.scalar.copy(pre[x.pre][0:96, :], banks[x.bank][0:96, :]), x)
                for n, x in enumerate(items[i, "k"]):
                    done(x)
                    free(nc.scalar.copy(kT[0:HD, 2 * n:2 * n + 2, :],
                                        banks[x.bank][0:HD, :].rearrange("p (m n) -> p m n", m=2)), x)
                for n, v in enumerate(items[i, "v"]):
                    done(v)
                    free(nc.scalar.copy(vA[:, n % 2, (n // 2) * 512:(n // 2 + 1) * 512], banks[v.bank][:]), v)
                attn_64(i, B_HEADS, False)

            def attn_c(i):
                xs, rr, vs = items[i, "qk"], items[i, "rot"], items[i, "v"]
                with act.Fori(0, C_GROUPS) as g:
                    for n, x in enumerate(xs):
                        done(x, g)
                        r = rr[(n - 2) % 8]
                        act.wait_ge(bank_free[r.bank], g * r.step_free + (r.free if n >= 2 else r.free - r.step_free))
                        free(nc.scalar.copy(pre[x.pre][:], banks[x.bank][:]), x)
                    for n, v in enumerate(vs):
                        done(v, g)
                        free(nc.scalar.copy(vC[:, n % 2, bass.ds(g * 1024 + (n // 2) * 512, 512)], banks[v.bank][:]), v)
                attn_64(i, C_HEADS, True, groups=C_GROUPS)

            def ffn(tag):
                body, tail = items[tag, "up"]

                def step(j, g, u, i=None):
                    done(g, i)
                    act.wait_ge(bank_free[u.bank], u.free - 1 if i is None else i + (u.free - 1))
                    free(fn(pre[j][:], banks[g.bank][:], ACT.Silu), g)

                with act.Fori(0, 3) as i:
                    for j, (g, u) in enumerate(body):
                        step(j, g, u, i)
                for j, (g, u) in enumerate(tail):
                    step(j, g, u)

            def ln(tag):
                s, m, v, b = items[tag]
                for j in range(4):
                    act.wait_ge(centred, count(centred))
                    fn(sq[:, 2 * j:2 * j + 2, :], xT[:, 2 * j:2 * j + 2, :], ACT.Square).then_inc(squares_ready, 1)
                deviation(v, ((0, 2, D),), 1)
                at = ROW[tag[1]] + tag[2]
                for k in range(KT):
                    act.wait_ge(ln_ready, count(ln_ready))
                    fn(xT[:, k, :], hT[:, k, :], ACT.Identity, bias=pcol[:, at + k:at + k + 1]).then_inc(y_ready, 1)

            def mix(l):
                it = items["m", l]
                b0 = ROW["b_in", l]

                def offset(dst, x, row, tiles=2, func=ACT.Identity):
                    done(x)
                    for m in range(tiles):
                        ins = fn(dst(m), banks[x.bank][:, m * T:(m + 1) * T], func, bias=pcol[:, b0 + row + m:b0 + row + m + 1])
                    free(ins, x)

                offset(lambda m: pool_u[:, m, PADW:], it["pool"], B_POOL)
                offset(lambda m: conv_a[:, m, :], it["conv_a"], B_CONV)
                offset(lambda m: conv_y[:, m, :], it["conv_g"], B_CONV + 2, func=ACT.Sigmoid)
                for n, (x, row) in enumerate(zip(it["qk"], (B_Q, B_Q + 2, B_K, B_QI, B_QI + 2, B_KI))):
                    if n >= 3:
                        freed(it["rot"][n - 3])
                    offset(lambda m: pre[x.pre][:, m * T:(m + 1) * T], x, row, tiles=1 if n == 5 else 2)
                v = it["v"]
                done(v)
                b = banks[v.bank][:, 0:272].rearrange("p (t n) -> p t n", t=NT)
                nc.scalar.copy(vD[:], b[:, :, 0:128])
                free(nc.scalar.mul(wi[:], b[:, :, 128:136], float(np.float32(IDX_HEADS ** -0.5))), v)
                for n, s in enumerate(it["idx"]):
                    done(s)
                    if n >= 2:
                        act.wait_ge(score_step, NT * IDX_HEADS * l + 2 * (n - 1))
                    free(fn(relu[n % 2], banks[s.bank][:], ACT.Relu), s)
                with act.Fori(0, 2) as i:
                    for n, x in enumerate(it["gates"]):
                        done(x, i)
                        for m in range(2):
                            ins = fn(gates[:, bass.ds(i * 12 + (2 * n + m), 1), :], banks[x.bank][:, m * T:(m + 1) * T].unsqueeze(1),
                                     ACT.Sigmoid, bias=pcol[:, bass.ds(i * 12 + (b0 + B_GATE + 2 * n + m), 1)])
                        free(ins, x)
                s, m_, v, b = it["cln"]
                act.wait_ge(centred, count(centred))
                fn(sq[:, 0:2, :], conv_y[:], ACT.Square).then_inc(squares_ready, 1)
                deviation(v, ((0, 2, 256),), 1)
                at = ROW["conv_ln_b_2"] + 2 * l
                for m in range(2):
                    act.wait_ge(ln_ready, count(ln_ready))
                    fn(convT[:, m, :], conv_y[:, m, :], ACT.Silu, bias=pcol[:, at + m:at + m + 1]).then_inc(y_ready, 1)
                attn_64(("m", l), N_HEADS, True, dst=attnT)

            def ffn2(tag, l):
                body, tail = items[tag, "up"]
                w, b = ROW["ffn_dw_w_2"] + l * FCW * 44 + 2 * 44, ROW["ffn_dw_b_2"] + l * 44
                base = 3 + 11 * l

                def step(n, j, g, u, i=None):
                    def col(at):
                        return pcol[:, at:at + 1] if i is None else pcol[:, bass.ds(i * 6 + at, 1)]

                    act.wait_ge(hidden_ready, base + n + 1 - 3 if i is None else i * 3 + (base + j + 1 - 3))
                    for x, dst, tile in ((g, pre[j], 0), (u, uval[j], 22)):
                        done(x, i)
                        for m in range(2):
                            c = tile + 2 * n + m
                            ins = fn(dst[:, m * T:(m + 1) * T], banks[x.bank][:, m * T:(m + 1) * T], ACT.Identity,
                                     scale=col(w + c), bias=col(b + c))
                        ins.then_inc(taps_started, 1)

                def silu(n, j, g, i=None):
                    act.wait_ge(bank_free[g.bank], g.free if i is None else i + g.free)
                    fn(pre[j][:], pre[j][:], ACT.Silu).then_inc(gate_ready, 1)

                with act.Fori(0, 3) as i:
                    for j, (g, u) in enumerate(body):
                        step(j, j, g, u, i)
                        silu(j, j, g, i)
                for j, (g, u) in enumerate(tail):
                    step(9 + j, j, g, u)
                    silu(9 + j, j, g)

            source = [items["start"]["x"]]
            for kind, arg in phases():
                if kind == "start":
                    start()
                elif kind == "rms":
                    norm_squares(source[0])
                    deviation(items[arg[0], arg[1]][0], ((0, 2, D),))
                elif kind == "A":
                    attn_a(arg)
                    source[0] = items[arg, "wo"]
                elif kind == "B":
                    attn_b(arg)
                    source[0] = items[arg, "wo"]
                elif kind == "C":
                    attn_c(arg)
                    source[0] = items[arg, "wo"]
                elif kind == "ffn":
                    ffn(("ffn", arg))
                    source[0] = items[("ffn", arg), "down"]
                elif kind == "final":
                    norm_squares(source[0])
                    deviation(items["final"][0], ((0, 2, D),))
                elif kind == "ln":
                    ln(arg)
                elif kind == "mix":
                    mix(arg)
                elif kind == "ffn2":
                    ffn2(("ffn2", arg), arg)

        @block.vector
        def _(dve):
            v_ = nc.vector
            tally = {}
            steps = [0]

            def count(s, n=1):
                tally[s.name] = tally.get(s.name, 0) + n
                return tally[s.name]

            def done(x, i=None):
                dve.wait_ge(pe_done, x.done if i is None else i * x.step_done + x.done)

            def freed(x, i=None):
                dve.wait_ge(bank_free[x.bank], x.free if i is None else i * x.step_free + x.free)

            def free(ins, x):
                ins.then_inc(bank_free[x.bank], 1)

            def link(ins, behind=0):
                steps[0] += 1
                ins.then_inc(dve_step, 1)
                if steps[0] > behind:
                    dve.wait_ge(dve_step, steps[0] - behind)

            def start():
                v_.memset(eps[:, 0:1], EPS)
                v_.memset(eps[:, 1:2], LN_EPS)
                v_.memset(eps[:, 3:4], 0.0)
                link(v_.memset(eps[:, 2:3], math.pi / 2))
                for n in range(3):
                    v_.memset(negmax[n][:], 0.0).then_inc(hidden_ready, 1)
                dve.wait_ge(lam_landed, 16 * 8)
                for n in range(2):
                    ins = v_.tensor_tensor(lamp[:, 2 * n:2 * n + 2, :], lamv[:, 4 * n:4 * n + 2, :],
                                           lamv[:, 4 * n + 2:4 * n + 4, :], ALU.mult)
                link(ins)
                v_.tensor_reduce(lams[:], lamp[:], AX.X, ALU.add).then_inc(lam_sums, 1)
                dve.wait_ge(lam_exps, 1)
                link(v_.tensor_tensor(neglam[:], lame[:, 2:4], lame[:, 0:2], ALU.subtract))
                for l in range(2):
                    ins = v_.tensor_scalar(neglam[:, l:l + 1], neglam[:, l:l + 1], -lambda_init(3 * l), None, ALU.add)
                link(ins)
                for x, j in zip(items["start"]["x"], range(4)):
                    done(x)
                    free(v_.tensor_copy(xT[:, 2 * j:2 * j + 2, :], banks[x.bank][:].rearrange("p (m n) -> p m n", m=2)), x)
                for n, x in enumerate(items["start"]["rows"]):
                    done(x)
                    w = min(512, N_ROWS - 512 * n)
                    free(v_.tensor_copy(pcol[:, 512 * n:512 * n + w], banks[x.bank][:, 0:w]), x)
                for x in items["start"]["rows"]:
                    freed(x)
                for l in range(2):
                    ins = v_.tensor_scalar(subg[:, l:l + 1], pcol[:, ROW["a_subln"] + l:ROW["a_subln"] + l + 1],
                                           1.0 - lambda_init(3 * l), None, ALU.mult)
                link(ins)
                ang, turns, scr = expo[1][:, 0:T], expo[1][:, T:2 * T], expo[1][:, 2 * T:3 * T]
                dve.wait_ge(pos_landed, 32)
                link(v_.tensor_copy(ang, pos_i[:]))
                link(v_.tensor_scalar(ang, ang, invf[:, 0:1], None, ALU.mult))
                link(v_.tensor_scalar(turns, ang, 1.0 / (2 * math.pi), MAGIC, ALU.mult, ALU.add))
                link(v_.tensor_scalar(turns, turns, -MAGIC, None, ALU.add))
                for part in TWO_PI:
                    link(v_.scalar_tensor_tensor(ang, turns, -part, ang, ALU.mult, ALU.add))
                link(v_.tensor_scalar(expo[0][:, 0:T], ang, PI_IN, -PI_IN, ALU.min, ALU.max))
                v_.tensor_scalar(scr, expo[0][:, 0:T], -1.0, None, ALU.mult).then_inc(angles_ready, 1)
                dve.wait_ge(angles_ready, 1)
                v_.tensor_tensor(expo[0][:, T:2 * T], scr, expo[0][:, 0:T], ALU.max).then_inc(angles_ready, 1)
                dve.wait_ge(sines_ready, 1)
                for n in range(2):
                    ins = v_.tensor_scalar(tabd[:, n, :], tabd[:, 2 + n, :], HD ** -0.5, None, ALU.mult)
                link(ins)
                dve.wait_ge(consts_landed, 16 * 7)

            def rms(tag, at, src=None, dst=None):
                s, b = items[tag]
                freed(s)
                v_.reciprocal(rs[:, 0:2], std[:, 0:2]).then_inc(rs_ready, 1)
                done(b)
                for k in range(KT):
                    v_.scalar_tensor_tensor(dst[:, k, :], xT[:, k, :], pcol[:, at + k:at + k + 1], banks[b.bank][:, 0:T],
                                            ALU.mult, ALU.mult).then_inc(h_ready, 1)

            def rotate(n, x, r, dst, cos, sin, i=None, lo=0, hi=P, tiles=2, ready=rot_ready):
                w = tiles * T
                done(r, i)
                shape = [hi - lo, tiles, T]

                def wide(tb):
                    return tb[lo:hi, :].unsqueeze(1).to_broadcast(shape)

                p3 = pre[x.pre][lo:hi, 0:w].rearrange("p (m n) -> p m n", m=tiles)
                r3 = rot[n % 2][lo:hi, 0:w].rearrange("p (m n) -> p m n", m=tiles)
                v_.tensor_tensor(dst, p3, wide(cos), ALU.mult)
                free(v_.tensor_tensor(r3, banks[r.bank][lo:hi, 0:w].rearrange("p (m n) -> p m n", m=tiles), wide(sin),
                                      ALU.mult), r)
                freed(r, i)
                v_.tensor_tensor(dst, dst, r3, ALU.add).then_inc(ready, 1)

            def residual(its, scale=None):
                for j, x in enumerate(its):
                    done(x)
                    b = banks[x.bank][:].rearrange("p (m n) -> p m n", m=2)
                    xs = xT[:, 2 * j:2 * j + 2, :]
                    if scale is None:
                        free(v_.tensor_tensor(xs, xs, b, ALU.add), x)
                    else:
                        free(v_.scalar_tensor_tensor(xs, xs, scale, b, ALU.mult, ALU.add), x)

            def attn_a(i):
                l = i // 3
                for n, (x, r) in enumerate(zip(items[i, "qk"], items[i, "rot"])):
                    side = 0 if n < 4 else 2
                    rotate(n, x, r, qT[:, 2 * n:2 * n + 2, :], tab[:, side, :], tab[:, side + 1, :])
                S = items[i, "S"]
                for h in range(A_HEADS + 1):
                    if h < A_HEADS:
                        for sub in range(2):
                            n = 2 * h + sub
                            done(S[n])
                            v_.tensor_reduce(negmax[n % 4][:], banks[S[n].bank][:].rearrange("p (m n) -> p m n", m=2), AX.X,
                                             ALU.max, negate=True).then_inc(negmax_ready, 1)
                    if h >= 1:
                        n = 2 * (h - 1)
                        e = expo[(h - 1) % 2]
                        rec = [erec[(n + sub) % 4] for sub in range(2)]
                        for sub in range(2):
                            freed(S[n + sub])
                            link(v_.reciprocal(rec[sub][:], esum[(n + sub) % 4][:]))
                        link(v_.tensor_scalar(rec[1][:], rec[1][:], neglam[:, l:l + 1], None, ALU.mult))
                        for tt in range(NT):
                            e0 = e[:, tt * T:(tt + 1) * T]
                            ins = v_.tensor_scalar(e0, e0, rec[0][:, tt:tt + 1], None, ALU.mult)
                        link(ins)
                        for tt in range(NT):
                            e0, e1 = e[:, tt * T:(tt + 1) * T], e[:, 512 + tt * T:512 + (tt + 1) * T]
                            ins = v_.scalar_tensor_tensor(e0, e1, rec[1][:, tt:tt + 1], e0, ALU.mult, ALU.add)
                        ins.then_inc(probs_ready, 1)
                s, sp_items = items[i, "subln"]
                freed(s)
                v_.reciprocal(rs[:, 0:16], std[:, 0:16]).then_inc(rs_ready, 1)
                for g, b in enumerate(sp_items):
                    done(b)
                    for hh in range(2):
                        ins = v_.scalar_tensor_tensor(oT[:, 2 * g + hh, :], oT[:, 2 * g + hh, :], subg[:, l:l + 1],
                                                      banks[b.bank][:, hh * T:(hh + 1) * T], ALU.mult, ALU.mult)
                    free(ins, b)
                residual(items[i, "wo"])

            def attn_64(tag, heads, mask=None, groups=1):
                S, TT = items[tag, "S"], items[tag, "T"]
                w = T * groups
                for h in range(heads + 1):
                    if h < heads:
                        if mask is None:
                            done(S[h][0])
                            v_.tensor_reduce(negmax[h % 4][:], banks[S[h][0].bank][:].rearrange("p (m n) -> p m n", m=2),
                                             AX.X, ALU.max, negate=True).then_inc(negmax_ready, 1)
                        else:
                            e = expo[h % 2]
                            if h >= 2:
                                for it in TT[h - 2]:
                                    done(it)
                            if groups == 1:
                                spans = [(e[:, 0:512], mask[:, 0:512], banks[S[h][0].bank][:])]
                            else:
                                e3, m3 = (z[:, 0:1536].rearrange("p (t n) -> p t n", t=NT) for z in (e, mask))
                                spans = [(e[:, 0:512], mask[:, 0:512], banks[S[h][0].bank][:]),
                                         (e3[:, :, 512:768], m3[:, :, 512:768],
                                          banks[S[h][1].bank][:].rearrange("p (t n) -> p t n", t=NT)),
                                         (e[:, 768:1280], mask[:, 768:1280], banks[S[h][2].bank][:])]
                            for (dst, msk, src), s in zip(spans, S[h]):
                                done(s)
                                free(v_.tensor_tensor(dst, src, msk, ALU.add), s)
                            for s in S[h]:
                                freed(s)
                            v_.tensor_reduce(negmax[h % 4][:], e[:, 0:NT * w].rearrange("p (t n) -> p t n", t=NT), AX.X,
                                             ALU.max, negate=True).then_inc(negmax_ready, 1)
                    if h >= 1:
                        g = h - 1
                        if mask is None:
                            freed(S[g][0])
                        else:
                            dve.wait_ge(exp_ready, count(exp_ready))
                        link(v_.reciprocal(erec[g % 4][:], esum[g % 4][:]))
                        for tt in range(NT):
                            e = expo[g % 2][:, w * tt:w * (tt + 1)]
                            ins = v_.tensor_scalar(e, e, erec[g % 4][:, tt:tt + 1], None, ALU.mult)
                        ins.then_inc(probs_ready, 1)

            def attn_b(i):
                s, b = items[i, "stat"]
                freed(s)
                v_.reciprocal(rs[:, 0:4], std[:, 0:4]).then_inc(rs_ready, 1)
                done(b)
                for k in range(5):
                    at = ROW["b_q_norm"] + k
                    a = 0 if k < 3 else T
                    v_.scalar_tensor_tensor(hT[:, k, :], latT[:, k, :], pcol[:, at:at + 1], banks[b.bank][:, a:a + T],
                                            ALU.mult, ALU.mult).then_inc(h_ready, 1)
                rotate(0, items[i, "raw"][2], items[i, "krot"], kr[64:96, :].unsqueeze(1), tabk[:, 0, :], tabk[:, 1, :],
                       lo=64, hi=96, tiles=1, ready=kr_ready)
                for n, (x, r) in enumerate(zip(items[i, "qk"], items[i, "rot"])):
                    rotate(n + 1, x, r, qT[0:96, 2 * n:2 * n + 2, :], tab[:, 4, :], tab[:, 5, :], hi=96)
                attn_64(i, B_HEADS)
                residual(items[i, "wo"])

            def attn_c(i):
                with dve.Fori(0, C_GROUPS) as g:
                    for n, (x, r) in enumerate(zip(items[i, "qk"], items[i, "rot"])):
                        side = 0 if n < 4 else 2
                        dst = (qT if n < 4 else kT)[:, bass.ds(g * 8 + 2 * (n % 4), 2), :]
                        rotate(n, x, r, dst, tab[:, side, :], tab[:, side + 1, :], i=g)
                attn_64(i, C_HEADS, mask=cmask, groups=C_GROUPS)
                residual(items[i, "wo"])

            def ffn(tag):
                body, tail = items[tag, "up"]

                def step(dst, j, g, u, i=None):
                    freed(g, i)
                    done(u, i)
                    free(v_.tensor_tensor(dst, pre[j][:].rearrange("p (m n) -> p m n", m=2),
                                          banks[u.bank][:].rearrange("p (m n) -> p m n", m=2), ALU.mult), u)

                with dve.Fori(0, 3) as i:
                    for j, (g, u) in enumerate(body):
                        step(hidden[:, bass.ds(i * 6 + 2 * j, 2), :], j, g, u, i)
                for j, (g, u) in enumerate(tail):
                    step(hidden[:, 18 + 2 * j:20 + 2 * j, :], j, g, u)
                residual(items[tag, "down"])

            def ln(tag):
                s, m, v, b = items[tag]
                done(s)
                free(v_.tensor_scalar(rs[:, 0:2], banks[s.bank][:, 0:2], -1.0 / D, None, ALU.mult), s)
                done(m)
                for j in range(4):
                    xs = xT[:, 2 * j:2 * j + 2, :]
                    v_.tensor_tensor(xs, xs, banks[m.bank][:, 0:T].unsqueeze(1).to_broadcast([P, 2, T]),
                                     ALU.add).then_inc(centred, 1)
                freed(v)
                v_.reciprocal(rs[:, 0:2], std[:, 0:2]).then_inc(rs_ready, 1)
                done(b)
                at = ROW[tag[0]] + tag[2]
                for k in range(KT):
                    v_.scalar_tensor_tensor(hT[:, k, :], xT[:, k, :], pcol[:, at + k:at + k + 1], banks[b.bank][:, 0:T],
                                            ALU.mult, ALU.mult).then_inc(ln_ready, 1)

            def mix(l):
                it = items["m", l]
                v_.memset(pool_u[:, :, 0:PADW], 0.0)
                link(v_.memset(conv_h[:, :, 0:PADW], 0.0))
                dsts = (qT[:, 0:2, :], qT[:, 2:4, :], kdT, qiT[:, 0:2, :], qiT[:, 2:4, :], kidT.unsqueeze(1))
                for n, (x, r, dst) in enumerate(zip(it["qk"], it["rot"], dsts)):
                    side = 2 if n in (2, 5) else 0
                    rotate(n, x, r, dst, tabd[:, side, :], tabd[:, side + 1, :], tiles=1 if n == 5 else 2)
                freed(it["v"])
                base = NT * IDX_HEADS * l
                for n, s in enumerate(it["idx"]):
                    freed(s)
                    for tt in range(NT):
                        src, wh = relu[n % 2][:, tt * T:(tt + 1) * T], wi[:, tt, n:n + 1]
                        if n == 0:
                            v_.tensor_scalar(score[:, tt, :], src, wh, None, ALU.mult).then_inc(score_step, 1)
                        else:
                            dve.wait_ge(score_step, base + 2 * n + tt - 1)
                            v_.scalar_tensor_tensor(score[:, tt, :], src, wh, score[:, tt, :], ALU.mult,
                                                    ALU.add).then_inc(score_step, 1)
                for tt in range(NT):
                    dve.wait_ge(score_masked, count(score_masked))
                    src = score[:, tt, :]
                    for _ in range(TOPK // 8):
                        link(v_.max(m8[:], src))
                        link(v_.match_replace(work[:, tt, :], m8[:], src, TAKEN))
                        src = work[:, tt, :]
                    link(v_.tensor_scalar(src, src, TAKEN, 1.0, ALU.is_equal, ALU.subtract))
                    v_.tensor_scalar(src, src, -NEG, None, ALU.mult).then_inc(picked, 1)
                freed(it["conv_g"])
                link(v_.tensor_tensor(conv_h[:, :, PADW:], conv_a[:], conv_y[:], ALU.mult))
                cw, cb = ROW["conv_dw_w_2"] + l * CONV_W * 2, ROW["conv_dw_b_2"] + 2 * l
                for j in range(CONV_W):
                    for m in range(2):
                        h = conv_h[:, m, PADW - CONV_W + 1 + j:PADW - CONV_W + 1 + j + T]
                        wj = pcol[:, cw + 2 * j + m:cw + 2 * j + m + 1]
                        if j == 0:
                            ins = v_.tensor_scalar(conv_y[:, m, :], h, wj, pcol[:, cb + m:cb + m + 1], ALU.mult, ALU.add)
                        else:
                            ins = v_.scalar_tensor_tensor(conv_y[:, m, :], h, wj, conv_y[:, m, :], ALU.mult, ALU.add)
                        if j == CONV_W - 1:
                            if m == 1:
                                ins.then_inc(conv_out, 1)
                            else:
                                link(ins, behind=1)
                        else:
                            link(ins, behind=1)
                end = T + PADW
                freed(it["pool"])
                link(v_.tensor_tensor(pool_w2[:, :, 1:], pool_u[:, :, 1:], pool_u[:, :, :end - 1], ALU.add))
                link(v_.tensor_tensor(pool_w4[:, :, 3:], pool_w2[:, :, 3:], pool_w2[:, :, 1:end - 2], ALU.add))
                v_.tensor_tensor(mixed[0:64, 0, :], pool_w2[0:64, 0, PADW:], inv_cnt[0:64, 0, :], ALU.mult)
                link(v_.tensor_tensor(pool_w2[:, 1, 7:], pool_w4[:, 1, 7:], pool_w4[:, 1, 3:end - 4], ALU.add))
                v_.tensor_tensor(mixed[64:128, 0, :], pool_w4[64:128, 0, PADW:], inv_cnt[64:128, 0, :], ALU.mult)
                v_.tensor_tensor(mixed[0:64, 1, :], pool_w2[0:64, 1, PADW:], inv_cnt[0:64, 1, :], ALU.mult)
                link(v_.tensor_tensor(pool_w4[64:128, 1, 15:], pool_w2[64:128, 1, 15:], pool_w2[64:128, 1, 7:end - 8], ALU.add))
                link(v_.tensor_tensor(mixed[64:128, 1, :], pool_w4[64:128, 1, PADW:], inv_cnt[64:128, 1, :], ALU.mult))
                v_.tensor_tensor(mixed[:], mixed[:], pool_u[:, :, PADW:], ALU.subtract).then_inc(mixed_ready, 1)
                x = it["poolmix"]
                done(x)
                at = ROW["pool_scale_2"] + 2 * l
                for m in range(2):
                    ins = v_.tensor_scalar(poolT[:, m, :], banks[x.bank][:, m * T:(m + 1) * T], pcol[:, at + m:at + m + 1],
                                           None, ALU.mult)
                free(ins, x)
                s, m_, v, b = it["cln"]
                done(s)
                free(v_.tensor_scalar(rs[:, 0:2], banks[s.bank][:, 0:2], -1.0 / 256, None, ALU.mult), s)
                done(m_)
                v_.tensor_tensor(conv_y[:], conv_y[:], banks[m_.bank][:, 0:T].unsqueeze(1).to_broadcast([P, 2, T]),
                                 ALU.add).then_inc(centred, 1)
                freed(v)
                v_.reciprocal(rs[:, 0:2], std[:, 0:2]).then_inc(rs_ready, 1)
                done(b)
                at = ROW["conv_ln_g_2"] + 2 * l
                for m in range(2):
                    v_.scalar_tensor_tensor(conv_y[:, m, :], conv_y[:, m, :], pcol[:, at + m:at + m + 1],
                                            banks[b.bank][:, 0:T], ALU.mult, ALU.mult).then_inc(ln_ready, 1)
                dve.wait_ge(keep_ready, count(keep_ready, NT))
                attn_64(("m", l), N_HEADS, mask=work.rearrange("p t n -> p (t n)"))
                for n, x in enumerate(it["branch"]):
                    br, m = divmod(n, 4)
                    done(x)
                    dst = hT[:, 2 * m:2 * m + 2, :]
                    tmp = rot[n % 2][:].rearrange("p (m n) -> p m n", m=2)
                    b = banks[x.bank][:].rearrange("p (m n) -> p m n", m=2)
                    g = gates[:, 8 * br + 2 * m:8 * br + 2 * m + 2, :]
                    free(v_.tensor_tensor(dst if br == 0 else tmp, b, g, ALU.mult), x)
                    if br:
                        freed(x)
                        ins = v_.tensor_tensor(dst, dst, tmp, ALU.add)
                        if br == 2:
                            ins.then_inc(merged_ready, 1)
                        else:
                            link(ins)
                residual(items[("m", l), "wo"], ALPHA)

            def ffn2(tag, l):
                body, tail = items[tag, "up"]
                w = ROW["ffn_dw_w_2"] + l * FCW * 44
                started0, gates0 = 22 * l, 11 * l
                chain0 = steps[0]

                def step(dst, n, j, g, u, i=None):
                    def col(at):
                        return pcol[:, at:at + 1] if i is None else pcol[:, bass.ds(i * 6 + at, 1)]

                    for y, (x, buf, tile) in enumerate(((g, pre[j], 0), (u, uval[j], 22))):
                        at = started0 + 2 * n + y + 1
                        dve.wait_ge(taps_started, at if i is None else i * 6 + at)
                        for m in range(2):
                            o, b, c = buf[:, m * T:(m + 1) * T], banks[x.bank][:, m * T:(m + 1) * T], tile + 2 * n + m
                            v_.scalar_tensor_tensor(o[:, 1:], b[:, :T - 1], col(w + 44 + c), o[:, 1:], ALU.mult,
                                                    ALU.add).then_inc(dve_step, 1)
                            if i is None:
                                steps[0] += 1
                                dve.wait_ge(dve_step, steps[0])
                            else:
                                dve.wait_ge(dve_step, i * 12 + (chain0 + 4 * j + 2 * y + m + 1))
                            ins = v_.scalar_tensor_tensor(o[:, 2:], b[:, :T - 2], col(w + c), o[:, 2:], ALU.mult, ALU.add)
                        free(ins, x)
                    at = gates0 + n + 1
                    dve.wait_ge(gate_ready, at if i is None else i * 3 + at)
                    freed(u, i)
                    v_.tensor_tensor(dst, pre[j][:].rearrange("p (m n) -> p m n", m=2),
                                     uval[j].rearrange("p (m n) -> p m n", m=2), ALU.mult).then_inc(hidden_ready, 1)

                with dve.Fori(0, 3) as i:
                    for j, (g, u) in enumerate(body):
                        step(hidden[:, bass.ds(i * 6 + 2 * j, 2), :], j, j, g, u, i)
                steps[0] += 36
                for j, (g, u) in enumerate(tail):
                    step(hidden[:, 18 + 2 * j:20 + 2 * j, :], 9 + j, j, g, u)
                residual(items[tag, "down"], ALPHA)

            for kind, arg in phases():
                if kind == "start":
                    start()
                elif kind == "rms":
                    rms(arg[:2], ROW[arg[1]] + arg[2], dst=hT)
                elif kind == "A":
                    attn_a(arg)
                elif kind == "B":
                    attn_b(arg)
                elif kind == "C":
                    attn_c(arg)
                elif kind == "ffn":
                    ffn(("ffn", arg))
                elif kind == "final":
                    rms("final", ROW["final_norm"], dst=xT)
                elif kind == "ln":
                    ln(arg)
                elif kind == "mix":
                    mix(arg)
                elif kind == "ffn2":
                    ffn2(("ffn2", arg), arg)
                elif kind == "end":
                    for n, x in enumerate(items["end"]):
                        done(x)
                        free(v_.tensor_copy(xrows[:, n // 2, (n % 2) * 512:(n % 2 + 1) * 512], banks[x.bank][:]), x)


def lambda_init(i):
    return 0.8 - 0.6 * math.exp(-0.3 * i)


TWO_PI = (6.28125, float(np.float32(0.0019340515136718750)),
          2 * math.pi - 6.28125 - float(np.float32(0.0019340515136718750)))
MAGIC = 12582912.0
PI_IN = 3.1415925


def last_read(chunk):
    return chunk.done + (chunk.rounds - 1) * chunk.step_done if chunk.step_done else chunk.done


def constants():
    f = np.float32

    def rope(rot_dim):
        pos = np.arange(T, dtype=f)
        inv = (f(500000.0) ** (-np.arange(0, rot_dim, 2, dtype=f) / f(rot_dim))).astype(f)
        ang = (pos[:, None] * inv[None, :]).astype(f)
        return np.cos(ang).astype(f), np.sin(ang).astype(f)

    def tables(cos, sin, starts, rows):
        r = cos.shape[1]
        c, s = np.ones((P, T), f), np.zeros((P, T), f)
        for a in starts:
            for z in range(2):
                c[a + z * r:a + (z + 1) * r] = cos.T
                s[a + z * r:a + (z + 1) * r] = sin.T
        return c, s

    def swap(starts, r):
        w = np.zeros((P, P), f)
        for a in starts:
            for d in range(r):
                w[a + r + d, a + d] = -1.0
                w[a + d, a + r + d] = 1.0
        return w

    ca, sa = tables(*rope(16), (0, 64), P)
    cb, sb_ = tables(*rope(32), (64,), P)
    b_scale = f((B_NOPE + B_ROPE) ** -0.5)
    tab = np.stack([ca * f(0.125), sa * f(0.125), ca, sa, cb * b_scale, sb_ * b_scale], 1)
    tabk = np.stack([cb, sb_], 1)
    rotm = np.stack([swap((0, 64), 8), swap((64,), 16), swap((0, 64), 32)], 1)
    q = np.arange(P)[:, None] + P * np.arange(NT)[None, :]
    key = np.arange(T)
    dist = q[:, :, None] - key
    ok = np.stack([np.abs(dist) <= 64, dist % 4 == 0, dist % 16 == 0], 2)
    cmask = np.where(ok, f(0), f(NEG)).reshape(P, NT * C_GROUPS * T)
    cnt = np.zeros((P, 2, T), f)
    for g, win in enumerate(POOL_WINDOWS):
        cnt[HD * (g % 2):HD * (g % 2) + HD, g // 2] = 1.0 / np.minimum(np.arange(T) + 1, win)
    invf = f(10000.0) ** (-np.arange(32, dtype=f) / f(32))
    return {"c_tab": tab, "c_tabk": tabk, "c_rotm": rotm, "c_cmask": cmask.astype(f), "c_inv_cnt": cnt,
            "c_invf": np.tile(invf.astype(f), 4)[:, None]}


_INS = ["x", "attn_norm", "ffn_norm", "final_norm", "a_w_qkv", "a_lambda_q1", "a_lambda_k1", "a_lambda_q2",
        "a_lambda_k2", "a_subln", "a_w_o", "b_w_a", "b_q_norm", "b_kv_norm", "b_w_qb", "b_w_kvb", "b_w_o",
        "c_w_qkv", "c_w_o", "f_w_gu", "f_w_out", "positions_2", "ln_in_g_2", "ln_in_b_2", "w_in_2", "b_in_2",
        "pool_w_2", "pool_scale_2", "w_pool_out_2", "conv_dw_w_2", "conv_dw_b_2", "conv_ln_g_2", "conv_ln_b_2",
        "w_conv_out_2", "w_attn_out_2", "w_o_2", "ln1_g_2", "ln1_b_2", "w_up_2", "ffn_dw_w_2", "ffn_dw_b_2",
        "w_down_2", "ln2_g_2", "ln2_b_2"]


def kernel(**inputs):
    import concourse.bacc as bacc
    from concourse.bass_utils import run_bass_kernel_spmd

    nc = bacc.Bacc("TRN2", target_bir_lowering=False, num_devices=1)
    arrays, t = {}, {}
    for name, a in [*((n, inputs[n]) for n in _INS), *constants().items()]:
        a = np.ascontiguousarray(a)
        arrays[f"in_{name}"] = a
        t[name] = nc.dram_tensor(f"in_{name}", a.shape, mybir.dt.from_np(a.dtype), kind="ExternalInput").ap()
    t["out"] = nc.dram_tensor("out", (1, T, D), F32, kind="ExternalOutput").ap()
    build(nc, t)
    r = run_bass_kernel_spmd(nc, [arrays], core_ids=[0])
    return r.results[0]["out"]
```

```python
import math
from contextlib import ExitStack

import numpy as np
import concourse.bass as bass
from concourse import mybir

F32 = mybir.dt.float32
F32R = mybir.dt.float32r
I32 = mybir.dt.int32
ALU = mybir.AluOpType
ACT = mybir.ActivationFunctionType
AX = mybir.AxisListType

P = 128
T = 256
NT = T // P
D = 1024
KT = D // P
FFN = 2816
FT = FFN // P
DEPTH, DEPTH_2 = 4, 2
EPS, LN_EPS = 1e-6, 1e-5
ALPHA = (2 * DEPTH_2) ** 0.25
A_HEADS = 8
B_HEADS, B_QR, B_KVR, B_NOPE, B_ROPE, B_V = 16, 384, 256, 64, 32, 64
C_HEADS, C_GROUPS = 16, 3
HD = 64
N_HEADS, N_KV, IDX_HEADS, TOPK = 8, 2, 8, 64
CONV_W, FCW = 31, 3
FF_2 = 2816
POOL_WINDOWS = (2, 4, 8, 16)
FILL, TAKEN, NEG = -3.0e38, float(np.float32(-3.3e38)), -1.0e30

ROTATED_BEFORE_C = 16
SLOTS = 3
UNIT = 2048
BANKS = 8

ROWS = [("attn_norm", 32), ("ffn_norm", 32), ("final_norm", 8), ("a_subln", 2), ("b_q_norm", 3),
        ("b_kv_norm", 2), ("ln_in_g_2", 8), ("ln_in_b_2", 8), ("ln1_g_2", 16), ("ln1_b_2", 16),
        ("ln2_g_2", 16), ("ln2_b_2", 16), ("pool_scale_2", 4), ("conv_dw_w_2", 2 * CONV_W * 2),
        ("conv_dw_b_2", 4), ("conv_ln_g_2", 4), ("conv_ln_b_2", 4), ("ffn_dw_w_2", 2 * FCW * 44),
        ("ffn_dw_b_2", 88)]
Z_POOL, Z_CONV, Z_Q, Z_K, Z_V, Z_QI, Z_KI, Z_WI, Z_GATE = 0, 256, 768, 1280, 1408, 1536, 2048, 2112, 2120
B_ROWS = ([(Z_POOL + P * i, P) for i in range(10)] + [(Z_K, HD), (Z_K + HD, HD)]
          + [(Z_QI + P * i, P) for i in range(4)] + [(Z_KI, HD)] + [(Z_GATE + P * i, P) for i in range(24)])
B_POOL, B_CONV, B_Q, B_K, B_QI, B_KI, B_GATE = 0, 2, 6, 10, 12, 16, 17


def row_starts():
    at, n = {}, 0
    for name, rows in ROWS:
        at[name] = n
        n += rows
    for l in range(DEPTH_2):
        at["b_in", l] = n
        n += len(B_ROWS)
    return at, n


ROW, N_ROWS = row_starts()
ROW_TILES = -(-N_ROWS // P)


class Item:

    def __init__(self, bank, free):
        self.bank, self.free, self.done, self.step_done, self.step_free = bank, free, 0, 0, 0


class Unit:

    def __init__(self, index, loads, span=0, step_done=0):
        self.index, self.loads, self.slot = index, loads, index % SLOTS
        self.span, self.done, self.step_done = span, 0, step_done

    def at(self, i):
        u = Unit(self.index + i * self.span, self.loads)
        u.done = self.done + i * self.step_done
        return u


def build(nc, t, stages=99):
    with ExitStack() as ctx:
        def sb(name, shape, dt=F32, where=None):
            return (where or ctx).enter_context(nc.sbuf_tensor(name, shape, dt))

        def sem(name):
            return ctx.enter_context(nc.semaphore(name))

        raw = [sb(f"weights{s}", [P, UNIT]) for s in range(SLOTS)]
        w_hi = [sb(f"weights_hi{s}", [P, UNIT], F32R) for s in range(SLOTS)]
        w_lo = [sb(f"weights_lo{s}", [P, UNIT], F32R) for s in range(SLOTS)]
        xT = sb("xT", [P, KT, T])
        hT = sb("hT", [P, KT, T])
        h_hi = sb("h_hi", [P, KT, T], F32R)
        h_lo = sb("h_lo", [P, KT, T], F32R)
        sq = sb("sq", [P, KT, T])
        pres = sb("pres", [P, 6 * T])
        rots = sb("rots", [P, 4 * T])
        tab = sb("tab", [P, 6, T])
        rotm = sb("rotm", [P, 3, P])
        ident = sb("ident", [P, P])
        ones = sb("ones", [P, P])
        pcol = sb("pcol", [P, ROW_TILES * P])
        brow = sb("brow", [1, DEPTH_2, 136])
        eps = sb("eps", [P, 4])
        std = sb("std", [P, 16])
        rs = sb("rs", [P, 16])
        negmax = [sb(f"negmax{i}", [P, 2]) for i in range(4)]
        esum = [sb(f"esum{i}", [P, 2]) for i in range(4)]
        erec = [sb(f"erec{i}", [P, 2]) for i in range(4)]
        lams = sb("lams", [P, 4])
        lame = sb("lame", [P, 4])
        neglam = sb("neglam", [P, 2])
        subg = sb("subg", [P, 2])
        invf = sb("invf", [P, 1])
        wi = sb("wi", [P, 2, 8])
        m8 = sb("m8", [P, 8])
        idle = sb("idle", [P, 4])
        banks = [ctx.enter_context(nc.psum_tensor(f"bank{b}", [P, 512], F32)) for b in range(BANKS)]

        with ExitStack() as area:
            Q = sb("Q", [P, 6144], where=area)
            K = sb("K", [P, 6144], where=area)
            V = sb("V", [P, 6144], where=area)
        with ExitStack() as area:
            hid_hi = sb("hid_hi", [P, FT * T], F32R, where=area)
            hid_lo = sb("hid_lo", [P, FT * T], F32R, where=area)
        with ExitStack() as area:
            G = sb("G", [P, 24 * T], where=area)
            Y = sb("Y", [P, 12 * T], where=area)
            attn_hi = sb("attn_hi", [P, 4, T], F32R, where=area)
            attn_lo = sb("attn_lo", [P, 4, T], F32R, where=area)
            poolw = sb("poolw", [P, DEPTH_2, 2, P], where=area)
            Z = sb("Z", [P, 4352], where=area)
            pool_hi = sb("pool_hi", [P, 2, T], F32R, where=area)
            pool_lo = sb("pool_lo", [P, 2, T], F32R, where=area)
            conv_hi = sb("conv_hi", [P, 2, T], F32R, where=area)
            conv_lo = sb("conv_lo", [P, 2, T], F32R, where=area)

        xrows = Q[:, 0:2048].rearrange("p (t n) -> p t n", t=NT)
        hflat = hT[:].rearrange("p m n -> p (m n)")
        expoT = [hflat[:, 1024 * i:1024 * (i + 1)] for i in range(2)]
        pre = [pres[:, 2 * T * i:2 * T * (i + 1)] for i in range(3)]
        rot = [rots[:, 2 * T * i:2 * T * (i + 1)] for i in range(2)]
        cmask = rots[:]
        prow1 = hflat[:, 0:P]
        prow2 = K[:, 2048:2048 + (ROW_TILES - 1) * P].rearrange("p (r n) -> p r n", n=P)
        qT = Q[:].rearrange("p (m n) -> p m n", n=T)
        kT = K[:].rearrange("p (m n) -> p m n", n=T)
        vA = V[:, 0:2048].rearrange("p (t n) -> p t n", t=NT)
        vC = V[:].rearrange("p (t n) -> p t n", t=NT)
        expoA = [V[:, 2048:3072], V[:, 3072:4096], pres[:, 0:1024]]
        expo = [sq[:].rearrange("p m n -> p (m n)")[:, 1024 * i:1024 * (i + 1)] for i in range(2)]
        expo.append(pres[:, 0:1024])
        latT = V[:, 4096:4096 + 5 * T].rearrange("p (m n) -> p m n", n=T)
        oT = V[:, 4096:6144].rearrange("p (m n) -> p m n", n=T)
        kr = V[:, 5376:5632]
        lamv = K[:, 0:512].rearrange("p (v d) -> p v d", d=HD)
        lamp = K[:, 512:768].rearrange("p (v d) -> p v d", d=HD)
        yT = Y[:].rearrange("p (m n) -> p m n", n=T)
        qD, kidT, kdT, qiT = yT[:, 0:4], yT[:, 4], yT[:, 5:7], yT[:, 7:11]
        vD = Y[:, 11 * T:12 * T].rearrange("p (t n) -> p t n", t=NT)
        gates = G[:].rearrange("p (m n) -> p m n", n=T)
        PADW = 32
        pool_u = Z[:, 0:576].rearrange("p (m n) -> p m n", m=2)
        pool_w2 = Z[:, 576:1152].rearrange("p (m n) -> p m n", m=2)
        pool_w4 = Z[:, 1152:1728].rearrange("p (m n) -> p m n", m=2)
        conv_a = Z[:, 1152:1664].rearrange("p (m n) -> p m n", m=2)
        conv_h = Z[:, 1728:2304].rearrange("p (m n) -> p m n", m=2)
        conv_y = Z[:, 2304:2816].rearrange("p (m n) -> p m n", m=2)
        mixed = Z[:, 2816:3328].rearrange("p (m n) -> p m n", m=2)
        score = Z[:, 3328:3840].rearrange("p (t n) -> p t n", t=NT)
        work = Z[:, 3840:4352].rearrange("p (t n) -> p t n", t=NT)
        tabd, inv_cnt = tab[:, 4:6, :], tab[:, 2:4, :]
        relu = [expoT[0][:, 0:512], expoT[1][:, 0:512]]
        pos_i = tab[:, 4, :].bitcast(I32)
        ang, turns, scr, red = (K[:, 1024 + T * i:1024 + T * (i + 1)] for i in range(4))

        pe_done = sem("pe_done")
        bank_free = [sem(f"bank_free{b}") for b in range(BANKS)]
        landed = [sem(f"weights_landed{s}") for s in range(SLOTS)]
        hi_ready = sem("hi_ready")
        lo_ready = sem("lo_ready")
        x_landed = sem("x_landed")
        rows_landed = sem("rows_landed")
        rows2_landed = sem("rows2_landed")
        consts_landed = sem("consts_landed")
        consts2_landed = sem("consts2_landed")
        cmask_landed = sem("cmask_landed")
        lam_landed = sem("lam_landed")
        pos_landed = sem("pos_landed")
        poolw_zeroed = sem("poolw_zeroed")
        area_free = sem("area_free")
        poolw_landed = sem("poolw_landed")
        out_stored = sem("out_stored")
        ident_ready = sem("ident_ready")
        lam_sums = sem("lam_sums")
        lam_exps = sem("lam_exps")
        angles_ready = sem("angles_ready")
        sines_ready = sem("sines_ready")
        squares_ready = sem("squares_ready")
        rs_ready = sem("rs_ready")
        to_split = sem("to_split")
        hi_part = sem("hi_part")
        h_ready = sem("h_ready")
        centred = sem("centred")
        ln_ready = sem("ln_ready")
        y_ready = sem("y_ready")
        rot_ready = sem("rot_ready")
        kr_ready = sem("kr_ready")
        kr_spread = sem("kr_spread")
        negmax_ready = sem("negmax_ready")
        exp_ready = sem("exp_ready")
        probs_ready = sem("probs_ready")
        dve_step = sem("dve_step")
        product_ready = sem("product_ready")
        hid_step = sem("hid_step")
        hidden_ready = sem("hidden_ready")
        taps_started = sem("taps_started")
        gate_ready = sem("gate_ready")
        score_step = sem("score_step")
        score_masked = sem("score_masked")
        picked = sem("picked")
        keep_ready = sem("keep_ready")
        conv_out = sem("conv_out")
        mixed_ready = sem("mixed_ready")
        branch_ready = sem("branch_ready")
        act_step = sem("act_step")

        def phases():
            yield "start", 0
            n = 0
            for i in range(DEPTH):
                kind = "ABC"[i % 3]
                yield "rms", (i, "attn_norm", KT * i)
                if i == 0:
                    yield "lambda", 0
                if i == DEPTH - 1:
                    yield "second", 0
                yield kind, i
                yield "rms", (i, "ffn_norm", KT * i)
                if i == DEPTH - 1:
                    yield "rows2", 0
                yield "ffn", i
                n += 1
                if n >= stages:
                    yield "end", 0
                    return
            yield "final", 0
            yield "ln", ("ln_in_g_2", "ln_in_b_2", 0)
            for l in range(DEPTH_2):
                yield "mix", l
                yield "ln", ("ln1_g_2", "ln1_b_2", KT * l)
                yield "ffn2", l
                n += 1
                last = n >= stages or l == DEPTH_2 - 1
                yield ("ln_last" if last else "ln"), ("ln2_g_2", "ln2_b_2", KT * l)
                if last:
                    break
            yield "end", 0

        def row_loads(part):
            out = []

            def add(at, src, c0=0, c1=P):
                n, done = src.shape[0], 0
                while done < n:
                    r = at + done
                    m = min(n - done, P - r % P)
                    dst = prow1 if r < P else prow2[:, r // P - 1, :]
                    if (r >= P) == part:
                        out.append((dst[r % P:r % P + m, c0:c1], src[done:done + m, :]))
                    done += m

            for name, rows in ROWS:
                a = t[name]
                if len(a.shape) == 1:
                    a = a.rearrange("(r n) -> r n", n=P)
                elif len(a.shape) == 2:
                    a = a.rearrange("l (r n) -> (l r) n", n=P)
                else:
                    a = a.rearrange("l c (r n) -> (l c r) n", n=P)
                add(ROW[name], a)
            for l in range(DEPTH_2):
                b, at = t["b_in_2"][l], ROW["b_in", l]
                for first, n, col in ((B_POOL, 10, Z_POOL), (B_QI, 4, Z_QI), (B_GATE, 24, Z_GATE)):
                    add(at + first, b[col:col + n * P].rearrange("(r n) -> r n", n=P))
                add(at + B_K, b[Z_K:Z_K + 2 * HD].rearrange("(r n) -> r n", n=P))
                for half in range(2):
                    k0 = Z_K + HD * (1 - half)
                    add(at + B_K + 1, b[k0:k0 + HD].rearrange("(r n) -> r n", n=HD), HD * half, HD * half + HD)
                    add(at + B_KI, b[Z_KI:Z_KI + HD].rearrange("(r n) -> r n", n=HD), HD * half, HD * half + HD)
            return out

        def rows_of(name, l):
            w = t[name] if l is None else t[name][l]
            return w.rearrange("(k p) n -> p k n", p=P)

        def view(width):
            return lambda slot: slot[:, 0:UNIT // width * width].rearrange("p (k n) -> p k n", n=width)

        def block_loads(name, l, n0, width=256, at=0, k=KT):
            w = rows_of(name, l)
            cols = slice(n0, n0 + width) if isinstance(n0, int) else bass.ds(n0, width)
            return [(lambda s, a=a: view(UNIT // k)(s)[:, a:a + k // 2, at:at + width], w[:, a:a + k // 2, cols])
                    for a in (0, k // 2)]

        def deep_loads(name, l, k0, n0=0):
            w = rows_of(name, l)
            return [(lambda s, j=j: view(1024)(s)[:, j, :],
                     w[:, k0 + j, n0:n0 + 1024] if isinstance(k0, int)
                     else w[:, bass.ds(k0 + j, 1), n0:n0 + 1024].rearrange("p k n -> p (k n)")) for j in range(2)]

        def gate_loads(name, l, n0):
            w = rows_of(name, l)
            out = []
            for z in range(2):
                cols = slice(n0 + z * FFN, n0 + z * FFN + P) if isinstance(n0, int) else bass.ds(n0 + z * FFN, P)
                out.append((lambda s, z=z: view(256)(s)[:, :, z * P:(z + 1) * P], w[:, :, cols]))
            return out

        block = ctx.enter_context(nc.Block())
        units, items, total = [], {}, [0]

        @block.tensor
        def _(pe):
            n_done = [0]
            uses = [0] * BANKS
            tally = {}

            def count(s, n=1):
                tally[s.name] = tally.get(s.name, 0) + n
                return tally[s.name]

            def open_item(bank, released=True):
                if uses[bank]:
                    pe.wait_ge(bank_free[bank], uses[bank])
                uses[bank] += released
                return Item(bank, uses[bank])

            def close(ins, *what):
                n_done[0] += 1
                ins.then_inc(pe_done, 1)
                for w in what:
                    w.done = n_done[0]

            def next_unit(loads):
                u = Unit(total[0], loads)
                total[0] += 1
                units.append(u)
                pe.wait_ge(lo_ready, u.index + 1)
                return u

            def loop_units(loads, n, rounds, per):
                for j in range(n):
                    u = Unit(total[0] + j, lambda r, j=j: loads(r, j), span=n, step_done=per)
                    u.rounds = rounds
                    units.append(u)
                    yield u

            def parts(u, width):
                return view(width)(w_hi[u.slot]), view(width)(w_lo[u.slot])

            def product(out, a, b, first, last):
                for n, (x, y) in enumerate(((a[0], b[0]), (a[0], b[1]), (a[1], b[0]))):
                    mm = nc.tensor.matmul(out, x, y, start=(first and n == 0), stop=(last and n == 2),
                                          skip_group_check=True)
                return mm

            def tiles(outs, w, cols, src, k=KT, gate=None):
                for j in range(k):
                    if gate is not None:
                        pe.wait_ge(h_ready, gate + j + 1)
                    s = [x[:, j, :] for x in src]
                    for m, (o, c) in enumerate(zip(outs, cols)):
                        mm = product(o, [x[:, j, c:c + P] for x in w], s, j == 0 and m == 0, j == k - 1)
                return mm

            def halves(bank):
                return [banks[bank][:, 0:T], banks[bank][:, T:2 * T]]

            def token_major(out, w, cols, tt, k=KT, k0=0, last=True):
                for j in range(k):
                    mm = product(out, [x[:, k0 + j, tt * P:(tt + 1) * P] for x in h], [x[:, j, cols] for x in w],
                                 j == 0, last and j == k - 1)
                return mm

            h = (h_hi, h_lo)

            def stats(bank, col, src, ts):
                for tt in range(NT):
                    for n, j in enumerate(ts):
                        mm = nc.tensor.matmul(banks[bank][:, col + tt:col + tt + 1], src[:, j, tt * P:(tt + 1) * P],
                                              ones[:, 0:1], start=(n == 0), stop=(n == len(ts) - 1))
                return mm

            def spread(bank, at, col):
                for tt in range(NT):
                    mm = nc.tensor.matmul(banks[bank][:, at + tt * P:at + (tt + 1) * P],
                                          rs[:, col + tt:col + tt + 1].to_broadcast([P, P]), ident[:],
                                          start=True, stop=True)
                return mm

            def start():
                pe.wait_ge(ident_ready, 3)
                pe.wait_ge(x_landed, 16)
                xs = []
                for j in range(4):
                    x = open_item(j)
                    for kk in range(2):
                        for tt in range(NT):
                            mm = nc.tensor.transpose(banks[j][:, kk * T + tt * P:kk * T + (tt + 1) * P],
                                                     xrows[:, tt, (2 * j + kk) * P:(2 * j + kk + 1) * P], ident[:])
                    close(mm, x)
                    xs.append(x)
                pe.wait_ge(rows_landed, 16 * len(row_loads(0)))
                r = open_item(4)
                close(nc.tensor.transpose(banks[4][:, 0:P], prow1, ident[:]), r)
                items["start"] = xs, r
                for b in (5, 6):
                    x = open_item(b)
                    close(nc.tensor.matmul(banks[b][:, 0:P], ident[:], ident[:], start=True, stop=True), x)
                    items["idle", b] = x

            def rows2():
                pe.wait_ge(rows2_landed, 16 * len(row_loads(1)))
                out = []
                for j in range(0, ROW_TILES - 1, 4):
                    r = open_item(j // 4)
                    for jj in range(j, min(j + 4, ROW_TILES - 1)):
                        n = min(P, N_ROWS - (jj + 1) * P)
                        mm = nc.tensor.transpose(banks[r.bank][:, (jj - j) * P:(jj - j) * P + n], prow2[0:n, jj, :],
                                                 ident[0:n, 0:n])
                    close(mm, r)
                    out.append(r)
                items["rows2"] = out

            def rms(tag):
                pe.wait_ge(squares_ready, count(squares_ready, 4))
                s = open_item(6)
                close(stats(6, 0, sq, range(KT)), s)
                pe.wait_ge(rs_ready, count(rs_ready))
                b = open_item(7, released=False)
                close(spread(7, 0, 0), b)
                items[tag] = s, b

            def rotation(r, x, m, n=2 * T, lo=0, hi=P, i=None):
                pe.wait_ge(bank_free[x.bank], x.free if i is None else i * x.step_free + x.free)
                close(nc.tensor.matmul(banks[r.bank][lo:hi, 0:n], rotm[lo:hi, m, lo:hi],
                                       pre[x.pre][lo:hi, 0:n], start=True, stop=True), r)

            def deep(name, l, n_units, src, tag, bank0, ready, looped=False):
                head, loop, tail = [], [], []
                out = None

                def step(u, n, first, last, at=None):
                    nonlocal out
                    ready(n, None)
                    if out is None:
                        out = [open_item(bank0 + b) for b in range(4)]
                    w = parts(u, 1024)
                    for m in range(8):
                        o = halves(out[m // 2].bank)[m % 2]
                        for j in range(2):
                            s = [x[:, (2 * n + j) * T:(2 * n + j + 1) * T] for x in src]
                            mm = product(o, [x[:, j, m * P:(m + 1) * P] for x in w], s,
                                         first and j == 0 and m % 2 == 0, last and j == 1)
                        if last and m % 2 == 1 and m < 7:
                            close(mm, out[m // 2])
                    close(mm, u, *([out[3]] if last else []))

                if not looped:
                    for n in range(n_units):
                        u = next_unit(deep_loads(name, l, 2 * n))
                        step(u, n, n == 0, n == n_units - 1)
                        head.append(u)
                else:
                    for n in range(3):
                        u = next_unit(deep_loads(name, l, 2 * n))
                        step(u, n, n == 0, False)
                        head.append(u)
                    total[0] -= 3
                    done0 = n_done[0] - 3
                    n_done[0] = done0
                    with pe.Fori(1, 3) as i:
                        for n, u in enumerate(loop_units(lambda r, j: deep_loads(name, l, r * 6 + 2 * j), 3, (1, 3), 3)):
                            pe.wait_ge(lo_ready, i * 3 + (u.index + 1))
                            ready(n, i)
                            w = parts(u, 1024)
                            for m in range(8):
                                o = halves(out[m // 2].bank)[m % 2]
                                for j in range(2):
                                    s = [x[:, bass.ds(i * (6 * T) + (2 * n + j) * T, T)] for x in src]
                                    mm = product(o, [x[:, j, m * P:(m + 1) * P] for x in w], s, False, False)
                            close(mm, u)
                            loop.append(u)
                    total[0] += 9
                    n_done[0] = done0 + 9
                    for n in range(9, 11):
                        u = next_unit(deep_loads(name, l, 2 * n))
                        step(u, n, False, n == 10)
                        tail.append(u)
                items[tag] = out
                items[tag, "units"] = head, loop, tail

            def wo(name, l, tag, bank0, src_items=None):
                base = None if src_items else count(h_ready, 4) - 4

                def ready(n, i):
                    if src_items:
                        x = src_items[n]
                        pe.wait_ge(bank_free[x.bank], x.free)
                    else:
                        pe.wait_ge(h_ready, base + n + 1)
                flat = [x[:].rearrange("p m n -> p (m n)") for x in h]
                deep(name, l, 4, flat, tag, bank0, ready)

            def ffn(name_up, name_down, l, tag):
                gate = count(h_ready, KT) - KT
                hid0 = 3 + count(hidden_ready, FT) - FT
                head, body = [], []
                for j in range(3):
                    u = next_unit(gate_loads(name_up, l, j * P))
                    x = open_item(4 + j)
                    close(tiles(halves(4 + j), parts(u, 256), (0, P), h, gate=gate if j == 0 else None), x, u)
                    head.append((u, x))
                rounds = 7
                done0, total[0] = n_done[0] - 3, total[0] - 3
                n_done[0] = done0
                uses0 = [n - 1 for n in uses]
                with pe.Fori(1, rounds) as i:
                    for j, u in enumerate(loop_units(lambda r, j: gate_loads(name_up, l, r * 384 + j * P), 3, (1, rounds), 3)):
                        pe.wait_ge(lo_ready, i * 3 + (u.index + 1))
                        b = 4 + j
                        pe.wait_ge(bank_free[b], i + uses0[b])
                        x = Item(b, uses0[b] + 1)
                        x.step_done, x.step_free = 3, 1
                        close(tiles(halves(b), parts(u, 256), (0, P), h), x, u)
                        body.append((u, x))
                n_done[0] = done0 + 3 * rounds
                total[0] += 3 * rounds
                for j in range(3):
                    uses[4 + j] += rounds - 1
                u = next_unit(gate_loads(name_up, l, 21 * P))
                x = open_item(4)
                close(tiles(halves(4), parts(u, 256), (0, P), h), x, u)
                items[tag, "up"] = head, body, [(u, x)]

                def ready(n, i):
                    pe.wait_ge(hidden_ready, hid0 + 2 * n + 2 if i is None else i * 6 + (hid0 + 2 * n + 2))
                deep(name_down, l, 11, (hid_hi, hid_lo), (tag, "down"), 0, ready, looped=True)

            def transposes(hd, plan, expos):
                pe.wait_ge(probs_ready, count(probs_ready))
                out = []
                for g, moves in enumerate(plan):
                    it = open_item(4 + (hd * len(plan) + g) % 2)
                    for a, b in moves:
                        mm = nc.tensor.transpose(banks[it.bank][:, b:b + P], expos[hd % 3][:, a:a + P], ident[:])
                    close(mm, it)
                    out.append(it)
                return out

            plain = [[(T * tt + kt * P, kt * T + tt * P) for kt in range(2) for tt in range(NT)]]

            def attn_a(i):
                l = i // 3
                gate = count(h_ready, KT) - KT
                us, xs, rr, vs = [], [], [], []
                pending = None
                for n in range(12):
                    u = next_unit(block_loads("a_w_qkv", l, 256 * n))
                    w = parts(u, 256)
                    if n < 8:
                        x = open_item(n % 3)
                        x.pre = n % 3
                        close(tiles(halves(x.bank), w, (0, P), h, gate=gate if n == 0 else None), x, u)
                        xs.append(x)
                    else:
                        v = open_item(5 + n % 2)
                        for tt in range(NT):
                            mm = token_major(halves(v.bank)[tt], w, slice(0, 256), tt)
                        close(mm, v, u)
                        vs.append(v)
                    if pending is not None:
                        r = open_item(3 + (n - 1) % 2)
                        rotation(r, pending, 0)
                        rr.append(r)
                    pending = x if n < 8 else None
                    us.append(u)
                items[i, "qk"], items[i, "rot"], items[i, "v"], items[i, "units"] = xs, rr, vs, us
                pe.wait_ge(rot_ready, count(rot_ready, 8))
                for v in vs[-2:]:
                    pe.wait_ge(bank_free[v.bank], v.free)
                S, TT, O = [], [], []
                for hd in range(A_HEADS + 3):
                    if hd < A_HEADS:
                        for sub in range(2):
                            s = open_item((2 * hd + sub) % 4)
                            a = HD * sub
                            for tt in range(NT):
                                mm = nc.tensor.matmul(banks[s.bank][:, tt * T:(tt + 1) * T],
                                                      qT[a:a + HD, hd, tt * P:(tt + 1) * P],
                                                      qT[a:a + HD, KT + hd, :], start=True, stop=True)
                            close(mm, s)
                            S.append(s)
                    if 2 <= hd < A_HEADS + 2:
                        TT.append(transposes(hd - 2, plain, expoA))
                    if hd >= 3:
                        g = hd - 3
                        if g % 2 == 0:
                            o = open_item(6 + (g // 2) % 2)
                            O.append(o)
                        pe.wait_ge(bank_free[TT[g][0].bank], TT[g][0].free)
                        for kt in range(NT):
                            mm = nc.tensor.matmul(halves(o.bank)[g % 2], vA[:, kt, g * P:(g + 1) * P],
                                                  expoT[g % 2][:, kt * T:(kt + 1) * T],
                                                  start=(kt == 0), stop=(kt == NT - 1))
                        close(mm, o)
                        TT[g][0].used = n_done[0]
                items[i, "S"], items[i, "T"], items[i, "O"] = S, TT, O
                pe.wait_ge(squares_ready, count(squares_ready, 4))
                s = open_item(5)
                for hd in range(A_HEADS):
                    mm = stats(5, 2 * hd, sq, [hd])
                close(mm, s)
                pe.wait_ge(rs_ready, count(rs_ready))
                sp_items = []
                for g in range(4):
                    b = open_item(g)
                    for hh in range(2):
                        mm = spread(g, hh * T, 2 * (2 * g + hh))
                    close(mm, b)
                    sp_items.append(b)
                items[i, "subln"] = s, sp_items
                wo("a_w_o", l, (i, "wo"), 4)

            def attn_64(tag, heads, score_parts, pv_parts, plan, v_of, masked=True):
                S, TT, O = [], [], []
                per = 2 if len(plan) == 2 else 1
                for hd in range(heads + 3):
                    if hd < heads:
                        mine = []
                        for n, part in enumerate(score_parts(hd)):
                            s = open_item((per * hd + n) % 4)
                            for a, b, lhsT, rhs in part:
                                mm = nc.tensor.matmul(banks[s.bank][:, a:b], lhsT, rhs, start=True, stop=True)
                            close(mm, s)
                            mine.append(s)
                        S.append(mine)
                    if 2 <= hd < heads + 2:
                        TT.append(transposes(hd - 2, plan, expo))
                    if hd >= 3:
                        g = hd - 3
                        if g % 4 == 0:
                            o = open_item(6 + (g // 4) % 2)
                            O.append(o)
                        for it in TT[g]:
                            pe.wait_ge(bank_free[it.bank], it.free)
                        a = HD * (g % 2)
                        c0 = (g // 2 % 2) * T
                        for n, (v, e0, e1, q0, q1) in enumerate(pv_parts):
                            mm = nc.tensor.matmul(banks[o.bank][a:a + HD, c0 + q0:c0 + q1], v_of(g, *v),
                                                  expoT[g % 2][:, e0:e1], start=(n == 0), stop=(n == len(pv_parts) - 1))
                        close(mm, o)
                        for it in TT[g]:
                            it.used = n_done[0]
                items[tag, "S"], items[tag, "T"], items[tag, "O"] = S, TT, O

            plain_pv = [((kt,), kt * T, (kt + 1) * T, 0, T) for kt in range(2)]

            def attn_b(i):
                gate = count(h_ready, KT) - KT
                us, raw_items = [], [open_item(b) for b in range(3)]
                for n in range(2):
                    u = next_unit(block_loads("b_w_a", 0, 256 * n))
                    close(tiles(halves(n), parts(u, 256), (0, P), h, gate=gate if n == 0 else None), raw_items[n], u)
                    us.append(u)
                w = rows_of("b_w_a", 0)
                u = next_unit([(lambda s: view(256)(s)[:, :, 0:P], w[:, :, 512:640]),
                               (lambda s: view(256)(s)[:, :, 192:224], w[:, :, 640:672])])
                close(tiles(halves(2), parts(u, 256), (0, P), h), raw_items[2], u)
                raw_items[2].pre = 2
                us.append(u)
                pe.wait_ge(squares_ready, count(squares_ready, 3))
                s = open_item(6)
                stats(6, 0, sq, range(3))
                close(stats(6, 2, sq, range(3, 5)), s)
                r = open_item(3)
                rotation(r, raw_items[2], 1, n=T, lo=64, hi=96)
                pe.wait_ge(rs_ready, count(rs_ready))
                b = open_item(7, released=False)
                spread(7, 0, 0)
                close(spread(7, T, 2), b)
                items[i, "raw"], items[i, "stat"], items[i, "krot"] = raw_items, (s, b), r
                pe.wait_ge(h_ready, count(h_ready, 5))
                xs, rr, ks, vs = [], [], [], []
                pending = None
                wq = rows_of("b_w_qb", 0)
                for q in range(4):
                    u = next_unit([(lambda s, z=z: s[:, 0:1152].rearrange("p (k n) -> p k n", n=384)[:, :, 192 * z:192 * z + 192],
                                    wq[:, :, q * 384 + 192 * z:q * 384 + 192 * z + 192]) for z in range(2)])
                    w = [x[:, 0:1152].rearrange("p (k n) -> p k n", n=384) for x in (w_hi[u.slot], w_lo[u.slot])]
                    for m in range(2):
                        n = 2 * q + m
                        x = open_item(n % 3)
                        x.pre = n % 3
                        for hh in range(2):
                            col = (2 * m + hh) * 96
                            for j in range(3):
                                mm = product(banks[x.bank][0:96, hh * T:(hh + 1) * T], [y[:, j, col:col + 96] for y in w],
                                             [y[:, j, :] for y in h], j == 0, j == 2)
                        close(mm, x, *([u] if m else []))
                        xs.append(x)
                        if pending is not None:
                            r = open_item(3 + (n - 1) % 2)
                            rotation(r, pending, 1, hi=96)
                            rr.append(r)
                        pending = x
                    us.append(u)
                for half in range(2):
                    u = next_unit(deep_loads("b_w_kvb", 0, 0, half * 1024))
                    w = parts(u, 1024)
                    for m in range(4):
                        x = open_item(5 + m % 2)
                        for hh in range(2):
                            col = (2 * m + hh) * P
                            for j in range(2):
                                mm = product(halves(x.bank)[hh], [y[:, j, col:col + P] for y in w],
                                             [y[:, 3 + j, :] for y in h], j == 0, j == 1)
                        close(mm, x)
                        ks.append(x)
                        if m == 0 and half == 0:
                            r = open_item(3 + 7 % 2)
                            rotation(r, pending, 1, hi=96)
                            rr.append(r)
                    for tt in range(NT):
                        v = open_item(half * 2 + tt)
                        for j in range(2):
                            mm = product(banks[v.bank][:].rearrange("p (h d) -> p h d", d=HD),
                                         [y[:, 3 + j, tt * P:(tt + 1) * P] for y in h],
                                         [y[:, j, :].rearrange("p (h d) -> p h d", d=P)[:, :, HD:P] for y in w],
                                         j == 0, j == 1)
                        close(mm, v, *([u] if tt else []))
                        vs.append(v)
                    us.append(u)
                items[i, "qk"], items[i, "rot"], items[i, "k"], items[i, "v"], items[i, "units"] = xs, rr, ks, vs, us
                pe.wait_ge(rot_ready, count(rot_ready, 8))
                pe.wait_ge(kr_spread, count(kr_spread))
                for v in ks[-2:] + vs:
                    pe.wait_ge(bank_free[v.bank], v.free)
                attn_64(i, B_HEADS,
                        lambda hd: [[(tt * T, (tt + 1) * T, qT[0:96, hd, tt * P:(tt + 1) * P], kT[0:96, hd, :])
                                     for tt in range(NT)]],
                        plain_pv, plain, lambda hd, kt: vA[:, kt, hd * HD:(hd + 1) * HD])
                wo("b_w_o", 0, (i, "wo"), 0, items[i, "O"])

            c_plan = [[(512 * tt + kt * P, kt * T + tt * P) for kt in range(2) for tt in range(NT)],
                      [(512 * tt + T + g * P, g * T + tt * P) for g in range(2) for tt in range(NT)]]
            c_pv = ([((0, kt), kt * T, (kt + 1) * T, 0, T) for kt in range(2)]
                    + [((g, tt), 512 + (g - 1) * T + tt * P, 512 + (g - 1) * T + (tt + 1) * P, tt * P, (tt + 1) * P)
                       for g in (1, 2) for tt in range(NT)])

            def attn_c(i):
                gate = count(h_ready, KT) - KT
                done0, uses0 = n_done[0], list(uses)
                per, seen = 20, {b: 0 for b in range(5)}
                xs, rr, vs, us = [], [], [], []
                with pe.Fori(0, C_GROUPS) as g:
                    pending = None

                    def take(bank):
                        pe.wait_ge(bank_free[bank], g * 4 + (uses0[bank] + seen[bank]))
                        seen[bank] += 1
                        x = Item(bank, uses0[bank] + seen[bank])
                        x.step_done, x.step_free = per, 4
                        return x

                    for n, u in enumerate(loop_units(lambda r, j: block_loads("c_w_qkv", 0, r * 3072 + j * 256), 12, (0, C_GROUPS), per)):
                        pe.wait_ge(lo_ready, g * 12 + (u.index + 1))
                        w = parts(u, 256)
                        if n < 8:
                            x = take(n % 2)
                            x.pre = n % 2
                            close(tiles(halves(x.bank), w, (0, P), h, gate=gate if n == 0 else None), x, u)
                            xs.append(x)
                        else:
                            v = take(4)
                            for tt in range(NT):
                                mm = token_major(halves(4)[tt], w, slice(0, 256), tt)
                            close(mm, v, u)
                            vs.append(v)
                        if pending is not None:
                            r = take(2 + (n - 1) % 2)
                            rotation(r, pending, 0, i=g)
                            r.step_done = per
                            rr.append(r)
                        pending = x if n < 8 else None
                        us.append(u)
                assert n_done[0] == done0 + per and all(seen[b] == 4 for b in seen)
                n_done[0] = done0 + per * C_GROUPS
                total[0] += 12 * C_GROUPS
                for b in range(5):
                    uses[b] += 4 * C_GROUPS
                items[i, "qk"], items[i, "rot"], items[i, "v"], items[i, "units"] = xs, rr, vs, us
                pe.wait_ge(rot_ready, count(rot_ready, 8 * C_GROUPS))
                pe.wait_ge(bank_free[4], uses[4])

                def scores(hd):
                    a = HD * (hd % 2)
                    out = []
                    for tt in range(NT):
                        q0, q1 = tt * P, (tt + 1) * P
                        out.append([(0, T, qT[a:a + HD, hd // 2, q0:q1], kT[a:a + HD, hd // 2, :])]
                                   + [(g * P + P, g * P + 2 * P, qT[a:a + HD, 8 * g + hd // 2, q0:q1],
                                       kT[a:a + HD, 8 * g + hd // 2, q0:q1]) for g in (1, 2)])
                    return out

                attn_64(i, C_HEADS, scores, c_pv, c_plan,
                        lambda hd, g, kt: vC[:, kt, g * 1024 + hd * HD:g * 1024 + (hd + 1) * HD])
                wo("c_w_o", 0, (i, "wo"), 0, items[i, "O"])

            def ln(tag, last):
                s = open_item(6)
                close(stats(6, 0, xT, range(KT)), s)
                pe.wait_ge(bank_free[6], s.free)
                m = open_item(5, released=False)
                close(spread(5, 0, 0), m)
                pe.wait_ge(squares_ready, count(squares_ready, 4))
                v = open_item(6)
                close(stats(6, 0, sq, range(KT)), v)
                pe.wait_ge(rs_ready, count(rs_ready))
                b = open_item(7, released=False)
                close(spread(7, 0, 0), b)
                count(ln_ready, KT)
                items[tag] = s, m, v, b

            def mix(l):
                gate = count(h_ready, KT) - KT
                it, us = {}, []

                def pair(loads, bank, first=False, cols=(0, P)):
                    u = next_unit(loads)
                    x = open_item(bank)
                    close(tiles(halves(bank)[:len(cols)], parts(u, 256), cols, h, gate=gate if first else None), x, u)
                    us.append(u)
                    return x

                wz = rows_of("w_in_2", l)

                def twice(col, width):
                    return [(lambda s, z=z: view(256)(s)[:, :, width * z:width * (z + 1)], wz[:, :, col:col + width])
                            for z in range(2)]

                it["pool"] = pair(block_loads("w_in_2", l, Z_POOL), 0, first=True)
                it["conv_a"] = pair(block_loads("w_in_2", l, Z_CONV), 1)
                it["conv_g"] = pair(block_loads("w_in_2", l, Z_CONV + 256), 2)
                xs, rr = [], []
                plan = [(block_loads("w_in_2", l, Z_Q), (0, P)), (block_loads("w_in_2", l, Z_Q + 256), (0, P)),
                        (twice(Z_K, 2 * HD), (0, HD)), (block_loads("w_in_2", l, Z_QI), (0, P)),
                        (block_loads("w_in_2", l, Z_QI + 256), (0, P)), (twice(Z_KI, HD), (0,))]
                for n, (loads, cols) in enumerate(plan):
                    x = pair(loads, (3, 0, 1)[n % 3], cols=cols)
                    x.pre = n % 3
                    xs.append(x)
                    if n:
                        r = open_item(4 + (n - 1) % 2)
                        rotation(r, xs[n - 1], 2)
                        rr.append(r)
                u = next_unit([(lambda s: view(256)(s)[:, :, 0:P], wz[:, :, Z_V:Z_V + P]),
                               (lambda s: view(256)(s)[:, :, P:P + 8], wz[:, :, Z_WI:Z_WI + 8])])
                v = open_item(2)
                for tt in range(NT):
                    o = banks[2][:, tt * 136:(tt + 1) * 136]
                    token_major(o, parts(u, 256), slice(0, 136), tt, last=False)
                    mm = nc.tensor.matmul(o, ones[0:1, :], brow[0:1, l, :], start=False, stop=True, skip_group_check=True)
                close(mm, v, u)
                us.append(u)
                it["v"] = v
                r = open_item(5)
                rotation(r, xs[5], 2, n=T)
                rr.append(r)
                it["qk"], it["rot"], it["units"] = xs, rr, us
                pe.wait_ge(rot_ready, count(rot_ready, 6))
                it["idx"] = []
                for hd in range(IDX_HEADS):
                    s = open_item([0, 2, 3, 6][hd % 4])
                    a = HD * (hd % 2)
                    for tt in range(NT):
                        mm = nc.tensor.matmul(banks[s.bank][:, tt * T:(tt + 1) * T],
                                              qiT[a:a + HD, hd // 2, tt * P:(tt + 1) * P], kidT[a:a + HD, :],
                                              start=True, stop=True)
                    close(mm, s)
                    it["idx"].append(s)
                done0, uses0 = n_done[0], list(uses)
                body, rounds = [], 4
                with pe.Fori(0, rounds) as i:
                    for j, u in enumerate(loop_units(lambda r, j: block_loads("w_in_2", l, r * 768 + (Z_GATE + j * 256)), 3, (0, rounds), 3)):
                        pe.wait_ge(lo_ready, i * 3 + (u.index + 1))
                        b = (1, 4, 5)[j]
                        pe.wait_ge(bank_free[b], i + uses0[b])
                        x = Item(b, uses0[b] + 1)
                        x.step_done, x.step_free = 3, 1
                        close(tiles(halves(b), parts(u, 256), (0, P), h), x, u)
                        body.append((u, x))
                n_done[0] = done0 + 3 * rounds
                total[0] += 3 * rounds
                for b in (1, 4, 5):
                    uses[b] += rounds
                it["gates"] = body
                pe.wait_ge(mixed_ready, count(mixed_ready))
                if l == 0:
                    pe.wait_ge(poolw_landed, 16 * 4 * DEPTH_2)
                x = open_item(7)
                for m in range(2):
                    mm = nc.tensor.matmul(halves(7)[m], poolw[:, l, m, :], mixed[:, m, :], start=True, stop=True)
                close(mm, x)
                it["poolmix"] = x
                pe.wait_ge(conv_out, count(conv_out))
                s = open_item(6)
                close(stats(6, 0, conv_y, range(2)), s)
                pe.wait_ge(bank_free[6], s.free)
                m_ = open_item(5, released=False)
                close(spread(5, 0, 0), m_)
                pe.wait_ge(squares_ready, count(squares_ready))
                v = open_item(6)
                close(stats(6, 0, sq, range(2)), v)
                pe.wait_ge(rs_ready, count(rs_ready))
                b = open_item(7, released=False)
                close(spread(7, 0, 0), b)
                it["cln"] = s, m_, v, b
                pe.wait_ge(ln_ready, count(ln_ready, 2))
                tag = ("m", l)
                attn_64(tag, N_HEADS,
                        lambda hd: [[(tt * T, (tt + 1) * T, qD[HD * (hd % 2):HD * (hd % 2) + HD, hd // 2, tt * P:(tt + 1) * P],
                                      kdT[HD * (hd % 2):HD * (hd % 2) + HD, (hd + hd // 4) % 2, :]) for tt in range(NT)]],
                        plain_pv, plain, lambda hd, kt: vD[:, kt, (hd // 4) * HD:(hd // 4 + 1) * HD])
                ready0 = count(branch_ready, 2) - 2

                def flat(*xs):
                    return [x[:].rearrange("p m n -> p (m n)") for x in xs]

                deep("w_pool_out_2", l, 1, flat(pool_hi, pool_lo), (tag, "pool"), 0,
                     lambda n, i: pe.wait_ge(branch_ready, ready0 + 1))
                deep("w_conv_out_2", l, 1, flat(conv_hi, conv_lo), (tag, "conv"), 4,
                     lambda n, i: pe.wait_ge(branch_ready, ready0 + 2))
                O = items[tag, "O"]
                deep("w_attn_out_2", l, 2, flat(attn_hi, attn_lo), (tag, "attn"), 0,
                     lambda n, i: pe.wait_ge(bank_free[O[n].bank], O[n].free))
                wo("w_o_2", l, (tag, "wo"), 4)
                items["m", l] = it

            def end():
                if stages >= 5:
                    pe.wait_ge(y_ready, 2 * KT)
                else:
                    for x in items[last_add[0]]:
                        pe.wait_ge(bank_free[x.bank], x.free)
                out = []
                for tt in range(NT):
                    for g in range(2):
                        x = open_item(2 * tt + g)
                        for kk in range(4):
                            mm = nc.tensor.transpose(banks[x.bank][:, kk * P:(kk + 1) * P],
                                                     xT[:, 4 * g + kk, tt * P:(tt + 1) * P], ident[:])
                        close(mm, x)
                        out.append(x)
                items["end"] = out

            last_add = [None]
            for kind, arg in phases():
                if kind == "start":
                    start()
                elif kind == "rms":
                    rms(arg)
                elif kind == "A":
                    attn_a(arg)
                elif kind == "B":
                    attn_b(arg)
                elif kind == "C":
                    attn_c(arg)
                elif kind == "ffn":
                    ffn("f_w_gu", "f_w_out", arg, ("ffn", arg))
                    last_add[0] = (("ffn", arg), "down")
                elif kind == "rows2":
                    rows2()
                elif kind == "final":
                    rms("final")
                elif kind in ("ln", "ln_last"):
                    if arg[0] == "ln_in_g_2":
                        pe.wait_ge(y_ready, KT)
                    else:
                        for x in items[last_add[0]]:
                            pe.wait_ge(bank_free[x.bank], x.free)
                    ln(arg, kind == "ln_last")
                elif kind == "mix":
                    mix(arg)
                    last_add[0] = (("m", arg), "wo")
                elif kind == "ffn2":
                    ffn("w_up_2", "w_down_2", arg, ("ffn2", arg))
                    last_add[0] = (("ffn2", arg), "down")
                elif kind == "end":
                    end()

        @block.sync
        def _(sp):
            sp.dma_start(xrows, t["x"][0].rearrange("(t p) n -> p t n", p=P)).then_inc(x_landed, 16)

            def load(u, loads):
                for dst, src in loads:
                    sp.dma_start(dst(raw[u.slot]), src).then_inc(landed[u.slot], 16)

            n = 0
            while n < len(units):
                u = units[n]
                if not u.span:
                    if u.index >= SLOTS:
                        sp.wait_ge(lo_ready, u.index + 1 - SLOTS)
                    load(u, u.loads)
                    n += 1
                    continue
                body = units[n:n + u.span]
                first, last = u.rounds
                with sp.Fori(first, last) as i:
                    for b in body:
                        sp.wait_ge(lo_ready, i * b.span + (b.index + 1 - SLOTS))
                        load(b, b.loads(i))
                n += len(body)
            for x in items["end"]:
                sp.wait_ge(bank_free[x.bank], x.free)
            sp.dma_start(t["out"][0].rearrange("(t p) n -> p t n", p=P), xrows).then_inc(out_stored, 16)
            sp.wait_ge(out_stored, 16)

        @block.gpsimd
        def _(pool):
            gp = nc.gpsimd
            gp.memset(ones[:], 1.0).then_inc(ident_ready, 1)
            gp.memset(ident[:], 0.0).then_inc(ident_ready, 1)
            pool.wait_ge(ident_ready, 2)
            gp.affine_select(out=ident[:], in_=ident[:], compare_op=ALU.not_equal, fill=1.0, base=0,
                             pattern=[[-1, P]], channel_multiplier=1).then_inc(ident_ready, 1)
            for n in range(3):
                gp.memset(idle[:, n:n + 1], 0.0).then_inc(hidden_ready, 1)
            seen_m, seen_b, tiles_before, made_before = 0, 0, 0, 0

            def split_hidden(tag, second):
                head, body, tail = items[tag, "up"]

                def step(j, at, n, i=None):
                    k = tiles_before + n + 1
                    x = (body[j] if i is not None else tail[0] if n == FT - 1 else head[j])[1]
                    if second:
                        made = made_before + n + 1
                        pool.wait_ge(product_ready, made if i is None else i * 3 + made)
                    else:
                        pool.wait_ge(bank_free[x.bank], x.free if i is None else i + x.free)
                    gp.tensor_copy(hid_hi[:, at], hT[:, j, :]).then_inc(hid_step, 1)
                    pool.wait_ge(hid_step, k if i is None else i * 3 + k)
                    gp.tensor_tensor(hid_lo[:, at], hT[:, j, :], hid_hi[:, at].bitcast(F32),
                                     ALU.subtract).then_inc(hidden_ready, 1)

                for j in range(3):
                    step(j, slice(j * T, (j + 1) * T), j)
                with pool.Fori(1, 7) as i:
                    for j in range(3):
                        step(j, bass.ds(i * (3 * T) + j * T, T), j, i)
                step(0, slice(21 * T, 22 * T), 21)

            for kind, arg in phases():
                if kind == "B":
                    seen_b += 1
                    pool.wait_ge(kr_ready, seen_b)
                    gp.tensor_copy(kT[64:96, 0:B_HEADS, :],
                                   kr[64:96, :].unsqueeze(1).to_broadcast([32, B_HEADS, T])).then_inc(kr_spread, 1)
                if kind == "second":
                    pool.wait_ge(area_free, 1)
                    gp.memset(poolw[:], 0.0).then_inc(poolw_zeroed, 1)
                    pool.dma_start(inv_cnt, t["c_inv_cnt"]).then_inc(consts2_landed, 16)
                    for dst, src in row_loads(1):
                        pool.dma_start(dst, src).then_inc(rows2_landed, 16)
                    pool.wait_ge(poolw_zeroed, 1)
                    for l in range(DEPTH_2):
                        for g in range(4):
                            a = HD * (g % 2)
                            pool.dma_start(poolw[a:a + HD, l, g // 2, a:a + HD], t["pool_w_2"][l, g]).then_inc(poolw_landed, 16)
                if kind in ("ffn", "ffn2"):
                    split_hidden((kind, arg), kind == "ffn2")
                    tiles_before += FT
                    made_before += FT * (kind == "ffn2")
                if kind == "mix":
                    for tt in range(NT):
                        pool.wait_ge(score_step, IDX_HEADS * NT * seen_m + NT * (IDX_HEADS - 1) + tt + 1)
                        gp.affine_select(out=score[:, tt, :], in_=score[:, tt, :], compare_op=ALU.is_ge,
                                         fill=FILL, base=tt * P, pattern=[[-1, T]],
                                         channel_multiplier=1).then_inc(score_masked, 1)
                    for tt in range(NT):
                        pool.wait_ge(picked, NT * seen_m + tt + 1)
                        gp.affine_select(out=work[:, tt, :], in_=work[:, tt, :], compare_op=ALU.is_ge,
                                         fill=NEG, base=tt * P, pattern=[[-1, T]],
                                         channel_multiplier=1).then_inc(keep_ready, 1)
                    seen_m += 1

        @block.scalar
        def _(act):
            tally = {}
            fn = nc.scalar.activation

            def count(s, n=1):
                tally[s.name] = tally.get(s.name, 0) + n
                return tally[s.name]

            def done(x, i=None):
                act.wait_ge(pe_done, x.done if i is None else i * x.step_done + x.done)

            def freed(x):
                act.wait_ge(bank_free[x.bank], x.free)

            def free(ins, x):
                ins.then_inc(bank_free[x.bank], 1)

            def round_unit(slot, nth, i=None, step=0):
                act.wait_ge(landed[slot], 32 * nth if i is None else i * (32 * step) + 32 * nth)
                nc.scalar.copy(w_hi[slot][:], raw[slot][:]).then_inc(hi_ready, 1)

            def refill(u, i=None):
                if i is None and u.index + SLOTS >= total[0]:
                    return
                done(u, i)
                round_unit(u.slot, u.index // SLOTS + 2, i, u.span // SLOTS)

            def refills(tag):
                head, loop, tail = items[tag, "units"]
                for u in head:
                    refill(u)
                if loop and loop[-1].at(2).index + SLOTS < total[0]:
                    with act.Fori(1, 3) as i:
                        for u in loop:
                            refill(u, i)
                elif loop:
                    for u in [u.at(i) for i in (1, 2) for u in loop]:
                        refill(u)
                for u in tail:
                    refill(u)

            for dst, src in row_loads(0):
                act.dma_start(dst, src).then_inc(rows_landed, 16)
            for s in range(SLOTS):
                round_unit(s, 1)
            for dst, name in ((tab, "c_tab"), (rotm, "c_rotm"), (invf, "c_invf")):
                act.dma_start(dst[:], t[name]).then_inc(consts_landed, 16)
            for n, name in enumerate(("a_lambda_q1", "a_lambda_k1", "a_lambda_q2", "a_lambda_k2")):
                for l in range(2):
                    act.dma_start(lamv[:, 2 * n + l, :], t[name][l:l + 1, :].to_broadcast([P, HD])).then_inc(lam_landed, 16)
            for (a, b, col) in ((0, P, Z_V), (P, P + 8, Z_WI)):
                act.dma_start(brow[0:1, :, a:b], t["b_in_2"][:, col:col + b - a].unsqueeze(0)).then_inc(consts_landed, 16)

            def second():
                act.wait_ge(angles_ready, 2)
                fn(tabd[:, 1, :], red, ACT.Sin)
                fn(tabd[:, 0, :], scr, ACT.Sin, scale=-1.0, bias=eps[:, 2:3]).then_inc(sines_ready, 1)

            def norm_squares(source):
                for j, x in enumerate(source):
                    freed(x)
                    fn(sq[:, 2 * j:2 * j + 2, :], xT[:, 2 * j:2 * j + 2, :], ACT.Square).then_inc(squares_ready, 1)

            def deviation(s, spans, e=0):
                done(s)
                for a, b, n in spans:
                    ins = fn(std[:, a:b], banks[s.bank][:, a:b], ACT.Sqrt, scale=1.0 / n, bias=eps[:, e:e + 1])
                free(ins, s)

            def round_parts(n, width, scaled=None):
                for k in range(n):
                    if scaled:
                        freed(scaled[k])
                    else:
                        act.wait_ge(to_split, count(to_split))
                    s = slice(width * k, width * (k + 1))
                    nc.scalar.copy(h_hi[:, s, :], hT[:, s, :]).then_inc(hi_part, 1)

            def pair_of(x):
                return banks[x.bank][:].rearrange("p (m n) -> p m n", m=2)

            def attn_a(i):
                us, xs, rr, vs = items[i, "units"], items[i, "qk"], items[i, "rot"], items[i, "v"]
                for n, u in enumerate(us):
                    if n < 8:
                        x = xs[n]
                        done(x)
                        if n >= 3:
                            freed(rr[n - 3])
                        free(fn(pre[x.pre][:], banks[x.bank][:], ACT.Copy, scale=HD ** -0.5 if n < 4 else 1.0), x)
                    else:
                        v = vs[n - 8]
                        done(v)
                        free(nc.scalar.copy(vA[:, :, (n - 8) * 256:(n - 7) * 256], pair_of(v)), v)
                    refill(u)
                S, TT, O = items[i, "S"], items[i, "T"], items[i, "O"]
                for hd in range(A_HEADS + 3):
                    if hd < A_HEADS:
                        if hd >= 3:
                            done(TT[hd - 3][0])
                        for sub in range(2):
                            n = 2 * hd + sub
                            act.wait_ge(negmax_ready, count(negmax_ready))
                            for tt in range(NT):
                                ins = fn(expoA[hd % 3][:, 512 * sub + tt * T:512 * sub + (tt + 1) * T],
                                         banks[S[n].bank][:, tt * T:(tt + 1) * T], ACT.Exp,
                                         bias=negmax[n % 4][:, tt:tt + 1], accum_out=esum[n % 4][:, tt:tt + 1])
                            free(ins, S[n])
                    if 2 <= hd < A_HEADS + 2:
                        probs_t(hd - 2, TT)
                    if hd >= 3 and (hd - 3) % 2 == 1:
                        g = (hd - 3) // 2
                        done(O[g])
                        fn(sq[:, 2 * g:2 * g + 2, :], pair_of(O[g]), ACT.Square).then_inc(squares_ready, 1)
                        free(nc.scalar.copy(oT[:, 2 * g:2 * g + 2, :], pair_of(O[g])), O[g])
                deviation(items[i, "subln"][0], ((0, 16, P),))
                round_parts(4, 2, items[i, "subln"][1])
                refills((i, "wo"))

            def probs_t(hd, TT):
                if hd >= 2:
                    act.wait_ge(pe_done, TT[hd - 2][-1].used)
                for g, it in enumerate(TT[hd]):
                    done(it)
                    free(nc.scalar.copy(expoT[hd % 2][:, 512 * g:512 * (g + 1)], banks[it.bank][:]), it)

            def attn_64(tag, heads, masked, dst=None, natural=lambda x: x):
                S, TT, O = items[tag, "S"], items[tag, "T"], items[tag, "O"]
                w = T * len(TT[0])
                for hd in range(heads + 3):
                    if hd < heads:
                        act.wait_ge(negmax_ready, count(negmax_ready))
                        if not masked and hd >= 3:
                            for it in TT[hd - 3]:
                                done(it)
                        for tt in range(NT):
                            e = expo[hd % 3][:, w * tt:w * (tt + 1)]
                            ins = fn(e, e if masked else banks[S[hd][0].bank][:, tt * T:(tt + 1) * T], ACT.Exp,
                                     bias=negmax[hd % 4][:, tt:tt + 1], accum_out=esum[hd % 4][:, tt:tt + 1])
                        if masked:
                            ins.then_inc(exp_ready, 1)
                        else:
                            free(ins, S[hd][0])
                    if 2 <= hd < heads + 2:
                        probs_t(hd - 2, TT)
                    if hd >= 3 and (hd - 3) % 4 == 3:
                        g = (hd - 3) // 4
                        done(O[g])
                        out = natural((dst or h_hi)[:, 2 * g:2 * g + 2, :])
                        nc.scalar.copy(out, like(pair_of(O[g]), out)).then_inc(hi_part, 1)

            def like(b, out):
                return b if len(out.shape) == 3 else b.rearrange("p m (c u) -> p m c u", c=4)

            def attn_b(i):
                us, raw_items = items[i, "units"], items[i, "raw"]
                for n in range(2):
                    done(raw_items[n])
                    fn(sq[:, 2 * n:2 * n + 2, :], pair_of(raw_items[n]), ACT.Square).then_inc(squares_ready, 1)
                    free(nc.scalar.copy(latT[:, 2 * n:2 * n + 2, :], pair_of(raw_items[n])), raw_items[n])
                    refill(us[n])
                done(raw_items[2])
                fn(sq[:, 4, :], banks[2][:, 0:T], ACT.Square).then_inc(squares_ready, 1)
                nc.scalar.copy(latT[:, 4, :], banks[2][:, 0:T])
                free(nc.scalar.copy(pre[2][64:96, 0:T], banks[2][64:96, T:2 * T]), raw_items[2])
                refill(us[2])
                deviation(items[i, "stat"][0], ((0, 2, B_QR), (2, 4, B_KVR)))
                round_parts(5, 1)
                for n, x in enumerate(items[i, "qk"]):
                    done(x)
                    if n == 2:
                        freed(items[i, "krot"])
                    if n >= 3:
                        freed(items[i, "rot"][n - 3])
                    free(fn(pre[x.pre][0:96, :], banks[x.bank][0:96, :], ACT.Copy,
                            scale=float(np.float32((B_NOPE + B_ROPE) ** -0.5))), x)
                    if n % 2:
                        refill(us[3 + n // 2])
                for half in range(2):
                    for n in range(4 * half, 4 * half + 4):
                        x = items[i, "k"][n]
                        done(x)
                        free(nc.scalar.copy(kT[0:HD, 2 * n:2 * n + 2, :],
                                            banks[x.bank][0:HD, :].rearrange("p (m n) -> p m n", m=2)), x)
                    for tt in range(NT):
                        v = items[i, "v"][2 * half + tt]
                        done(v)
                        free(nc.scalar.copy(vA[:, tt, half * 512:(half + 1) * 512], banks[v.bank][:]), v)
                    refill(us[7 + half])
                attn_64(i, B_HEADS, False)
                refills((i, "wo"))

            def attn_c(i):
                us, xs, rr, vs = items[i, "units"], items[i, "qk"], items[i, "rot"], items[i, "v"]
                with act.Fori(0, C_GROUPS) as g:
                    for n, u in enumerate(us):
                        if n < 8:
                            x, r = xs[n], rr[(n - 2) % 8]
                            done(x, g)
                            act.wait_ge(bank_free[r.bank], g * r.step_free + (r.free if n >= 2 else r.free - r.step_free))
                            free(fn(pre[x.pre][:], banks[x.bank][:], ACT.Copy, scale=HD ** -0.5 if n < 4 else 1.0), x)
                        else:
                            v = vs[n - 8]
                            done(v, g)
                            free(nc.scalar.copy(vC[:, :, bass.ds(g * 1024 + (n - 8) * 256, 256)], pair_of(v)), v)
                        refill(u, g)
                act.wait_ge(rot_ready, ROTATED_BEFORE_C + 8 * C_GROUPS)
                act.dma_start(cmask, t["c_cmask"]).then_inc(cmask_landed, 16)
                act.dma_start(pos_i, t["positions_2"].to_broadcast([P, T])).then_inc(pos_landed, 16)
                attn_64(i, C_HEADS, True, natural=lambda x: x.rearrange("p m (u c) -> p m c u", c=4))
                refills((i, "wo"))

            def ffn(tag, before):
                head, body, tail = items[tag, "up"]

                def step(j, n, u, x, i=None):
                    done(x, i)
                    fn(pre[j][:, 0:T], banks[x.bank][:, 0:T], ACT.Silu).then_inc(gate_ready, 1)
                    refill(u, i)

                for j, (u, x) in enumerate(head):
                    step(j, j, u, x)
                with act.Fori(1, 7) as i:
                    for j, (u, x) in enumerate(body):
                        step(j, j, u, x, i)
                for u, x in tail:
                    step(0, FT - 1, u, x)
                refills((tag, "down"))

            def ln(tag, last):
                s, m, v, b = items[tag]
                for j in range(4):
                    act.wait_ge(centred, count(centred))
                    fn(sq[:, 2 * j:2 * j + 2, :], xT[:, 2 * j:2 * j + 2, :], ACT.Square).then_inc(squares_ready, 1)
                deviation(v, ((0, 2, D),), 1)
                if not last:
                    at = ROW[tag[1]] + tag[2]
                    for k in range(KT):
                        act.wait_ge(ln_ready, count(ln_ready))
                        fn(h_hi[:, k, :], hT[:, k, :], ACT.Identity, bias=pcol[:, at + k:at + k + 1]).then_inc(hi_part, 1)

            def mix(l):
                it = items["m", l]
                us = iter(it["units"])
                b0 = ROW["b_in", l]

                def offset(dst, x, row, tiles=2, func=ACT.Identity):
                    done(x)
                    for m in range(tiles):
                        ins = fn(dst(m), banks[x.bank][:, m * T:(m + 1) * T], func, bias=pcol[:, b0 + row + m:b0 + row + m + 1])
                    free(ins, x)
                    refill(next(us))

                offset(lambda m: pool_u[:, m, PADW:], it["pool"], B_POOL)
                offset(lambda m: conv_a[:, m, :], it["conv_a"], B_CONV)
                offset(lambda m: conv_y[:, m, :], it["conv_g"], B_CONV + 2, func=ACT.Sigmoid)
                for n, (x, row) in enumerate(zip(it["qk"], (B_Q, B_Q + 2, B_K, B_QI, B_QI + 2, B_KI))):
                    if n >= 3:
                        freed(it["rot"][n - 3])
                    offset(lambda m: pre[x.pre][:, m * T:(m + 1) * T], x, row, tiles=1 if n == 5 else 2)
                v = it["v"]
                done(v)
                b = banks[v.bank][:, 0:272].rearrange("p (t n) -> p t n", t=NT)
                nc.scalar.copy(vD[:], b[:, :, 0:128])
                free(nc.scalar.mul(wi[:], b[:, :, 128:136], float(np.float32(IDX_HEADS ** -0.5))), v)
                refill(next(us))
                for n, s in enumerate(it["idx"]):
                    done(s)
                    if n >= 2:
                        act.wait_ge(score_step, NT * IDX_HEADS * l + 2 * (n - 1))
                    free(fn(relu[n % 2], banks[s.bank][:], ACT.Relu, scale=HD ** -0.5), s)
                with act.Fori(0, 4) as i:
                    for n, (u, x) in enumerate(it["gates"]):
                        done(x, i)
                        for m in range(2):
                            ins = fn(gates[:, bass.ds(i * 6 + (2 * n + m), 1), :], banks[x.bank][:, m * T:(m + 1) * T].unsqueeze(1),
                                     ACT.Sigmoid, bias=pcol[:, bass.ds(i * 6 + (b0 + B_GATE + 2 * n + m), 1)])
                        free(ins, x)
                        refill(u, i)
                s, m_, v, b = it["cln"]
                act.wait_ge(centred, count(centred))
                fn(sq[:, 0:2, :], conv_y[:], ACT.Square).then_inc(squares_ready, 1)
                deviation(v, ((0, 2, 256),), 1)
                at = ROW["conv_ln_b_2"] + 2 * l
                for m in range(2):
                    act.wait_ge(ln_ready, count(ln_ready))
                    ins = fn(conv_y[:, m, :], conv_y[:, m, :], ACT.Silu, bias=pcol[:, at + m:at + m + 1])
                ins.then_inc(act_step, 1)
                act.wait_ge(act_step, l + 1)
                nc.scalar.copy(conv_hi[:], conv_y[:]).then_inc(hi_part, 1)
                tag = ("m", l)
                attn_64(tag, N_HEADS, True, dst=attn_hi)
                for branch in ("pool", "conv", "attn"):
                    refills((tag, branch))
                round_parts(4, 2)
                refills((tag, "wo"))

            def ffn2(tag, l, before):
                head, body, tail = items[tag, "up"]
                w, b = ROW["ffn_dw_w_2"] + l * FCW * 44 + 2 * 44, ROW["ffn_dw_b_2"] + l * 44

                def step(n, j, u, x, i=None):
                    def col(at):
                        return pcol[:, at:at + 1] if i is None else pcol[:, bass.ds(i * 3 + at, 1)]

                    k = before + n + 1
                    act.wait_ge(hidden_ready, k if i is None else i * 3 + k)
                    done(x, i)
                    for m, tile in ((0, 0), (1, 22)):
                        ins = fn(pre[j][:, m * T:(m + 1) * T], banks[x.bank][:, m * T:(m + 1) * T], ACT.Identity,
                                 scale=col(w + tile + n), bias=col(b + tile + n))
                    ins.then_inc(taps_started, 1)
                    refill(u, i)
                    act.wait_ge(bank_free[x.bank], x.free if i is None else i + x.free)
                    fn(pre[j][:, 0:T], pre[j][:, 0:T], ACT.Silu).then_inc(gate_ready, 1)

                for j, (u, x) in enumerate(head):
                    step(j, j, u, x)
                with act.Fori(1, 7) as i:
                    for j, (u, x) in enumerate(body):
                        step(j, j, u, x, i)
                for u, x in tail:
                    step(FT - 1, 0, u, x)
                refills((tag, "down"))

            source = [items["start"][0]]
            n_ffn = 0
            for kind, arg in phases():
                if kind == "lambda":
                    act.wait_ge(lam_sums, 1)
                    fn(lame[:], lams[:], ACT.Exp).then_inc(lam_exps, 1)
                elif kind == "second":
                    second()
                elif kind == "rms":
                    norm_squares(source[0])
                    deviation(items[arg][0], ((0, 2, D),))
                    round_parts(KT, 1)
                elif kind in "ABC":
                    (attn_a if kind == "A" else attn_b if kind == "B" else attn_c)(arg)
                    source[0] = items[arg, "wo"]
                elif kind == "ffn":
                    ffn(("ffn", arg), FT * n_ffn)
                    n_ffn += 1
                    source[0] = items[("ffn", arg), "down"]
                elif kind == "final":
                    norm_squares(source[0])
                    deviation(items["final"][0], ((0, 2, D),))
                elif kind in ("ln", "ln_last"):
                    ln(arg, kind == "ln_last")
                elif kind == "mix":
                    mix(arg)
                elif kind == "ffn2":
                    ffn2(("ffn2", arg), arg, FT * n_ffn)
                    n_ffn += 1

        @block.vector
        def _(dve):
            v_ = nc.vector
            tally = {}
            steps = [0]

            def count(s, n=1):
                tally[s.name] = tally.get(s.name, 0) + n
                return tally[s.name]

            def done(x, i=None):
                dve.wait_ge(pe_done, x.done if i is None else i * x.step_done + x.done)

            def freed(x, i=None):
                dve.wait_ge(bank_free[x.bank], x.free if i is None else i * x.step_free + x.free)

            def free(ins, x):
                ins.then_inc(bank_free[x.bank], 1)

            def link(ins, behind=0):
                steps[0] += 1
                ins.then_inc(dve_step, 1)
                if steps[0] > behind:
                    dve.wait_ge(dve_step, steps[0] - behind)

            def rest(slot, nth, i=None, step=0):
                dve.wait_ge(hi_ready, nth if i is None else i * step + nth)
                v_.tensor_tensor(w_lo[slot][:], raw[slot][:], w_hi[slot][:].bitcast(F32), ALU.subtract).then_inc(lo_ready, 1)

            def refill(u, i=None):
                if i is None and u.index + SLOTS >= total[0]:
                    return
                rest(u.slot, u.index + SLOTS + 1, i, u.span)

            def refills(tag):
                head, loop, tail = items[tag, "units"]
                for u in head:
                    refill(u)
                if loop and loop[-1].at(2).index + SLOTS < total[0]:
                    with dve.Fori(1, 3) as i:
                        for u in loop:
                            refill(u, i)
                elif loop:
                    for u in [u.at(i) for i in (1, 2) for u in loop]:
                        refill(u)
                for u in tail:
                    refill(u)

            def start():
                v_.memset(eps[:, 0:1], EPS)
                v_.memset(eps[:, 1:2], LN_EPS)
                v_.memset(eps[:, 3:4], 0.0)
                link(v_.memset(eps[:, 2:3], math.pi / 2))
                xs, r = items["start"]
                rest(0, 1)
                for j, x in enumerate(xs):
                    done(x)
                    free(v_.tensor_copy(xT[:, 2 * j:2 * j + 2, :], banks[x.bank][:].rearrange("p (m n) -> p m n", m=2)), x)
                done(r)
                free(v_.tensor_copy(pcol[:, 0:P], banks[r.bank][:, 0:P]), r)
                freed(r)
                for b in (5, 6):
                    x = items["idle", b]
                    done(x)
                    free(v_.tensor_copy(rot[b - 5][:, 0:P], banks[b][:, 0:P]), x)
                rest(1, 2)
                rest(2, 3)

            def lambdas():
                dve.wait_ge(lam_landed, 16 * 8)
                for n in range(2):
                    ins = v_.tensor_tensor(lamp[:, 2 * n:2 * n + 2, :], lamv[:, 4 * n:4 * n + 2, :],
                                           lamv[:, 4 * n + 2:4 * n + 4, :], ALU.mult)
                link(ins)
                v_.tensor_reduce(lams[:], lamp[:], AX.X, ALU.add).then_inc(lam_sums, 1)
                dve.wait_ge(lam_exps, 1)
                link(v_.tensor_tensor(neglam[:], lame[:, 2:4], lame[:, 0:2], ALU.subtract))
                for l in range(2):
                    v_.tensor_scalar(neglam[:, l:l + 1], neglam[:, l:l + 1], -lambda_init(3 * l), None, ALU.add)
                    ins = v_.tensor_scalar(subg[:, l:l + 1], pcol[:, ROW["a_subln"] + l:ROW["a_subln"] + l + 1],
                                           1.0 - lambda_init(3 * l), None, ALU.mult)
                link(ins)
                dve.wait_ge(consts_landed, 16 * 5)

            def second():
                dve.wait_ge(pos_landed, 16)
                v_.tensor_copy(ang, pos_i).then_inc(area_free, 1)
                dve.wait_ge(area_free, 1)
                link(v_.tensor_scalar(ang, ang, invf[:, 0:1], None, ALU.mult))
                link(v_.tensor_scalar(turns, ang, 1.0 / (2 * math.pi), MAGIC, ALU.mult, ALU.add))
                link(v_.tensor_scalar(turns, turns, -MAGIC, None, ALU.add))
                for part in TWO_PI:
                    link(v_.scalar_tensor_tensor(ang, turns, -part, ang, ALU.mult, ALU.add))
                link(v_.tensor_scalar(red, ang, PI_IN, -PI_IN, ALU.min, ALU.max))
                v_.tensor_scalar(turns, red, -1.0, None, ALU.mult).then_inc(angles_ready, 1)
                dve.wait_ge(angles_ready, 1)
                v_.tensor_tensor(scr, turns, red, ALU.max).then_inc(angles_ready, 1)

            def rows2():
                dve.wait_ge(sines_ready, 1)
                dve.wait_ge(consts2_landed, 16)
                for n, x in enumerate(items["rows2"]):
                    done(x)
                    w = min(512, N_ROWS - P - 512 * n)
                    free(v_.tensor_copy(pcol[:, P + 512 * n:P + 512 * n + w], banks[x.bank][:, 0:w]), x)
                for x in items["rows2"]:
                    freed(x)

            def split_rest(n, width, k):
                dve.wait_ge(hi_part, count(hi_part))
                s = slice(width * k, width * (k + 1))
                v_.tensor_tensor(h_lo[:, s, :], hT[:, s, :], h_hi[:, s, :].bitcast(F32), ALU.subtract).then_inc(h_ready, 1)

            def by_class(x):
                return x.rearrange("p (u c) -> p c u", c=4)

            def rms(tag, at, kind, final=False):
                s, b = items[tag]
                freed(s)
                v_.reciprocal(rs[:, 0:2], std[:, 0:2]).then_inc(rs_ready, 1)
                done(b)
                for k in range(KT + 2):
                    if k < KT:
                        dst, src, r = (xT if final else hT)[:, k, :], xT[:, k, :], banks[b.bank][:, 0:T]
                        if kind == "C":
                            dst, src, r = dst.rearrange("p (c u) -> p c u", c=4), by_class(src), by_class(r)
                        v_.scalar_tensor_tensor(dst, src, pcol[:, at + k:at + k + 1], r, ALU.mult,
                                                ALU.mult).then_inc(y_ready if final else to_split, 1)
                    if k >= 2 and not final:
                        split_rest(KT, 1, k - 2)

            def rotate(n, x, r, dst, cos, sin, i=None, lo=0, hi=P, tiles=2, ready=rot_ready):
                w = tiles * T
                done(r, i)
                shape = [hi - lo, tiles, T]

                def wide(tb):
                    return tb[lo:hi, :].unsqueeze(1).to_broadcast(shape)

                p3 = pre[x.pre][lo:hi, 0:w].rearrange("p (m n) -> p m n", m=tiles)
                r3 = rot[n % 2][lo:hi, 0:w].rearrange("p (m n) -> p m n", m=tiles)
                v_.tensor_tensor(dst, p3, wide(cos), ALU.mult)
                free(v_.tensor_tensor(r3, banks[r.bank][lo:hi, 0:w].rearrange("p (m n) -> p m n", m=tiles), wide(sin),
                                      ALU.mult), r)
                freed(r, i)
                v_.tensor_tensor(dst, dst, r3, ALU.add).then_inc(ready, 1)

            def residual(its, scale=None):
                for j, x in enumerate(its):
                    done(x)
                    b = banks[x.bank][:].rearrange("p (m n) -> p m n", m=2)
                    xs = xT[:, 2 * j:2 * j + 2, :]
                    if scale is None:
                        free(v_.tensor_tensor(xs, xs, b, ALU.add), x)
                    else:
                        free(v_.scalar_tensor_tensor(xs, xs, scale, b, ALU.mult, ALU.add), x)

            def attn_a(i):
                l = i // 3
                us, xs, rr = items[i, "units"], items[i, "qk"], items[i, "rot"]
                for n, u in enumerate(us):
                    refill(u)
                    if 1 <= n <= 8:
                        rotate(n, xs[n - 1], rr[n - 1], qT[:, 2 * n - 2:2 * n, :], tab[:, 0, :], tab[:, 1, :])
                S = items[i, "S"]
                for hd in range(A_HEADS + 1):
                    if hd < A_HEADS:
                        for sub in range(2):
                            n = 2 * hd + sub
                            done(S[n])
                            v_.tensor_reduce(negmax[n % 4][:], banks[S[n].bank][:].rearrange("p (m n) -> p m n", m=2), AX.X,
                                             ALU.max, negate=True).then_inc(negmax_ready, 1)
                    if hd >= 1:
                        n = 2 * (hd - 1)
                        e = expoA[(hd - 1) % 3]
                        rec = [erec[(n + sub) % 4] for sub in range(2)]
                        for sub in range(2):
                            freed(S[n + sub])
                            link(v_.reciprocal(rec[sub][:], esum[(n + sub) % 4][:]))
                        link(v_.tensor_scalar(rec[1][:], rec[1][:], neglam[:, l:l + 1], None, ALU.mult))
                        for tt in range(NT):
                            e0 = e[:, tt * T:(tt + 1) * T]
                            ins = v_.tensor_scalar(e0, e0, rec[0][:, tt:tt + 1], None, ALU.mult)
                        link(ins)
                        for tt in range(NT):
                            e0, e1 = e[:, tt * T:(tt + 1) * T], e[:, 512 + tt * T:512 + (tt + 1) * T]
                            ins = v_.scalar_tensor_tensor(e0, e1, rec[1][:, tt:tt + 1], e0, ALU.mult, ALU.add)
                        ins.then_inc(probs_ready, 1)
                s, sp_items = items[i, "subln"]
                freed(s)
                v_.reciprocal(rs[:, 0:16], std[:, 0:16]).then_inc(rs_ready, 1)
                for g in range(5):
                    if g < 4:
                        b = sp_items[g]
                        done(b)
                        m = slice(2 * g, 2 * g + 2)
                        free(v_.scalar_tensor_tensor(hT[:, m, :], oT[:, m, :], subg[:, l:l + 1],
                                                     banks[b.bank][:].rearrange("p (m n) -> p m n", m=2), ALU.mult, ALU.mult), b)
                    if g:
                        split_rest(4, 2, g - 1)
                refills((i, "wo"))
                residual(items[i, "wo"])

            def attn_64(tag, heads, mask=None, dst=None, scale=None, natural=lambda x: x):
                S, TT, O = items[tag, "S"], items[tag, "T"], items[tag, "O"]
                w = T * len(TT[0])
                for hd in range(heads + 4):
                    if hd < heads:
                        if mask is None:
                            done(S[hd][0])
                            v_.tensor_reduce(negmax[hd % 4][:], banks[S[hd][0].bank][:].rearrange("p (m n) -> p m n", m=2),
                                             AX.X, ALU.max, negate=True).then_inc(negmax_ready, 1)
                        else:
                            e = expo[hd % 3]
                            if hd >= 3:
                                for it in TT[hd - 3]:
                                    done(it)
                            for n, s in enumerate(S[hd]):
                                done(s)
                                c = slice(512 * n, 512 * (n + 1))
                                if scale is None:
                                    free(v_.tensor_tensor(e[:, c], banks[s.bank][:], mask[:, c], ALU.add), s)
                                else:
                                    free(v_.scalar_tensor_tensor(e[:, c], banks[s.bank][:], scale, mask[:, c], ALU.mult,
                                                                 ALU.add), s)
                            for s in S[hd]:
                                freed(s)
                            v_.tensor_reduce(negmax[hd % 4][:], e[:, 0:NT * w].rearrange("p (t n) -> p t n", t=NT), AX.X,
                                             ALU.max, negate=True).then_inc(negmax_ready, 1)
                    if 1 <= hd <= heads:
                        g = hd - 1
                        if mask is None:
                            freed(S[g][0])
                        else:
                            dve.wait_ge(exp_ready, count(exp_ready))
                        link(v_.reciprocal(erec[g % 4][:], esum[g % 4][:]))
                        for tt in range(NT):
                            e = expo[g % 3][:, w * tt:w * (tt + 1)]
                            ins = v_.tensor_scalar(e, e, erec[g % 4][:, tt:tt + 1], None, ALU.mult)
                        ins.then_inc(probs_ready, 1)
                    if hd >= 4 and hd % 4 == 3:
                        g = (hd - 4) // 4
                        dve.wait_ge(hi_part, count(hi_part))
                        a, b = dst or (h_hi, h_lo)
                        hi, lo = (natural(x[:, 2 * g:2 * g + 2, :]) for x in (a, b))
                        src = banks[O[g].bank][:].rearrange("p (m n) -> p m n", m=2)
                        if len(hi.shape) == 4:
                            src = src.rearrange("p m (c u) -> p m c u", c=4)
                        free(v_.tensor_tensor(lo, src, hi.bitcast(F32), ALU.subtract), O[g])

            def attn_b(i):
                us = items[i, "units"]
                for u in us[0:3]:
                    refill(u)
                s, b = items[i, "stat"]
                freed(s)
                v_.reciprocal(rs[:, 0:4], std[:, 0:4]).then_inc(rs_ready, 1)
                done(b)
                for k in range(7):
                    if k < 5:
                        at = ROW["b_q_norm"] + k
                        a = 0 if k < 3 else T
                        v_.scalar_tensor_tensor(hT[:, k, :], latT[:, k, :], pcol[:, at:at + 1], banks[b.bank][:, a:a + T],
                                                ALU.mult, ALU.mult).then_inc(to_split, 1)
                    if k >= 2:
                        split_rest(5, 1, k - 2)
                rotate(0, items[i, "raw"][2], items[i, "krot"], kr[64:96, :].unsqueeze(1), tab[:, 2, :], tab[:, 3, :],
                       lo=64, hi=96, tiles=1, ready=kr_ready)
                for n, (x, r) in enumerate(zip(items[i, "qk"], items[i, "rot"])):
                    if n % 2 == 0:
                        if n:
                            refill(us[2 + n // 2])
                    rotate(n + 1, x, r, qT[0:96, 2 * n:2 * n + 2, :], tab[:, 2, :], tab[:, 3, :], hi=96)
                for u in us[6:9]:
                    refill(u)
                attn_64(i, B_HEADS)
                refills((i, "wo"))
                residual(items[i, "wo"])

            def attn_c(i):
                us, xs, rr = items[i, "units"], items[i, "qk"], items[i, "rot"]
                with dve.Fori(0, C_GROUPS) as g:
                    for n, u in enumerate(us):
                        refill(u, g)
                        if 1 <= n <= 8:
                            m = n - 1
                            dst = (qT if m < 4 else kT)[:, bass.ds(g * 8 + 2 * (m % 4), 2), :]
                            rotate(m, xs[m], rr[m], dst, tab[:, 4, :], tab[:, 5, :], i=g)
                dve.wait_ge(cmask_landed, 16)
                attn_64(i, C_HEADS, mask=cmask, natural=lambda x: x.rearrange("p m (u c) -> p m c u", c=4))
                refills((i, "wo"))
                residual(items[i, "wo"])

            def ffn(tag, before):
                head, body, tail = items[tag, "up"]
                g0 = count(gate_ready, FT) - FT

                def step(j, n, u, x, i=None):
                    refill(u, i)
                    k = g0 + n + 1
                    dve.wait_ge(gate_ready, k if i is None else i * 3 + k)
                    k = before + n + 1
                    dve.wait_ge(hidden_ready, k if i is None else i * 3 + k)
                    free(v_.tensor_tensor(hT[:, j, :], banks[x.bank][:, T:2 * T], pre[j][:, 0:T], ALU.mult), x)

                for j, (u, x) in enumerate(head):
                    step(j, j, u, x)
                with dve.Fori(1, 7) as i:
                    for j, (u, x) in enumerate(body):
                        step(j, j, u, x, i)
                for u, x in tail:
                    step(0, FT - 1, u, x)
                refills((tag, "down"))
                residual(items[tag, "down"])

            def ln(tag, last):
                s, m, v, b = items[tag]
                done(s)
                free(v_.tensor_scalar(rs[:, 0:2], banks[s.bank][:, 0:2], -1.0 / D, None, ALU.mult), s)
                done(m)
                for j in range(4):
                    xs = xT[:, 2 * j:2 * j + 2, :]
                    v_.tensor_tensor(xs, xs, banks[m.bank][:, 0:T].unsqueeze(1).to_broadcast([P, 2, T]),
                                     ALU.add).then_inc(centred, 1)
                freed(v)
                v_.reciprocal(rs[:, 0:2], std[:, 0:2]).then_inc(rs_ready, 1)
                done(b)
                at, ab = ROW[tag[0]] + tag[2], ROW[tag[1]] + tag[2]
                n0 = tally.get("ln_ready", 0)
                count(ln_ready, KT)
                for k in range(KT + 2):
                    if k < KT:
                        v_.scalar_tensor_tensor(hT[:, k, :], xT[:, k, :], pcol[:, at + k:at + k + 1], banks[b.bank][:, 0:T],
                                                ALU.mult, ALU.mult).then_inc(ln_ready, 1)
                    if 1 <= k <= KT:
                        dve.wait_ge(ln_ready, n0 + k)
                        ins = v_.tensor_scalar(xT[:, k - 1, :], hT[:, k - 1, :], pcol[:, ab + k - 1:ab + k], None, ALU.add)
                        ins.then_inc(y_ready if last else dve_step, 1)
                        if not last:
                            steps[0] += 1
                    if k >= 2 and not last:
                        dve.wait_ge(dve_step, steps[0] - (k <= KT))
                        dve.wait_ge(hi_part, count(hi_part))
                        v_.tensor_tensor(h_lo[:, k - 2, :], xT[:, k - 2, :], h_hi[:, k - 2, :].bitcast(F32),
                                         ALU.subtract).then_inc(h_ready, 1)

            def mix(l):
                it = items["m", l]
                us = it["units"]
                v_.memset(pool_u[:, :, 0:PADW], 0.0)
                link(v_.memset(conv_h[:, :, 0:PADW], 0.0))
                for u in us[0:4]:
                    refill(u)
                dsts = (qD[:, 0:2, :], qD[:, 2:4, :], kdT, qiT[:, 0:2, :], qiT[:, 2:4, :], kidT.unsqueeze(1))
                for n, (x, r, dst) in enumerate(zip(it["qk"], it["rot"], dsts)):
                    refill(us[4 + n])
                    rotate(n, x, r, dst, tabd[:, 0, :], tabd[:, 1, :], tiles=1 if n == 5 else 2)
                freed(it["v"])
                base = NT * IDX_HEADS * l
                for n, s in enumerate(it["idx"]):
                    freed(s)
                    for tt in range(NT):
                        src, wh = relu[n % 2][:, tt * T:(tt + 1) * T], wi[:, tt, n:n + 1]
                        if n == 0:
                            v_.tensor_scalar(score[:, tt, :], src, wh, None, ALU.mult).then_inc(score_step, 1)
                        else:
                            dve.wait_ge(score_step, base + 2 * n + tt - 1)
                            v_.scalar_tensor_tensor(score[:, tt, :], src, wh, score[:, tt, :], ALU.mult,
                                                    ALU.add).then_inc(score_step, 1)

                def topk():
                    for tt in range(NT):
                        dve.wait_ge(score_masked, count(score_masked))
                        src = score[:, tt, :]
                        for _ in range(TOPK // 8):
                            link(v_.max(m8[:], src))
                            link(v_.match_replace(work[:, tt, :], m8[:], src, TAKEN))
                            src = work[:, tt, :]
                            yield
                        link(v_.tensor_scalar(src, src, TAKEN, 1.0, ALU.is_equal, ALU.subtract))
                        v_.tensor_scalar(src, src, -NEG, None, ALU.mult).then_inc(picked, 1)
                        yield

                def convolve():
                    freed(it["conv_g"])
                    link(v_.tensor_tensor(conv_h[:, :, PADW:], conv_a[:], conv_y[:], ALU.mult))
                    cw, cb = ROW["conv_dw_w_2"] + l * CONV_W * 2, ROW["conv_dw_b_2"] + 2 * l
                    for j in range(CONV_W):
                        for m in range(2):
                            hh = conv_h[:, m, PADW - CONV_W + 1 + j:PADW - CONV_W + 1 + j + T]
                            wj = pcol[:, cw + 2 * j + m:cw + 2 * j + m + 1]
                            if j == 0:
                                ins = v_.tensor_scalar(conv_y[:, m, :], hh, wj, pcol[:, cb + m:cb + m + 1], ALU.mult, ALU.add)
                            else:
                                ins = v_.scalar_tensor_tensor(conv_y[:, m, :], hh, wj, conv_y[:, m, :], ALU.mult, ALU.add)
                            if j == CONV_W - 1 and m == 1:
                                ins.then_inc(conv_out, 1)
                            else:
                                link(ins, behind=1)
                        if j % 2:
                            yield

                def pools():
                    end = T + PADW
                    freed(it["pool"])
                    link(v_.tensor_tensor(pool_w2[:, :, 1:], pool_u[:, :, 1:], pool_u[:, :, :end - 1], ALU.add))
                    link(v_.tensor_tensor(pool_w4[:, :, 3:], pool_w2[:, :, 3:], pool_w2[:, :, 1:end - 2], ALU.add))
                    v_.tensor_tensor(mixed[0:64, 0, :], pool_w2[0:64, 0, PADW:], inv_cnt[0:64, 0, :], ALU.mult)
                    link(v_.tensor_tensor(pool_w2[:, 1, 7:], pool_w4[:, 1, 7:], pool_w4[:, 1, 3:end - 4], ALU.add))
                    yield
                    v_.tensor_tensor(mixed[64:128, 0, :], pool_w4[64:128, 0, PADW:], inv_cnt[64:128, 0, :], ALU.mult)
                    v_.tensor_tensor(mixed[0:64, 1, :], pool_w2[0:64, 1, PADW:], inv_cnt[0:64, 1, :], ALU.mult)
                    link(v_.tensor_tensor(pool_w4[64:128, 1, 15:], pool_w2[64:128, 1, 15:], pool_w2[64:128, 1, 7:end - 8], ALU.add))
                    link(v_.tensor_tensor(mixed[64:128, 1, :], pool_w4[64:128, 1, PADW:], inv_cnt[64:128, 1, :], ALU.mult))
                    v_.tensor_tensor(mixed[:], mixed[:], pool_u[:, :, PADW:], ALU.subtract).then_inc(mixed_ready, 1)
                    yield

                n_steps = NT * (TOPK // 8 + 1) + CONV_W // 2 + 2
                work_ = (s for part in (topk, convolve, pools) for s in part())
                n_units = 12
                each = -(-n_steps // n_units)
                for j in range(n_units):
                    u = it["gates"][j % 3][0]
                    rest(u.slot, u.index + 3 * (j // 3) + SLOTS + 1)
                    for _ in range(each):
                        next(work_, None)
                for _ in work_:
                    pass
                x = it["poolmix"]
                done(x)
                at = ROW["pool_scale_2"] + 2 * l
                for m in range(2):
                    ins = v_.tensor_scalar(mixed[:, m, :], banks[x.bank][:, m * T:(m + 1) * T], pcol[:, at + m:at + m + 1],
                                           None, ALU.mult)
                free(ins, x)
                freed(x)
                link(v_.tensor_copy(pool_hi[:], mixed[:]))
                v_.tensor_tensor(pool_lo[:], mixed[:], pool_hi[:].bitcast(F32), ALU.subtract).then_inc(branch_ready, 1)
                s, m_, v, b = it["cln"]
                done(s)
                free(v_.tensor_scalar(rs[:, 0:2], banks[s.bank][:, 0:2], -1.0 / 256, None, ALU.mult), s)
                done(m_)
                v_.tensor_tensor(conv_y[:], conv_y[:], banks[m_.bank][:, 0:T].unsqueeze(1).to_broadcast([P, 2, T]),
                                 ALU.add).then_inc(centred, 1)
                freed(v)
                v_.reciprocal(rs[:, 0:2], std[:, 0:2]).then_inc(rs_ready, 1)
                done(b)
                at = ROW["conv_ln_g_2"] + 2 * l
                count(ln_ready, 2)
                for m in range(2):
                    v_.scalar_tensor_tensor(conv_y[:, m, :], conv_y[:, m, :], pcol[:, at + m:at + m + 1],
                                            banks[b.bank][:, 0:T], ALU.mult, ALU.mult).then_inc(ln_ready, 1)
                dve.wait_ge(hi_part, count(hi_part))
                v_.tensor_tensor(conv_lo[:], conv_y[:], conv_hi[:].bitcast(F32), ALU.subtract).then_inc(branch_ready, 1)
                dve.wait_ge(keep_ready, count(keep_ready, NT))
                tag = ("m", l)
                attn_64(tag, N_HEADS, mask=work.rearrange("p t n -> p (t n)"), dst=(attn_hi, attn_lo),
                        scale=HD ** -0.5)
                for br, name in enumerate(("pool", "conv", "attn")):
                    refills((tag, name))
                    for m, x in enumerate(items[tag, name]):
                        done(x)
                        dst = hT[:, 2 * m:2 * m + 2, :]
                        tmp = rot[m % 2][:].rearrange("p (m n) -> p m n", m=2)
                        b = banks[x.bank][:].rearrange("p (m n) -> p m n", m=2)
                        g = gates[:, 8 * br + 2 * m:8 * br + 2 * m + 2, :]
                        free(v_.tensor_tensor(dst if br == 0 else tmp, b, g, ALU.mult), x)
                        if br:
                            freed(x)
                            ins = v_.tensor_tensor(dst, dst, tmp, ALU.add)
                            if br == 2:
                                ins.then_inc(to_split, 1)
                            else:
                                link(ins)
                        if br == 2 and m:
                            split_rest(4, 2, m - 1)
                split_rest(4, 2, 3)
                refills((tag, "wo"))
                residual(items[tag, "wo"], ALPHA)

            def ffn2(tag, l, before):
                head, body, tail = items[tag, "up"]
                w = ROW["ffn_dw_w_2"] + l * FCW * 44
                started0 = 22 * l
                g0 = count(gate_ready, FT) - FT
                chain0 = steps[0]

                def step(n, j, u, x, i=None):
                    def col(at):
                        return pcol[:, at:at + 1] if i is None else pcol[:, bass.ds(i * 3 + at, 1)]

                    if i is not None or n:
                        make((j - 1) % 3, n - 1, i)
                    done(x, i)
                    at = started0 + n + 1
                    dve.wait_ge(taps_started, at if i is None else i * 3 + at)
                    for m, tile in ((0, 0), (1, 22)):
                        o, b = pre[j][:, m * T:(m + 1) * T], banks[x.bank][:, m * T:(m + 1) * T]
                        v_.scalar_tensor_tensor(o[:, 1:], b[:, :T - 1], col(w + 44 + tile + n), o[:, 1:], ALU.mult,
                                                ALU.add).then_inc(dve_step, 1)
                    for m, tile in ((0, 0), (1, 22)):
                        o, b = pre[j][:, m * T:(m + 1) * T], banks[x.bank][:, m * T:(m + 1) * T]
                        at = chain0 + 2 * n + m + 1
                        dve.wait_ge(dve_step, at if i is None else i * 6 + at)
                        ins = v_.scalar_tensor_tensor(o[:, 2:], b[:, :T - 2], col(w + tile + n), o[:, 2:], ALU.mult, ALU.add)
                    free(ins, x)
                    refill(u, i)

                def make(j, n, i):
                    at = g0 + n + 1
                    dve.wait_ge(gate_ready, at if i is None else i * 3 + at)
                    at = before + n + 1
                    dve.wait_ge(hidden_ready, at if i is None else i * 3 + at)
                    v_.tensor_tensor(hT[:, j, :], pre[j][:, 0:T], pre[j][:, T:2 * T], ALU.mult).then_inc(product_ready, 1)

                for j, (u, x) in enumerate(head):
                    step(j, j, u, x)
                with dve.Fori(1, 7) as i:
                    for j, (u, x) in enumerate(body):
                        step(j, j, u, x, i)
                for u, x in tail:
                    step(FT - 1, 0, u, x)
                make(0, FT - 1, None)
                steps[0] += 44
                refills((tag, "down"))
                residual(items[tag, "down"], ALPHA)

            n_ffn = 0
            for kind, arg in phases():
                if kind == "start":
                    start()
                elif kind == "lambda":
                    lambdas()
                elif kind == "second":
                    second()
                elif kind == "rms":
                    c = "ABC"[arg[0] % 3] if arg[1] == "attn_norm" else None
                    rms(arg, ROW[arg[1]] + arg[2], c)
                elif kind == "A":
                    attn_a(arg)
                elif kind == "B":
                    attn_b(arg)
                elif kind == "C":
                    attn_c(arg)
                elif kind == "ffn":
                    ffn(("ffn", arg), FT * n_ffn)
                    n_ffn += 1
                elif kind == "rows2":
                    rows2()
                elif kind == "final":
                    rms("final", ROW["final_norm"], None, final=True)
                elif kind in ("ln", "ln_last"):
                    ln(arg, kind == "ln_last")
                elif kind == "mix":
                    mix(arg)
                elif kind == "ffn2":
                    ffn2(("ffn2", arg), arg, FT * n_ffn)
                    n_ffn += 1
                elif kind == "end":
                    for n, x in enumerate(items["end"]):
                        done(x)
                        free(v_.tensor_copy(xrows[:, n // 2, (n % 2) * 512:(n % 2 + 1) * 512], banks[x.bank][:]), x)


def lambda_init(i):
    return 0.8 - 0.6 * math.exp(-0.3 * i)


TWO_PI = (6.28125, float(np.float32(0.0019340515136718750)),
          2 * math.pi - 6.28125 - float(np.float32(0.0019340515136718750)))
MAGIC = 12582912.0
PI_IN = 3.1415925


def constants():
    f = np.float32

    def rope(rot_dim):
        pos = np.arange(T, dtype=f)
        inv = (f(500000.0) ** (-np.arange(0, rot_dim, 2, dtype=f) / f(rot_dim))).astype(f)
        ang = (pos[:, None] * inv[None, :]).astype(f)
        return np.cos(ang).astype(f), np.sin(ang).astype(f)

    def tables(cos, sin, starts, rows):
        r = cos.shape[1]
        c, s = np.ones((P, T), f), np.zeros((P, T), f)
        for a in starts:
            for z in range(2):
                c[a + z * r:a + (z + 1) * r] = cos.T
                s[a + z * r:a + (z + 1) * r] = sin.T
        return c, s

    def swap(starts, r):
        w = np.zeros((P, P), f)
        for a in starts:
            for d in range(r):
                w[a + r + d, a + d] = -1.0
                w[a + d, a + r + d] = 1.0
        return w

    ca, sa = tables(*rope(16), (0, 64), P)
    cb, sb_ = tables(*rope(32), (64,), P)
    order = np.arange(T).reshape(T // 4, 4).T.reshape(T)
    tab = np.stack([ca, sa, cb, sb_, ca[:, order], sa[:, order]], 1)
    rotm = np.stack([swap((0, 64), 8), swap((64,), 16), swap((0, 64), 32)], 1)
    cmask = np.empty((P, NT, 4 * P), f)
    for tt in range(NT):
        own = order[tt * P:(tt + 1) * P]
        near = np.abs(own[:, None] - order[None, :]) <= 64
        apart = own[:, None] - own[None, :]
        cmask[:, tt] = np.where(np.concatenate([near, apart % 4 == 0, apart % 16 == 0], 1), f(0), f(NEG))
    cnt = np.zeros((P, 2, T), f)
    for g, win in enumerate(POOL_WINDOWS):
        cnt[HD * (g % 2):HD * (g % 2) + HD, g // 2] = 1.0 / np.minimum(np.arange(T) + 1, win)
    invf = f(10000.0) ** (-np.arange(32, dtype=f) / f(32))
    return {"c_tab": tab, "c_rotm": rotm, "c_cmask": cmask.reshape(P, NT * 4 * P), "c_inv_cnt": cnt,
            "c_invf": np.tile(invf.astype(f), 4)[:, None]}


_INS = ["x", "attn_norm", "ffn_norm", "final_norm", "a_w_qkv", "a_lambda_q1", "a_lambda_k1", "a_lambda_q2",
        "a_lambda_k2", "a_subln", "a_w_o", "b_w_a", "b_q_norm", "b_kv_norm", "b_w_qb", "b_w_kvb", "b_w_o",
        "c_w_qkv", "c_w_o", "f_w_gu", "f_w_out", "positions_2", "ln_in_g_2", "ln_in_b_2", "w_in_2", "b_in_2",
        "pool_w_2", "pool_scale_2", "w_pool_out_2", "conv_dw_w_2", "conv_dw_b_2", "conv_ln_g_2", "conv_ln_b_2",
        "w_conv_out_2", "w_attn_out_2", "w_o_2", "ln1_g_2", "ln1_b_2", "w_up_2", "ffn_dw_w_2", "ffn_dw_b_2",
        "w_down_2", "ln2_g_2", "ln2_b_2"]


def kernel(**inputs):
    import concourse.bacc as bacc
    from concourse.bass_utils import run_bass_kernel_spmd

    nc = bacc.Bacc("TRN2", target_bir_lowering=False, num_devices=1)
    arrays, t = {}, {}
    for name, a in [*((n, inputs[n]) for n in _INS), *constants().items()]:
        a = np.ascontiguousarray(a)
        arrays[f"in_{name}"] = a
        t[name] = nc.dram_tensor(f"in_{name}", a.shape, mybir.dt.from_np(a.dtype), kind="ExternalInput").ap()
    t["out"] = nc.dram_tensor("out", (1, T, D), F32, kind="ExternalOutput").ap()
    build(nc, t)
    r = run_bass_kernel_spmd(nc, [arrays], core_ids=[0])
    return r.results[0]["out"]
```

```python
import math
from contextlib import ExitStack

import numpy as np
import concourse.bass as bass
from concourse import mybir

F32 = mybir.dt.float32
F32R = mybir.dt.float32r
I32 = mybir.dt.int32
ALU = mybir.AluOpType
ACT = mybir.ActivationFunctionType
AX = mybir.AxisListType

P = 128
T = 256
NT = T // P
D = 1024
KT = D // P
FFN = 2816
FT = FFN // P
DEPTH, DEPTH_2 = 4, 2
EPS, LN_EPS = 1e-6, 1e-5
ALPHA = (2 * DEPTH_2) ** 0.25
A_HEADS = 8
B_HEADS, B_QR, B_KVR, B_NOPE, B_ROPE, B_V = 16, 384, 256, 64, 32, 64
C_HEADS, C_GROUPS = 16, 3
HD = 64
N_HEADS, N_KV, IDX_HEADS, TOPK = 8, 2, 8, 64
CONV_W, FCW = 31, 3
FF_2 = 2816
POOL_WINDOWS = (2, 4, 8, 16)
FILL, TAKEN, NEG = -3.0e38, float(np.float32(-3.3e38)), -1.0e30

ROTATED_BEFORE_C = 16
SLOTS = 3
UNIT = 2048
BANKS = 8

ROWS = [("attn_norm", 32), ("ffn_norm", 32), ("final_norm", 8), ("a_subln", 2), ("b_q_norm", 3),
        ("b_kv_norm", 2), ("ln_in_g_2", 8), ("ln_in_b_2", 8), ("ln1_g_2", 16), ("ln1_b_2", 16),
        ("ln2_g_2", 16), ("ln2_b_2", 16), ("pool_scale_2", 4), ("conv_dw_w_2", 2 * CONV_W * 2),
        ("conv_dw_b_2", 4), ("conv_ln_g_2", 4), ("conv_ln_b_2", 4), ("ffn_dw_w_2", 2 * FCW * 44),
        ("ffn_dw_b_2", 88)]
Z_POOL, Z_CONV, Z_Q, Z_K, Z_V, Z_QI, Z_KI, Z_WI, Z_GATE = 0, 256, 768, 1280, 1408, 1536, 2048, 2112, 2120
B_ROWS = ([(Z_POOL + P * i, P) for i in range(10)] + [(Z_K, HD), (Z_K + HD, HD)]
          + [(Z_QI + P * i, P) for i in range(4)] + [(Z_KI, HD)] + [(Z_GATE + P * i, P) for i in range(24)])
B_POOL, B_CONV, B_Q, B_K, B_QI, B_KI, B_GATE = 0, 2, 6, 10, 12, 16, 17


def row_starts():
    at, n = {}, 0
    for name, rows in ROWS:
        at[name] = n
        n += rows
    for l in range(DEPTH_2):
        at["b_in", l] = n
        n += len(B_ROWS)
    return at, n


ROW, N_ROWS = row_starts()
ROW_TILES = -(-N_ROWS // P)


class Item:

    def __init__(self, bank, free):
        self.bank, self.free, self.done, self.step_done, self.step_free = bank, free, 0, 0, 0


class Unit:

    def __init__(self, index, loads, span=0, step_done=0):
        self.index, self.loads, self.slot = index, loads, index % SLOTS
        self.span, self.done, self.step_done = span, 0, step_done

    def at(self, i):
        u = Unit(self.index + i * self.span, self.loads)
        u.done = self.done + i * self.step_done
        return u


def build(nc, t, stages=99):
    with ExitStack() as ctx:
        def sb(name, shape, dt=F32, where=None):
            return (where or ctx).enter_context(nc.sbuf_tensor(name, shape, dt))

        def sem(name):
            return ctx.enter_context(nc.semaphore(name))

        raw = [sb(f"weights{s}", [P, UNIT]) for s in range(SLOTS)]
        w_hi = [sb(f"weights_hi{s}", [P, UNIT], F32R) for s in range(SLOTS)]
        w_lo = [sb(f"weights_lo{s}", [P, UNIT], F32R) for s in range(SLOTS)]
        xT = sb("xT", [P, KT, T])
        hT = sb("hT", [P, KT, T])
        h_hi = sb("h_hi", [P, KT, T], F32R)
        h_lo = sb("h_lo", [P, KT, T], F32R)
        sq = sb("sq", [P, KT, T])
        pres = sb("pres", [P, 6 * T])
        rots = sb("rots", [P, 4 * T])
        tab = sb("tab", [P, 6, T])
        rotm = sb("rotm", [P, 3, P])
        ident = sb("ident", [P, P])
        ones = sb("ones", [P, P])
        pcol = sb("pcol", [P, ROW_TILES * P])
        brow = sb("brow", [1, DEPTH_2, 136])
        eps = sb("eps", [P, 4])
        std = sb("std", [P, 16])
        rs = sb("rs", [P, 16])
        negmax = [sb(f"negmax{i}", [P, 2]) for i in range(4)]
        esum = [sb(f"esum{i}", [P, 2]) for i in range(4)]
        erec = [sb(f"erec{i}", [P, 2]) for i in range(4)]
        tiny = sb("tiny", [P, 1])
        lams = sb("lams", [P, 4])
        lame = sb("lame", [P, 4])
        neglam = sb("neglam", [P, 2])
        subg = sb("subg", [P, 2])
        invf = sb("invf", [P, 1])
        wi = sb("wi", [P, 2, 8])
        m8 = sb("m8", [P, 8])
        idle = sb("idle", [P, 4])
        banks = [ctx.enter_context(nc.psum_tensor(f"bank{b}", [P, 512], F32)) for b in range(BANKS)]

        with ExitStack() as area:
            Q = sb("Q", [P, 6144], where=area)
            K = sb("K", [P, 6144], where=area)
            V = sb("V", [P, 6144], where=area)
        with ExitStack() as area:
            hid_hi = sb("hid_hi", [P, FT * T], F32R, where=area)
            hid_lo = sb("hid_lo", [P, FT * T], F32R, where=area)
        with ExitStack() as area:
            G = sb("G", [P, 24 * T], where=area)
            Y = sb("Y", [P, 12 * T], where=area)
            attn_hi = sb("attn_hi", [P, 4, T], F32R, where=area)
            attn_lo = sb("attn_lo", [P, 4, T], F32R, where=area)
            poolw = sb("poolw", [P, DEPTH_2, 2, P], where=area)
            Z = sb("Z", [P, 4352], where=area)
            pool_hi = sb("pool_hi", [P, 2, T], F32R, where=area)
            pool_lo = sb("pool_lo", [P, 2, T], F32R, where=area)
            conv_hi = sb("conv_hi", [P, 2, T], F32R, where=area)
            conv_lo = sb("conv_lo", [P, 2, T], F32R, where=area)

        xrows = Q[:, 0:2048].rearrange("p (t n) -> p t n", t=NT)
        hflat = hT[:].rearrange("p m n -> p (m n)")
        expoT = [hflat[:, 1024 * i:1024 * (i + 1)] for i in range(2)]
        pre = [pres[:, 2 * T * i:2 * T * (i + 1)] for i in range(3)]
        rot = [rots[:, 2 * T * i:2 * T * (i + 1)] for i in range(2)]
        cmask = rots[:]
        prow1 = hflat[:, 0:P]
        prow2 = K[:, 2048:2048 + (ROW_TILES - 1) * P].rearrange("p (r n) -> p r n", n=P)
        qT = Q[:].rearrange("p (m n) -> p m n", n=T)
        kT = K[:].rearrange("p (m n) -> p m n", n=T)
        vA = V[:, 0:2048].rearrange("p (t n) -> p t n", t=NT)
        vC = V[:].rearrange("p (t n) -> p t n", t=NT)
        expoA = [V[:, 2048:3072], V[:, 3072:4096], pres[:, 0:1024]]
        expo = [sq[:].rearrange("p m n -> p (m n)")[:, 1024 * i:1024 * (i + 1)] for i in range(2)]
        expo.append(pres[:, 0:1024])
        latT = V[:, 4096:4096 + 5 * T].rearrange("p (m n) -> p m n", n=T)
        oT = V[:, 4096:6144].rearrange("p (m n) -> p m n", n=T)
        kr = V[:, 5376:5632]
        lamv = K[:, 0:512].rearrange("p (v d) -> p v d", d=HD)
        lamp = K[:, 512:768].rearrange("p (v d) -> p v d", d=HD)
        yT = Y[:].rearrange("p (m n) -> p m n", n=T)
        qD, kidT, kdT, qiT = yT[:, 0:4], yT[:, 4], yT[:, 5:7], yT[:, 7:11]
        vD = Y[:, 11 * T:12 * T].rearrange("p (t n) -> p t n", t=NT)
        gates = G[:].rearrange("p (m n) -> p m n", n=T)
        PADW = 32
        pool_u = Z[:, 0:576].rearrange("p (m n) -> p m n", m=2)
        pool_w2 = Z[:, 576:1152].rearrange("p (m n) -> p m n", m=2)
        pool_w4 = Z[:, 1152:1728].rearrange("p (m n) -> p m n", m=2)
        conv_a = Z[:, 1152:1664].rearrange("p (m n) -> p m n", m=2)
        conv_h = Z[:, 1728:2304].rearrange("p (m n) -> p m n", m=2)
        conv_y = Z[:, 2304:2816].rearrange("p (m n) -> p m n", m=2)
        mixed = Z[:, 2816:3328].rearrange("p (m n) -> p m n", m=2)
        score = Z[:, 3328:3840].rearrange("p (t n) -> p t n", t=NT)
        work = Z[:, 3840:4352].rearrange("p (t n) -> p t n", t=NT)
        tabd, inv_cnt = tab[:, 4:6, :], tab[:, 2:4, :]
        relu = [expoT[0][:, 0:512], expoT[1][:, 0:512]]
        pos_i = tab[:, 4, :].bitcast(I32)
        ang, turns, scr, red = (K[:, 1024 + T * i:1024 + T * (i + 1)] for i in range(4))

        pe_done = sem("pe_done")
        bank_free = [sem(f"bank_free{b}") for b in range(BANKS)]
        landed = [sem(f"weights_landed{s}") for s in range(SLOTS)]
        hi_ready = sem("hi_ready")
        lo_ready = sem("lo_ready")
        x_landed = sem("x_landed")
        rows_landed = sem("rows_landed")
        rows2_landed = sem("rows2_landed")
        consts_landed = sem("consts_landed")
        consts2_landed = sem("consts2_landed")
        cmask_landed = sem("cmask_landed")
        lam_landed = sem("lam_landed")
        pos_landed = sem("pos_landed")
        poolw_zeroed = sem("poolw_zeroed")
        area_free = sem("area_free")
        poolw_landed = sem("poolw_landed")
        out_stored = sem("out_stored")
        ident_ready = sem("ident_ready")
        lam_sums = sem("lam_sums")
        lam_exps = sem("lam_exps")
        angles_ready = sem("angles_ready")
        sines_ready = sem("sines_ready")
        squares_ready = sem("squares_ready")
        rs_ready = sem("rs_ready")
        to_split = sem("to_split")
        hi_part = sem("hi_part")
        h_ready = sem("h_ready")
        centred = sem("centred")
        ln_ready = sem("ln_ready")
        y_ready = sem("y_ready")
        rot_ready = sem("rot_ready")
        kr_ready = sem("kr_ready")
        kr_spread = sem("kr_spread")
        negmax_ready = sem("negmax_ready")
        exp_ready = sem("exp_ready")
        probs_ready = sem("probs_ready")
        dve_step = sem("dve_step")
        product_ready = sem("product_ready")
        hid_step = sem("hid_step")
        hidden_ready = sem("hidden_ready")
        taps_started = sem("taps_started")
        gate_ready = sem("gate_ready")
        score_step = sem("score_step")
        score_masked = sem("score_masked")
        picked = sem("picked")
        keep_ready = sem("keep_ready")
        glu_ready = sem("glu_ready")
        conv_step = sem("conv_step")
        conv_out = sem("conv_out")
        mixed_ready = sem("mixed_ready")
        branch_ready = sem("branch_ready")
        act_step = sem("act_step")

        def phases():
            yield "start", 0
            n = 0
            for i in range(DEPTH):
                kind = "ABC"[i % 3]
                yield "rms", (i, "attn_norm", KT * i)
                if i == 0:
                    yield "lambda", 0
                if i == DEPTH - 1:
                    yield "second", 0
                yield kind, i
                yield "rms", (i, "ffn_norm", KT * i)
                if i == DEPTH - 1:
                    yield "rows2", 0
                yield "ffn", i
                n += 1
                if n >= stages:
                    yield "end", 0
                    return
            yield "final", 0
            yield "ln", ("ln_in_g_2", "ln_in_b_2", 0)
            for l in range(DEPTH_2):
                yield "mix", l
                yield "ln", ("ln1_g_2", "ln1_b_2", KT * l)
                yield "ffn2", l
                n += 1
                last = n >= stages or l == DEPTH_2 - 1
                yield ("ln_last" if last else "ln"), ("ln2_g_2", "ln2_b_2", KT * l)
                if last:
                    break
            yield "end", 0

        def row_loads(part):
            out = []

            def add(at, src, c0=0, c1=P):
                n, done = src.shape[0], 0
                while done < n:
                    r = at + done
                    m = min(n - done, P - r % P)
                    dst = prow1 if r < P else prow2[:, r // P - 1, :]
                    if (r >= P) == part:
                        out.append((dst[r % P:r % P + m, c0:c1], src[done:done + m, :]))
                    done += m

            for name, rows in ROWS:
                a = t[name]
                if len(a.shape) == 1:
                    a = a.rearrange("(r n) -> r n", n=P)
                elif len(a.shape) == 2:
                    a = a.rearrange("l (r n) -> (l r) n", n=P)
                else:
                    a = a.rearrange("l c (r n) -> (l c r) n", n=P)
                add(ROW[name], a)
            for l in range(DEPTH_2):
                b, at = t["b_in_2"][l], ROW["b_in", l]
                for first, n, col in ((B_POOL, 10, Z_POOL), (B_QI, 4, Z_QI), (B_GATE, 24, Z_GATE)):
                    add(at + first, b[col:col + n * P].rearrange("(r n) -> r n", n=P))
                add(at + B_K, b[Z_K:Z_K + 2 * HD].rearrange("(r n) -> r n", n=P))
                for half in range(2):
                    k0 = Z_K + HD * (1 - half)
                    add(at + B_K + 1, b[k0:k0 + HD].rearrange("(r n) -> r n", n=HD), HD * half, HD * half + HD)
                    add(at + B_KI, b[Z_KI:Z_KI + HD].rearrange("(r n) -> r n", n=HD), HD * half, HD * half + HD)
            return out

        def rows_of(name, l):
            w = t[name] if l is None else t[name][l]
            return w.rearrange("(k p) n -> p k n", p=P)

        def view(width):
            return lambda slot: slot[:, 0:UNIT // width * width].rearrange("p (k n) -> p k n", n=width)

        def block_loads(name, l, n0, width=256, at=0, k=KT):
            w = rows_of(name, l)
            cols = slice(n0, n0 + width) if isinstance(n0, int) else bass.ds(n0, width)
            return [(lambda s, a=a: view(UNIT // k)(s)[:, a:a + k // 2, at:at + width], w[:, a:a + k // 2, cols])
                    for a in (0, k // 2)]

        def deep_loads(name, l, k0, n0=0):
            w = rows_of(name, l)
            return [(lambda s, j=j: view(1024)(s)[:, j, :],
                     w[:, k0 + j, n0:n0 + 1024] if isinstance(k0, int)
                     else w[:, bass.ds(k0 + j, 1), n0:n0 + 1024].rearrange("p k n -> p (k n)")) for j in range(2)]

        def gate_loads(name, l, n0):
            w = rows_of(name, l)
            out = []
            for z in range(2):
                cols = slice(n0 + z * FFN, n0 + z * FFN + P) if isinstance(n0, int) else bass.ds(n0 + z * FFN, P)
                out.append((lambda s, z=z: view(256)(s)[:, :, z * P:(z + 1) * P], w[:, :, cols]))
            return out

        def by_class(x, natural):
            if len(x.shape) == 3:
                return x.rearrange("p m (u c) -> p m c u" if natural else "p m (c u) -> p m c u", c=4)
            return x.rearrange("p (u c) -> p c u" if natural else "p (c u) -> p c u", c=4)

        block = ctx.enter_context(nc.Block())
        units, items, total = [], {}, [0]

        @block.tensor
        def _(pe):
            n_done = [0]
            uses = [0] * BANKS
            tally = {}

            def count(s, n=1):
                tally[s.name] = tally.get(s.name, 0) + n
                return tally[s.name]

            def open_item(bank, released=True):
                if uses[bank]:
                    pe.wait_ge(bank_free[bank], uses[bank])
                uses[bank] += released
                return Item(bank, uses[bank])

            def close(ins, *what):
                n_done[0] += 1
                ins.then_inc(pe_done, 1)
                for w in what:
                    w.done = n_done[0]

            def next_unit(loads):
                u = Unit(total[0], loads)
                total[0] += 1
                units.append(u)
                pe.wait_ge(lo_ready, u.index + 1)
                return u

            def loop_units(loads, n, rounds, per):
                for j in range(n):
                    u = Unit(total[0] + j, lambda r, j=j: loads(r, j), span=n, step_done=per)
                    u.rounds = rounds
                    units.append(u)
                    yield u

            def parts(u, width):
                return view(width)(w_hi[u.slot]), view(width)(w_lo[u.slot])

            def product(out, a, b, first, last):
                for n, (x, y) in enumerate(((a[0], b[0]), (a[0], b[1]), (a[1], b[0]))):
                    mm = nc.tensor.matmul(out, x, y, start=(first and n == 0), stop=(last and n == 2),
                                          skip_group_check=True)
                return mm

            def tiles(outs, w, cols, src, k=KT, gate=None):
                for j in range(k):
                    if gate is not None:
                        pe.wait_ge(h_ready, gate + j + 1)
                    s = [x[:, j, :] for x in src]
                    for m, (o, c) in enumerate(zip(outs, cols)):
                        mm = product(o, [x[:, j, c:c + P] for x in w], s, j == 0 and m == 0, j == k - 1)
                return mm

            def halves(bank):
                return [banks[bank][:, 0:T], banks[bank][:, T:2 * T]]

            def token_major(out, w, cols, tt, k=KT, k0=0, last=True):
                for j in range(k):
                    mm = product(out, [x[:, k0 + j, tt * P:(tt + 1) * P] for x in h], [x[:, j, cols] for x in w],
                                 j == 0, last and j == k - 1)
                return mm

            h = (h_hi, h_lo)

            def stats(bank, col, src, ts):
                for tt in range(NT):
                    for n, j in enumerate(ts):
                        mm = nc.tensor.matmul(banks[bank][:, col + tt:col + tt + 1], src[:, j, tt * P:(tt + 1) * P],
                                              ones[:, 0:1], start=(n == 0), stop=(n == len(ts) - 1))
                return mm

            def spread(bank, at, col):
                for tt in range(NT):
                    mm = nc.tensor.matmul(banks[bank][:, at + tt * P:at + (tt + 1) * P],
                                          rs[:, col + tt:col + tt + 1].to_broadcast([P, P]), ident[:],
                                          start=True, stop=True)
                return mm

            def start():
                pe.wait_ge(ident_ready, 3)
                pe.wait_ge(x_landed, 16)
                xs = []
                for j in range(4):
                    x = open_item(j)
                    for kk in range(2):
                        for tt in range(NT):
                            mm = nc.tensor.transpose(banks[j][:, kk * T + tt * P:kk * T + (tt + 1) * P],
                                                     xrows[:, tt, (2 * j + kk) * P:(2 * j + kk + 1) * P], ident[:])
                    close(mm, x)
                    xs.append(x)
                pe.wait_ge(rows_landed, 16 * len(row_loads(0)))
                r = open_item(4)
                close(nc.tensor.transpose(banks[4][:, 0:P], prow1, ident[:]), r)
                items["start"] = xs, r
                for b in (5, 6):
                    x = open_item(b)
                    close(nc.tensor.matmul(banks[b][:, 0:P], ident[:], ident[:], start=True, stop=True), x)
                    items["idle", b] = x

            def rows2():
                pe.wait_ge(rows2_landed, 16 * len(row_loads(1)))
                out = []
                for j in range(0, ROW_TILES - 1, 4):
                    r = open_item(j // 4)
                    for jj in range(j, min(j + 4, ROW_TILES - 1)):
                        n = min(P, N_ROWS - (jj + 1) * P)
                        mm = nc.tensor.transpose(banks[r.bank][:, (jj - j) * P:(jj - j) * P + n], prow2[0:n, jj, :],
                                                 ident[0:n, 0:n])
                    close(mm, r)
                    out.append(r)
                items["rows2"] = out

            norm = [None]

            def norm_sums():
                if norm[0]:
                    pe.wait_ge(squares_ready, count(squares_ready, 4))
                    s = open_item(6)
                    close(stats(6, 0, sq, range(KT)), s)
                    items[norm[0]] = [s]

            def norm_spread():
                if norm[0]:
                    pe.wait_ge(rs_ready, count(rs_ready))
                    b = open_item(7)
                    close(spread(7, 0, 0), b)
                    items[norm[0]].append(b)
                    norm[0] = None

            def sums(bank, src, ready):
                x = open_item(bank)
                for j in range(KT):
                    if j % 2 == 0:
                        ready(j // 2)
                    mm = nc.tensor.matmul(banks[bank][:, 0:T], ones[:], src[:, j, :], start=(j == 0), stop=(j == KT - 1))
                close(mm, x)
                return x

            def final():
                x = sums(6, sq, lambda j: pe.wait_ge(squares_ready, count(squares_ready)))
                items["final"] = [x]

            def rotation(r, x, m, n=2 * T, lo=0, hi=P, i=None):
                pe.wait_ge(bank_free[x.bank], x.free if i is None else i * x.step_free + x.free)
                close(nc.tensor.matmul(banks[r.bank][lo:hi, 0:n], rotm[lo:hi, m, lo:hi],
                                       pre[x.pre][lo:hi, 0:n], start=True, stop=True), r)

            def deep(name, l, n_units, src, tag, bank0, ready, looped=False):
                head, loop, tail = [], [], []
                out = None

                def step(u, n, first, last, at=None):
                    nonlocal out
                    ready(n, None)
                    if out is None:
                        out = [open_item(bank0 + b) for b in range(4)]
                    w = parts(u, 1024)
                    for m in range(8):
                        o = halves(out[m // 2].bank)[m % 2]
                        for j in range(2):
                            s = [x[:, (2 * n + j) * T:(2 * n + j + 1) * T] for x in src]
                            mm = product(o, [x[:, j, m * P:(m + 1) * P] for x in w], s,
                                         first and j == 0 and m % 2 == 0, last and j == 1)
                        if last and m % 2 == 1 and m < 7:
                            close(mm, out[m // 2])
                    close(mm, u, *([out[3]] if last else []))

                if not looped:
                    for n in range(n_units):
                        u = next_unit(deep_loads(name, l, 2 * n))
                        step(u, n, n == 0, n == n_units - 1)
                        head.append(u)
                else:
                    for n in range(3):
                        u = next_unit(deep_loads(name, l, 2 * n))
                        step(u, n, n == 0, False)
                        head.append(u)
                    total[0] -= 3
                    done0 = n_done[0] - 3
                    n_done[0] = done0
                    with pe.Fori(1, 3) as i:
                        for n, u in enumerate(loop_units(lambda r, j: deep_loads(name, l, r * 6 + 2 * j), 3, (1, 3), 3)):
                            pe.wait_ge(lo_ready, i * 3 + (u.index + 1))
                            ready(n, i)
                            w = parts(u, 1024)
                            for m in range(8):
                                o = halves(out[m // 2].bank)[m % 2]
                                for j in range(2):
                                    s = [x[:, bass.ds(i * (6 * T) + (2 * n + j) * T, T)] for x in src]
                                    mm = product(o, [x[:, j, m * P:(m + 1) * P] for x in w], s, False, False)
                            close(mm, u)
                            loop.append(u)
                    total[0] += 9
                    n_done[0] = done0 + 9
                    for n in range(9, 11):
                        u = next_unit(deep_loads(name, l, 2 * n))
                        step(u, n, False, n == 10)
                        tail.append(u)
                items[tag] = out
                items[tag, "units"] = head, loop, tail

            def wo(name, l, tag, bank0, src_items=None):
                base = None if src_items else count(h_ready, 4) - 4

                def ready(n, i):
                    if src_items:
                        x = src_items[n]
                        pe.wait_ge(bank_free[x.bank], x.free)
                    else:
                        pe.wait_ge(h_ready, base + n + 1)
                flat = [x[:].rearrange("p m n -> p (m n)") for x in h]
                deep(name, l, 4, flat, tag, bank0, ready)

            def ffn(name_up, name_down, l, tag):
                gate = count(h_ready, KT) - KT
                hid0 = 3 + count(hidden_ready, FT) - FT
                head, body = [], []
                for j in range(3):
                    u = next_unit(gate_loads(name_up, l, j * P))
                    x = open_item(4 + j)
                    close(tiles(halves(4 + j), parts(u, 256), (0, P), h, gate=gate if j == 0 else None), x, u)
                    head.append((u, x))
                    (norm_sums, norm_spread, lambda: None)[j]()
                rounds = 7
                done0, total[0] = n_done[0] - 3, total[0] - 3
                n_done[0] = done0
                uses0 = [n - 1 for n in uses]
                with pe.Fori(1, rounds) as i:
                    for j, u in enumerate(loop_units(lambda r, j: gate_loads(name_up, l, r * 384 + j * P), 3, (1, rounds), 3)):
                        pe.wait_ge(lo_ready, i * 3 + (u.index + 1))
                        b = 4 + j
                        pe.wait_ge(bank_free[b], i + uses0[b])
                        x = Item(b, uses0[b] + 1)
                        x.step_done, x.step_free = 3, 1
                        close(tiles(halves(b), parts(u, 256), (0, P), h), x, u)
                        body.append((u, x))
                n_done[0] = done0 + 3 * rounds
                total[0] += 3 * rounds
                for j in range(3):
                    uses[4 + j] += rounds - 1
                u = next_unit(gate_loads(name_up, l, 21 * P))
                x = open_item(4)
                close(tiles(halves(4), parts(u, 256), (0, P), h), x, u)
                items[tag, "up"] = head, body, [(u, x)]

                def ready(n, i):
                    pe.wait_ge(hidden_ready, hid0 + 2 * n + 2 if i is None else i * 6 + (hid0 + 2 * n + 2))
                deep(name_down, l, 11, (hid_hi, hid_lo), (tag, "down"), 0, ready, looped=True)

            def transposes(hd, plan, expos):
                pe.wait_ge(probs_ready, count(probs_ready))
                out = []
                for g, moves in enumerate(plan):
                    it = open_item(4 + (hd * len(plan) + g) % 2)
                    for a, b in moves:
                        mm = nc.tensor.transpose(banks[it.bank][:, b:b + P], expos[hd % 3][:, a:a + P], ident[:])
                    close(mm, it)
                    out.append(it)
                return out

            plain = [[(T * tt + kt * P, kt * T + tt * P) for kt in range(2) for tt in range(NT)]]

            def attn_a(i):
                l = i // 3
                gate = count(h_ready, KT) - KT
                us, xs, rr, vs = [], [], [], []
                pending = None
                for n in range(12):
                    u = next_unit(block_loads("a_w_qkv", l, 256 * n))
                    w = parts(u, 256)
                    if n < 8:
                        x = open_item(n % 3)
                        x.pre = n % 3
                        close(tiles(halves(x.bank), w, (0, P), h, gate=gate if n == 0 else None), x, u)
                        xs.append(x)
                    else:
                        v = open_item(5 + n % 2)
                        for tt in range(NT):
                            mm = token_major(halves(v.bank)[tt], w, slice(0, 256), tt)
                        close(mm, v, u)
                        vs.append(v)
                    if pending is not None:
                        r = open_item(3 + (n - 1) % 2)
                        rotation(r, pending, 0)
                        rr.append(r)
                    if n < 2:
                        (norm_sums, norm_spread)[n]()
                    pending = x if n < 8 else None
                    us.append(u)
                items[i, "qk"], items[i, "rot"], items[i, "v"], items[i, "units"] = xs, rr, vs, us
                pe.wait_ge(rot_ready, count(rot_ready, 8))
                for v in vs[-2:]:
                    pe.wait_ge(bank_free[v.bank], v.free)
                S, TT, O = [], [], []
                for hd in range(A_HEADS + 4):
                    if hd < A_HEADS:
                        for sub in range(2):
                            s = open_item((2 * hd + sub) % 4)
                            a = HD * sub
                            for tt in range(NT):
                                mm = nc.tensor.matmul(banks[s.bank][:, tt * T:(tt + 1) * T],
                                                      qT[a:a + HD, hd, tt * P:(tt + 1) * P],
                                                      qT[a:a + HD, KT + hd, :], start=True, stop=True)
                            close(mm, s)
                            S.append(s)
                    if hd >= 4:
                        g = hd - 4
                        if g % 2 == 0:
                            o = open_item(6 + (g // 2) % 2)
                            O.append(o)
                        pe.wait_ge(bank_free[TT[g][0].bank], TT[g][0].free)
                        for kt in range(NT):
                            mm = nc.tensor.matmul(halves(o.bank)[g % 2], vA[:, kt, g * P:(g + 1) * P],
                                                  expoT[g % 2][:, kt * T:(kt + 1) * T],
                                                  start=(kt == 0), stop=(kt == NT - 1))
                        close(mm, o)
                        TT[g][0].used = n_done[0]
                    if 2 <= hd < A_HEADS + 2:
                        TT.append(transposes(hd - 2, plain, expoA))
                items[i, "S"], items[i, "T"], items[i, "O"] = S, TT, O
                pe.wait_ge(squares_ready, count(squares_ready, 4))
                s = open_item(5)
                for hd in range(A_HEADS):
                    mm = stats(5, 2 * hd, sq, [hd])
                close(mm, s)
                pe.wait_ge(rs_ready, count(rs_ready))
                sp_items = []
                for g in range(4):
                    b = open_item(g)
                    for hh in range(2):
                        mm = spread(g, hh * T, 2 * (2 * g + hh))
                    close(mm, b)
                    sp_items.append(b)
                items[i, "subln"] = s, sp_items
                wo("a_w_o", l, (i, "wo"), 4)

            def attn_64(tag, heads, score_parts, pv_parts, plan, v_of, masked=True):
                S, TT, O = [], [], []
                per = 2 if len(plan) == 2 else 1
                for hd in range(heads + 4):
                    if hd < heads:
                        mine = []
                        for n, part in enumerate(score_parts(hd)):
                            s = open_item((per * hd + n) % 4)
                            for a, b, lhsT, rhs in part:
                                mm = nc.tensor.matmul(banks[s.bank][:, a:b], lhsT, rhs, start=True, stop=True)
                            close(mm, s)
                            mine.append(s)
                        S.append(mine)
                    if hd >= 4:
                        g = hd - 4
                        if g % 4 == 0:
                            o = open_item(6 + (g // 4) % 2)
                            O.append(o)
                        for it in TT[g]:
                            pe.wait_ge(bank_free[it.bank], it.free)
                        a = HD * (g % 2)
                        c0 = (g // 2 % 2) * T
                        for n, (v, e0, e1, q0, q1) in enumerate(pv_parts):
                            mm = nc.tensor.matmul(banks[o.bank][a:a + HD, c0 + q0:c0 + q1], v_of(g, *v),
                                                  expoT[g % 2][:, e0:e1], start=(n == 0), stop=(n == len(pv_parts) - 1))
                        close(mm, o)
                        for it in TT[g]:
                            it.used = n_done[0]
                    if 2 <= hd < heads + 2:
                        TT.append(transposes(hd - 2, plan, expo))
                items[tag, "S"], items[tag, "T"], items[tag, "O"] = S, TT, O

            plain_pv = [((kt,), kt * T, (kt + 1) * T, 0, T) for kt in range(2)]

            def attn_b(i):
                gate = count(h_ready, KT) - KT
                us, raw_items = [], []
                for n in range(2):
                    u = next_unit(block_loads("b_w_a", 0, 256 * n))
                    raw_items.append(open_item(n))
                    close(tiles(halves(n), parts(u, 256), (0, P), h, gate=gate if n == 0 else None), raw_items[n], u)
                    (norm_sums, norm_spread)[n]()
                    us.append(u)
                w = rows_of("b_w_a", 0)
                u = next_unit([(lambda s: view(256)(s)[:, :, 0:P], w[:, :, 512:640]),
                               (lambda s: view(256)(s)[:, :, 192:224], w[:, :, 640:672])])
                raw_items.append(open_item(2))
                close(tiles(halves(2), parts(u, 256), (0, P), h), raw_items[2], u)
                raw_items[2].pre = 2
                us.append(u)
                pe.wait_ge(squares_ready, count(squares_ready, 3))
                s = open_item(6)
                stats(6, 0, sq, range(3))
                close(stats(6, 2, sq, range(3, 5)), s)
                r = open_item(3)
                rotation(r, raw_items[2], 1, n=T, lo=64, hi=96)
                pe.wait_ge(rs_ready, count(rs_ready))
                b = open_item(7, released=False)
                spread(7, 0, 0)
                close(spread(7, T, 2), b)
                items[i, "raw"], items[i, "stat"], items[i, "krot"] = raw_items, (s, b), r
                pe.wait_ge(h_ready, count(h_ready, 5))
                xs, rr, ks, vs = [], [], [], []
                pending = None
                wq = rows_of("b_w_qb", 0)
                for q in range(4):
                    u = next_unit([(lambda s, z=z: s[:, 0:1152].rearrange("p (k n) -> p k n", n=384)[:, :, 192 * z:192 * z + 192],
                                    wq[:, :, q * 384 + 192 * z:q * 384 + 192 * z + 192]) for z in range(2)])
                    w = [x[:, 0:1152].rearrange("p (k n) -> p k n", n=384) for x in (w_hi[u.slot], w_lo[u.slot])]
                    for m in range(2):
                        n = 2 * q + m
                        x = open_item(n % 3)
                        x.pre = n % 3
                        for hh in range(2):
                            col = (2 * m + hh) * 96
                            for j in range(3):
                                mm = product(banks[x.bank][0:96, hh * T:(hh + 1) * T], [y[:, j, col:col + 96] for y in w],
                                             [y[:, j, :] for y in h], j == 0, j == 2)
                        close(mm, x, *([u] if m else []))
                        xs.append(x)
                        if pending is not None:
                            r = open_item(3 + (n - 1) % 2)
                            rotation(r, pending, 1, hi=96)
                            rr.append(r)
                        pending = x
                    us.append(u)
                for half in range(2):
                    u = next_unit(deep_loads("b_w_kvb", 0, 0, half * 1024))
                    w = parts(u, 1024)
                    for m in range(4):
                        x = open_item(5 + m % 2)
                        for hh in range(2):
                            col = (2 * m + hh) * P
                            for j in range(2):
                                mm = product(halves(x.bank)[hh], [y[:, j, col:col + P] for y in w],
                                             [y[:, 3 + j, :] for y in h], j == 0, j == 1)
                        close(mm, x)
                        ks.append(x)
                        if m == 0 and half == 0:
                            r = open_item(3 + 7 % 2)
                            rotation(r, pending, 1, hi=96)
                            rr.append(r)
                    for tt in range(NT):
                        v = open_item(half * 2 + tt)
                        for j in range(2):
                            mm = product(banks[v.bank][:].rearrange("p (h d) -> p h d", d=HD),
                                         [y[:, 3 + j, tt * P:(tt + 1) * P] for y in h],
                                         [y[:, j, :].rearrange("p (h d) -> p h d", d=P)[:, :, HD:P] for y in w],
                                         j == 0, j == 1)
                        close(mm, v, *([u] if tt else []))
                        vs.append(v)
                    us.append(u)
                items[i, "qk"], items[i, "rot"], items[i, "k"], items[i, "v"], items[i, "units"] = xs, rr, ks, vs, us
                pe.wait_ge(rot_ready, count(rot_ready, 8))
                pe.wait_ge(kr_spread, count(kr_spread))
                for v in ks[-2:] + vs:
                    pe.wait_ge(bank_free[v.bank], v.free)
                attn_64(i, B_HEADS,
                        lambda hd: [[(tt * T, (tt + 1) * T, qT[0:96, hd, tt * P:(tt + 1) * P], kT[0:96, hd, :])
                                     for tt in range(NT)]],
                        plain_pv, plain, lambda hd, kt: vA[:, kt, hd * HD:(hd + 1) * HD])
                wo("b_w_o", 0, (i, "wo"), 0, items[i, "O"])

            c_plan = [[(512 * tt + kt * P, kt * T + tt * P) for kt in range(2) for tt in range(NT)],
                      [(512 * tt + T + g * P, g * T + tt * P) for g in range(2) for tt in range(NT)]]
            c_pv = ([((0, kt), kt * T, (kt + 1) * T, 0, T) for kt in range(2)]
                    + [((g, tt), 512 + (g - 1) * T + tt * P, 512 + (g - 1) * T + (tt + 1) * P, tt * P, (tt + 1) * P)
                       for g in (1, 2) for tt in range(NT)])

            def attn_c(i):
                gate = count(h_ready, KT) - KT
                norm_sums()
                norm_spread()
                done0, uses0 = n_done[0], list(uses)
                per, seen = 20, {b: 0 for b in range(6)}
                xs, rr, vs, us = [], [], [], []
                shares = {0: 4, 1: 4, 2: 4, 3: 4, 4: 2, 5: 2}
                with pe.Fori(0, C_GROUPS) as g:
                    pending = None

                    def take(bank):
                        pe.wait_ge(bank_free[bank], g * shares[bank] + (uses0[bank] + seen[bank]))
                        seen[bank] += 1
                        x = Item(bank, uses0[bank] + seen[bank])
                        x.step_done, x.step_free = per, shares[bank]
                        return x

                    for n, u in enumerate(loop_units(lambda r, j: block_loads("c_w_qkv", 0, r * 3072 + j * 256), 12, (0, C_GROUPS), per)):
                        pe.wait_ge(lo_ready, g * 12 + (u.index + 1))
                        w = parts(u, 256)
                        if n < 8:
                            x = take(n % 2)
                            x.pre = n % 2
                            close(tiles(halves(x.bank), w, (0, P), h, gate=gate if n == 0 else None), x, u)
                            xs.append(x)
                        else:
                            v = take(4 + n % 2)
                            for tt in range(NT):
                                mm = token_major(halves(v.bank)[tt], w, slice(0, 256), tt)
                            close(mm, v, u)
                            vs.append(v)
                        if pending is not None:
                            r = take(2 + (n - 1) % 2)
                            rotation(r, pending, 0, i=g)
                            r.step_done = per
                            rr.append(r)
                        pending = x if n < 8 else None
                        us.append(u)
                assert n_done[0] == done0 + per and seen == shares
                n_done[0] = done0 + per * C_GROUPS
                total[0] += 12 * C_GROUPS
                for b, n in shares.items():
                    uses[b] += n * C_GROUPS
                items[i, "qk"], items[i, "rot"], items[i, "v"], items[i, "units"] = xs, rr, vs, us
                pe.wait_ge(rot_ready, count(rot_ready, 8 * C_GROUPS))
                for b in (4, 5):
                    pe.wait_ge(bank_free[b], uses[b])

                def scores(hd):
                    a = HD * (hd % 2)
                    out = []
                    for tt in range(NT):
                        q0, q1 = tt * P, (tt + 1) * P
                        out.append([(0, T, qT[a:a + HD, hd // 2, q0:q1], kT[a:a + HD, hd // 2, :])]
                                   + [(g * P + P, g * P + 2 * P, qT[a:a + HD, 8 * g + hd // 2, q0:q1],
                                       kT[a:a + HD, 8 * g + hd // 2, q0:q1]) for g in (1, 2)])
                    return out

                attn_64(i, C_HEADS, scores, c_pv, c_plan,
                        lambda hd, g, kt: vC[:, kt, g * 1024 + hd * HD:g * 1024 + (hd + 1) * HD])
                wo("c_w_o", 0, (i, "wo"), 0, items[i, "O"])

            def ln(tag, source):
                at = 0 if source and source[0].bank else 4
                if source:
                    m = sums(at, xT, lambda j: pe.wait_ge(bank_free[source[j].bank], source[j].free))
                else:
                    m = sums(at, xT, lambda j: pe.wait_ge(y_ready, 2 * j + 2))
                v = sums(at + 1, sq, lambda j: pe.wait_ge(squares_ready, count(squares_ready)))
                count(ln_ready, KT)
                items[tag] = m, v

            def mix(l):
                gate = count(h_ready, KT) - KT
                it, us = {}, []

                def pair(loads, bank, first=False, cols=(0, P)):
                    u = next_unit(loads)
                    x = open_item(bank)
                    close(tiles(halves(bank)[:len(cols)], parts(u, 256), cols, h, gate=gate if first else None), x, u)
                    us.append(u)
                    return x

                wz = rows_of("w_in_2", l)

                def twice(col, width):
                    return [(lambda s, z=z: view(256)(s)[:, :, width * z:width * (z + 1)], wz[:, :, col:col + width])
                            for z in range(2)]

                it["pool"] = pair(block_loads("w_in_2", l, Z_POOL), 0, first=True)
                it["conv_a"] = pair(block_loads("w_in_2", l, Z_CONV), 1)
                it["conv_g"] = pair(block_loads("w_in_2", l, Z_CONV + 256), 2)
                xs, rr = [], []
                plan = [(twice(Z_KI, HD), (0,)), (block_loads("w_in_2", l, Z_QI), (0, P)),
                        (block_loads("w_in_2", l, Z_QI + 256), (0, P)), (twice(Z_K, 2 * HD), (0, HD)),
                        (block_loads("w_in_2", l, Z_Q), (0, P)), (block_loads("w_in_2", l, Z_Q + 256), (0, P))]
                for n, (loads, cols) in enumerate(plan):
                    x = pair(loads, (3, 0, 1)[n % 3], cols=cols)
                    x.pre = n % 3
                    xs.append(x)
                    if n:
                        r = open_item(4 + (n - 1) % 2)
                        rotation(r, xs[n - 1], 2, n=T if n == 1 else 2 * T)
                        rr.append(r)
                u = next_unit([(lambda s: view(256)(s)[:, :, 0:P], wz[:, :, Z_V:Z_V + P]),
                               (lambda s: view(256)(s)[:, :, P:P + 8], wz[:, :, Z_WI:Z_WI + 8])])
                v = open_item(2)
                for tt in range(NT):
                    o = banks[2][:, tt * 136:(tt + 1) * 136]
                    token_major(o, parts(u, 256), slice(0, 136), tt, last=False)
                    mm = nc.tensor.matmul(o, ones[0:1, :], brow[0:1, l, :], start=False, stop=True, skip_group_check=True)
                close(mm, v, u)
                us.append(u)
                it["v"] = v
                r = open_item(5)
                rotation(r, xs[5], 2)
                rr.append(r)
                it["qk"], it["rot"], it["units"] = xs, rr, us
                pe.wait_ge(rot_ready, count(rot_ready, 3))
                it["idx"] = []
                for hd in range(IDX_HEADS):
                    s = open_item([0, 2, 3, 6][hd % 4])
                    a = HD * (hd % 2)
                    for tt in range(NT):
                        mm = nc.tensor.matmul(banks[s.bank][:, tt * T:(tt + 1) * T],
                                              qiT[a:a + HD, hd // 2, tt * P:(tt + 1) * P], kidT[a:a + HD, :],
                                              start=True, stop=True)
                    close(mm, s)
                    it["idx"].append(s)
                done0, uses0 = n_done[0], list(uses)
                body, rounds = [], 4
                with pe.Fori(0, rounds) as i:
                    for j, u in enumerate(loop_units(lambda r, j: block_loads("w_in_2", l, r * 768 + (Z_GATE + j * 256)), 3, (0, rounds), 3)):
                        pe.wait_ge(lo_ready, i * 3 + (u.index + 1))
                        b = (1, 4, 5)[j]
                        pe.wait_ge(bank_free[b], i + uses0[b])
                        x = Item(b, uses0[b] + 1)
                        x.step_done, x.step_free = 3, 1
                        close(tiles(halves(b), parts(u, 256), (0, P), h), x, u)
                        body.append((u, x))
                n_done[0] = done0 + 3 * rounds
                total[0] += 3 * rounds
                for b in (1, 4, 5):
                    uses[b] += rounds
                it["gates"] = body
                pe.wait_ge(mixed_ready, count(mixed_ready))
                if l == 0:
                    pe.wait_ge(poolw_landed, 16 * 4 * DEPTH_2)
                x = open_item(7)
                for m in range(2):
                    mm = nc.tensor.matmul(halves(7)[m], poolw[:, l, m, :], mixed[:, m, :], start=True, stop=True)
                close(mm, x)
                it["poolmix"] = x
                pe.wait_ge(conv_step, count(conv_step, 2 * CONV_W - 1))
                pe.wait_ge(conv_out, count(conv_out))
                s = open_item(6)
                close(stats(6, 0, conv_y, range(2)), s)
                pe.wait_ge(bank_free[6], s.free)
                m_ = open_item(5, released=False)
                close(spread(5, 0, 0), m_)
                pe.wait_ge(squares_ready, count(squares_ready))
                v = open_item(6)
                close(stats(6, 0, sq, range(2)), v)
                pe.wait_ge(rs_ready, count(rs_ready))
                b = open_item(7, released=False)
                close(spread(7, 0, 0), b)
                it["cln"] = s, m_, v, b
                pe.wait_ge(ln_ready, count(ln_ready, 2))
                tag = ("m", l)
                pe.wait_ge(rot_ready, count(rot_ready, 3))
                attn_64(tag, N_HEADS,
                        lambda hd: [[(tt * T, (tt + 1) * T, qD[HD * (hd % 2):HD * (hd % 2) + HD, hd // 2, tt * P:(tt + 1) * P],
                                      kdT[HD * (hd % 2):HD * (hd % 2) + HD, (hd + hd // 4) % 2, :]) for tt in range(NT)]],
                        plain_pv, plain, lambda hd, kt: vD[:, kt, (hd // 4) * HD:(hd // 4 + 1) * HD])
                ready0 = count(branch_ready, 2) - 2

                def flat(*xs):
                    return [x[:].rearrange("p m n -> p (m n)") for x in xs]

                deep("w_pool_out_2", l, 1, flat(pool_hi, pool_lo), (tag, "pool"), 0,
                     lambda n, i: pe.wait_ge(branch_ready, ready0 + 1))
                deep("w_conv_out_2", l, 1, flat(conv_hi, conv_lo), (tag, "conv"), 4,
                     lambda n, i: pe.wait_ge(branch_ready, ready0 + 2))
                O = items[tag, "O"]
                deep("w_attn_out_2", l, 2, flat(attn_hi, attn_lo), (tag, "attn"), 0,
                     lambda n, i: pe.wait_ge(bank_free[O[n].bank], O[n].free))
                wo("w_o_2", l, (tag, "wo"), 4)
                items["m", l] = it

            def end():
                out = []
                for g in range(2):
                    if stages > DEPTH:
                        pe.wait_ge(y_ready, KT * (2 * min(stages - DEPTH, DEPTH_2) + 1) + 4 * g + 4)
                    else:
                        for x in items[last_add[0]]:
                            pe.wait_ge(bank_free[x.bank], x.free)
                    for tt in range(NT):
                        x = open_item(2 * tt + g)
                        for kk in range(4):
                            mm = nc.tensor.transpose(banks[x.bank][:, kk * P:(kk + 1) * P],
                                                     xT[:, 4 * g + kk, tt * P:(tt + 1) * P], ident[:])
                        close(mm, x)
                        out.append(x)
                items["end"] = out

            last_add = [None]
            for kind, arg in phases():
                if kind == "start":
                    start()
                elif kind == "rms":
                    norm[0] = arg
                elif kind == "A":
                    attn_a(arg)
                elif kind == "B":
                    attn_b(arg)
                elif kind == "C":
                    attn_c(arg)
                elif kind == "ffn":
                    ffn("f_w_gu", "f_w_out", arg, ("ffn", arg))
                    last_add[0] = (("ffn", arg), "down")
                elif kind == "rows2":
                    rows2()
                elif kind == "final":
                    final()
                elif kind in ("ln", "ln_last"):
                    ln(arg, None if arg[0] == "ln_in_g_2" else items[last_add[0]])
                elif kind == "mix":
                    mix(arg)
                    last_add[0] = (("m", arg), "wo")
                elif kind == "ffn2":
                    ffn("w_up_2", "w_down_2", arg, ("ffn2", arg))
                    last_add[0] = (("ffn2", arg), "down")
                elif kind == "end":
                    end()

        @block.sync
        def _(sp):
            sp.dma_start(xrows, t["x"][0].rearrange("(t p) n -> p t n", p=P)).then_inc(x_landed, 16)

            def load(u, loads):
                for dst, src in loads:
                    sp.dma_start(dst(raw[u.slot]), src).then_inc(landed[u.slot], 16)

            n = 0
            while n < len(units):
                u = units[n]
                if n == 1:
                    sp.wait_ge(rows_landed, 16 * len(row_loads(0)))
                    for dst, name in ((tab, "c_tab"), (rotm, "c_rotm"), (invf, "c_invf")):
                        sp.dma_start(dst[:], t[name]).then_inc(consts_landed, 16)
                    for v, name in enumerate(("a_lambda_q1", "a_lambda_k1", "a_lambda_q2", "a_lambda_k2")):
                        for l in range(2):
                            sp.dma_start(lamv[:, 2 * v + l, :], t[name][l:l + 1, :].to_broadcast([P, HD])).then_inc(lam_landed, 16)
                if n == 2:
                    for (a, b, col) in ((0, P, Z_V), (P, P + 8, Z_WI)):
                        sp.dma_start(brow[0:1, :, a:b], t["b_in_2"][:, col:col + b - a].unsqueeze(0)).then_inc(consts_landed, 16)
                if not u.span:
                    if u.index >= SLOTS:
                        sp.wait_ge(lo_ready, u.index + 1 - SLOTS)
                    load(u, u.loads)
                    n += 1
                    continue
                body = units[n:n + u.span]
                first, last = u.rounds
                with sp.Fori(first, last) as i:
                    for b in body:
                        sp.wait_ge(lo_ready, i * b.span + (b.index + 1 - SLOTS))
                        load(b, b.loads(i))
                n += len(body)
            out = t["out"][0].rearrange("(t p) n -> p t n", p=P)
            for g in range(2):
                for x in items["end"][2 * g:2 * g + 2]:
                    sp.wait_ge(bank_free[x.bank], x.free)
                sp.dma_start(out[:, :, 512 * g:512 * (g + 1)], xrows[:, :, 512 * g:512 * (g + 1)]).then_inc(out_stored, 16)
            sp.wait_ge(out_stored, 32)

        @block.gpsimd
        def _(pool):
            gp = nc.gpsimd
            gp.memset(ones[:], 1.0).then_inc(ident_ready, 1)
            gp.memset(ident[:], 0.0).then_inc(ident_ready, 1)
            pool.wait_ge(ident_ready, 2)
            gp.affine_select(out=ident[:], in_=ident[:], compare_op=ALU.not_equal, fill=1.0, base=0,
                             pattern=[[-1, P]], channel_multiplier=1).then_inc(ident_ready, 1)
            for n in range(3):
                gp.memset(idle[:, n:n + 1], 0.0).then_inc(hidden_ready, 1)
            seen_m, seen_b, tiles_before = 0, 0, 0

            def split_hidden():
                def step(j, at, n, i=None):
                    k = tiles_before + n + 1
                    pool.wait_ge(product_ready, k if i is None else i * 3 + k)
                    gp.tensor_copy(hid_hi[:, at], hT[:, j, :]).then_inc(hid_step, 1)
                    pool.wait_ge(hid_step, k if i is None else i * 3 + k)
                    gp.tensor_tensor(hid_lo[:, at], hT[:, j, :], hid_hi[:, at].bitcast(F32),
                                     ALU.subtract).then_inc(hidden_ready, 1)

                for j in range(3):
                    step(j, slice(j * T, (j + 1) * T), j)
                with pool.Fori(1, 7) as i:
                    for j in range(3):
                        step(j, bass.ds(i * (3 * T) + j * T, T), j, i)
                step(0, slice(21 * T, 22 * T), 21)

            for kind, arg in phases():
                if kind == "B":
                    seen_b += 1
                    pool.wait_ge(kr_ready, seen_b)
                    gp.tensor_copy(kT[64:96, 0:B_HEADS, :],
                                   kr[64:96, :].unsqueeze(1).to_broadcast([32, B_HEADS, T])).then_inc(kr_spread, 1)
                if kind == "second":
                    pool.wait_ge(area_free, 1)
                    gp.memset(poolw[:], 0.0).then_inc(poolw_zeroed, 1)
                    pool.dma_start(inv_cnt, t["c_inv_cnt"]).then_inc(consts2_landed, 16)
                    for dst, src in row_loads(1):
                        pool.dma_start(dst, src).then_inc(rows2_landed, 16)
                    pool.wait_ge(poolw_zeroed, 1)
                    for l in range(DEPTH_2):
                        for g in range(4):
                            a = HD * (g % 2)
                            pool.dma_start(poolw[a:a + HD, l, g // 2, a:a + HD], t["pool_w_2"][l, g]).then_inc(poolw_landed, 16)
                if kind in ("ffn", "ffn2"):
                    split_hidden()
                    tiles_before += FT
                if kind == "mix":
                    l = arg
                    gp.memset(conv_h[:, :, 0:PADW], 0.0)
                    x = items["m", l]["conv_g"]
                    pool.wait_ge(bank_free[x.bank], x.free)
                    gp.tensor_tensor(conv_h[:, :, PADW:], conv_a[:], conv_y[:], ALU.mult).then_inc(glu_ready, 1)
                    pool.wait_ge(glu_ready, l + 1)
                    cw, cb = ROW["conv_dw_w_2"] + l * CONV_W * 2, ROW["conv_dw_b_2"] + 2 * l
                    for j in range(CONV_W):
                        hh = conv_h[:, 0, PADW - CONV_W + 1 + j:PADW - CONV_W + 1 + j + T]
                        wj = pcol[:, cw + 2 * j:cw + 2 * j + 1]
                        done = l * (2 * CONV_W - 1) + 2 * j
                        if j == 0:
                            gp.tensor_scalar(conv_y[:, 0, :], hh, wj, pcol[:, cb:cb + 1], ALU.mult, ALU.add).then_inc(conv_step, 1)
                        else:
                            gp.tensor_scalar(hT[:, 2 + j % 2, :], hh, wj, None, ALU.mult).then_inc(conv_step, 1)
                            pool.wait_ge(conv_step, done)
                            gp.tensor_tensor(conv_y[:, 0, :], conv_y[:, 0, :], hT[:, 2 + j % 2, :], ALU.add).then_inc(conv_step, 1)
                    for tt in range(NT):
                        pool.wait_ge(score_step, IDX_HEADS * NT * seen_m + NT * (IDX_HEADS - 1) + tt + 1)
                        gp.affine_select(out=score[:, tt, :], in_=score[:, tt, :], compare_op=ALU.is_ge,
                                         fill=FILL, base=tt * P, pattern=[[-1, T]],
                                         channel_multiplier=1).then_inc(score_masked, 1)
                    for tt in range(NT):
                        pool.wait_ge(picked, NT * seen_m + tt + 1)
                        gp.affine_select(out=work[:, tt, :], in_=work[:, tt, :], compare_op=ALU.is_ge,
                                         fill=NEG, base=tt * P, pattern=[[-1, T]],
                                         channel_multiplier=1).then_inc(keep_ready, 1)
                    seen_m += 1

        @block.scalar
        def _(act):
            tally = {}
            fn = nc.scalar.activation

            def count(s, n=1):
                tally[s.name] = tally.get(s.name, 0) + n
                return tally[s.name]

            def done(x, i=None):
                act.wait_ge(pe_done, x.done if i is None else i * x.step_done + x.done)

            def freed(x):
                act.wait_ge(bank_free[x.bank], x.free)

            def free(ins, x):
                ins.then_inc(bank_free[x.bank], 1)

            def round_unit(slot, nth, i=None, step=0):
                act.wait_ge(landed[slot], 32 * nth if i is None else i * (32 * step) + 32 * nth)
                nc.scalar.copy(w_hi[slot][:], raw[slot][:]).then_inc(hi_ready, 1)

            def refill(u, i=None):
                if i is None and u.index + SLOTS >= total[0]:
                    return
                done(u, i)
                round_unit(u.slot, u.index // SLOTS + 2, i, u.span // SLOTS)

            late = []

            def refills(tag, hold=False):
                head, loop, tail = items[tag, "units"]
                if hold:
                    late.append((tail or head)[-1])
                    head, tail = (head, tail[:-1]) if tail else (head[:-1], tail)
                for u in head:
                    refill(u)
                if loop and loop[-1].at(2).index + SLOTS < total[0]:
                    with act.Fori(1, 3) as i:
                        for u in loop:
                            refill(u, i)
                elif loop:
                    for u in [u.at(i) for i in (1, 2) for u in loop]:
                        refill(u)
                for u in tail:
                    refill(u)

            for dst, src in row_loads(0):
                act.dma_start(dst, src).then_inc(rows_landed, 16)
            round_unit(0, 1)
            def second():
                act.wait_ge(angles_ready, 2)
                fn(tabd[:, 1, :], red, ACT.Sin)
                fn(tabd[:, 0, :], scr, ACT.Sin, scale=-1.0, bias=eps[:, 2:3]).then_inc(sines_ready, 1)

            def rms(source, at, ordered):
                freed(items["start"][1])
                for j, x in enumerate(source):
                    freed(x)
                    for k in (2 * j, 2 * j + 1):
                        fn(ordered(h_hi[:, k, :], False), ordered(xT[:, k, :], True), ACT.Identity,
                           scale=pcol[:, at + k:at + k + 1], bias=eps[:, 3:4]).then_inc(hi_part, 1)
                for j in range(4):
                    s = slice(2 * j, 2 * j + 2)
                    fn(ordered(sq[:, s, :], False), ordered(xT[:, s, :], True), ACT.Square).then_inc(squares_ready, 1)
                if late:
                    refill(late.pop())
                else:
                    round_unit(1, 1)
                    round_unit(2, 1)

            def norm_deviation():
                deviation(items[norm[0]][0], ((0, 2, D),))

            def whole_deviation(x, n, e, out):
                done(x)
                free(fn(out, banks[x.bank][:, 0:T], ACT.Sqrt, scale=1.0 / n, bias=eps[:, e:e + 1]), x)

            def deviation(s, spans, e=0):
                done(s)
                for a, b, n in spans:
                    ins = fn(std[:, a:b], banks[s.bank][:, a:b], ACT.Sqrt, scale=1.0 / n, bias=eps[:, e:e + 1])
                free(ins, s)

            norm = [None]

            def round_parts(n, width, scaled=None):
                for k in range(n):
                    if scaled:
                        freed(scaled[k])
                    else:
                        act.wait_ge(to_split, count(to_split))
                    s = slice(width * k, width * (k + 1))
                    nc.scalar.copy(h_hi[:, s, :], hT[:, s, :]).then_inc(hi_part, 1)

            def pair_of(x):
                return banks[x.bank][:].rearrange("p (m n) -> p m n", m=2)

            def attn_a(i):
                us, xs, rr, vs = items[i, "units"], items[i, "qk"], items[i, "rot"], items[i, "v"]
                for n, u in enumerate(us):
                    if n < 8:
                        x = xs[n]
                        done(x)
                        if n >= 3:
                            freed(rr[n - 3])
                        free(fn(pre[x.pre][:], banks[x.bank][:], ACT.Copy, scale=HD ** -0.5 if n < 4 else 1.0), x)
                        if n == 0:
                            norm_deviation()
                    else:
                        v = vs[n - 8]
                        if n == 8:
                            act.wait_ge(rs_ready, count(rs_ready))
                        done(v)
                        for tt in range(NT):
                            ins = fn(vA[:, tt, (n - 8) * 256:(n - 7) * 256], pair_of(v)[:, tt, :], ACT.Identity,
                                     scale=rs[:, tt:tt + 1], bias=eps[:, 3:4])
                        free(ins, v)
                    refill(u)
                S, TT, O = items[i, "S"], items[i, "T"], items[i, "O"]
                for hd in range(A_HEADS + 4):
                    if hd < A_HEADS:
                        if hd >= 3:
                            done(TT[hd - 3][0])
                        for sub in range(2):
                            n = 2 * hd + sub
                            act.wait_ge(negmax_ready, count(negmax_ready))
                            for tt in range(NT):
                                ins = fn(expoA[hd % 3][:, 512 * sub + tt * T:512 * sub + (tt + 1) * T],
                                         banks[S[n].bank][:, tt * T:(tt + 1) * T], ACT.Exp,
                                         bias=negmax[n % 4][:, tt:tt + 1], accum_out=esum[n % 4][:, tt:tt + 1])
                            free(ins, S[n])
                    if hd >= 4 and hd % 2 == 1:
                        g = (hd - 4) // 2
                        done(O[g])
                        fn(sq[:, 2 * g:2 * g + 2, :], pair_of(O[g]), ACT.Square).then_inc(squares_ready, 1)
                        free(nc.scalar.copy(oT[:, 2 * g:2 * g + 2, :], pair_of(O[g])), O[g])
                    if 2 <= hd < A_HEADS + 2:
                        probs_t(hd - 2, TT)
                deviation(items[i, "subln"][0], ((0, 16, P),))
                count(rs_ready)
                round_parts(4, 2, items[i, "subln"][1])
                refills((i, "wo"), True)

            def probs_t(hd, TT):
                if hd >= 2:
                    act.wait_ge(pe_done, TT[hd - 2][-1].used)
                for g, it in enumerate(TT[hd]):
                    done(it)
                    free(nc.scalar.copy(expoT[hd % 2][:, 512 * g:512 * (g + 1)], banks[it.bank][:]), it)

            def attn_64(tag, heads, masked, dst=None, natural=lambda x: x):
                S, TT, O = items[tag, "S"], items[tag, "T"], items[tag, "O"]
                w = T * len(TT[0])
                for hd in range(heads + 4):
                    if hd < heads:
                        act.wait_ge(negmax_ready, count(negmax_ready))
                        if not masked and hd >= 3:
                            for it in TT[hd - 3]:
                                done(it)
                        for tt in range(NT):
                            e = expo[hd % 3][:, w * tt:w * (tt + 1)]
                            ins = fn(e, e if masked else banks[S[hd][0].bank][:, tt * T:(tt + 1) * T], ACT.Exp,
                                     bias=negmax[hd % 4][:, tt:tt + 1], accum_out=esum[hd % 4][:, tt:tt + 1])
                        if masked:
                            ins.then_inc(exp_ready, 1)
                        else:
                            free(ins, S[hd][0])
                    if hd >= 4 and hd % 4 == 3:
                        g = (hd - 4) // 4
                        done(O[g])
                        out = natural((dst or h_hi)[:, 2 * g:2 * g + 2, :])
                        nc.scalar.copy(out, like(pair_of(O[g]), out)).then_inc(hi_part, 1)
                    if 2 <= hd < heads + 2:
                        probs_t(hd - 2, TT)

            def like(b, out):
                return b if len(out.shape) == 3 else b.rearrange("p m (c u) -> p m c u", c=4)

            def attn_b(i):
                us, raw_items = items[i, "units"], items[i, "raw"]
                norm_deviation()
                refill(us[0])
                for n, (a, b) in enumerate(((0, 2), (2, 4), (4, 5))):
                    freed(raw_items[n])
                    fn(sq[:, a:b, :], latT[:, a:b, :], ACT.Square).then_inc(squares_ready, 1)
                    if n == 1:
                        refill(us[1])
                deviation(items[i, "stat"][0], ((0, 2, B_QR), (2, 4, B_KVR)))
                count(rs_ready, 2)
                round_parts(5, 1)
                refill(us[2])
                for n, x in enumerate(items[i, "qk"]):
                    done(x)
                    if n == 2:
                        freed(items[i, "krot"])
                    if n >= 3:
                        freed(items[i, "rot"][n - 3])
                    free(fn(pre[x.pre][0:96, :], banks[x.bank][0:96, :], ACT.Copy,
                            scale=float(np.float32((B_NOPE + B_ROPE) ** -0.5))), x)
                    if n % 2:
                        refill(us[3 + n // 2])
                for half in range(2):
                    for n in range(4 * half, 4 * half + 4):
                        x = items[i, "k"][n]
                        done(x)
                        free(nc.scalar.copy(kT[0:HD, 2 * n:2 * n + 2, :],
                                            banks[x.bank][0:HD, :].rearrange("p (m n) -> p m n", m=2)), x)
                    for tt in range(NT):
                        v = items[i, "v"][2 * half + tt]
                        done(v)
                        free(nc.scalar.copy(vA[:, tt, half * 512:(half + 1) * 512], banks[v.bank][:]), v)
                    refill(us[7 + half])
                attn_64(i, B_HEADS, False)
                refills((i, "wo"), True)

            def attn_c(i):
                us, xs, rr, vs = items[i, "units"], items[i, "qk"], items[i, "rot"], items[i, "v"]
                norm_deviation()
                act.wait_ge(rs_ready, count(rs_ready))
                with act.Fori(0, C_GROUPS) as g:
                    for n, u in enumerate(us):
                        if n < 8:
                            x, r = xs[n], rr[(n - 2) % 8]
                            done(x, g)
                            act.wait_ge(bank_free[r.bank], g * r.step_free + (r.free if n >= 2 else r.free - r.step_free))
                            free(fn(pre[x.pre][:], banks[x.bank][:], ACT.Copy, scale=HD ** -0.5 if n < 4 else 1.0), x)
                        else:
                            v = vs[n - 8]
                            done(v, g)
                            for tt in range(NT):
                                ins = fn(vC[:, tt, bass.ds(g * 1024 + (n - 8) * 256, 256)], pair_of(v)[:, tt, :],
                                         ACT.Identity, scale=rs[:, tt:tt + 1], bias=eps[:, 3:4])
                            free(ins, v)
                        refill(u, g)
                act.wait_ge(rot_ready, ROTATED_BEFORE_C + 8 * C_GROUPS)
                act.dma_start(cmask, t["c_cmask"]).then_inc(cmask_landed, 16)
                act.dma_start(pos_i, t["positions_2"].to_broadcast([P, T])).then_inc(pos_landed, 16)
                attn_64(i, C_HEADS, True, natural=lambda x: x.rearrange("p m (u c) -> p m c u", c=4))
                refills((i, "wo"), True)

            def ffn(tag, before):
                head, body, tail = items[tag, "up"]

                def step(j, n, u, x, i=None):
                    refill(u, i)
                    act.wait_ge(bank_free[x.bank], x.free if i is None else i + x.free)
                    fn(pre[j][:, 0:T], pre[j][:, 0:T], ACT.Silu).then_inc(gate_ready, 1)

                norm_deviation()
                count(rs_ready)

                for j, (u, x) in enumerate(head):
                    step(j, j, u, x)
                with act.Fori(1, 7) as i:
                    for j, (u, x) in enumerate(body):
                        step(j, j, u, x, i)
                for u, x in tail:
                    step(0, FT - 1, u, x)
                refills((tag, "down"), True)

            def ln(tag, last):
                m, v = items[tag]
                fn(tiny[:], eps[:, 0:1], ACT.Sqrt)
                for j in range(4):
                    if j < 3:
                        act.wait_ge(centred, count(centred))
                    else:
                        freed(m)
                    fn(sq[:, 2 * j:2 * j + 2, :], xT[:, 2 * j:2 * j + 2, :], ACT.Square).then_inc(squares_ready, 1)
                whole_deviation(v, D, 1, sq[:, 0, :])
                at, ready = ROW[tag[1]] + tag[2], count(ln_ready, KT) - KT

                def offset(dst, k):
                    act.wait_ge(ln_ready, ready + k + 1)
                    return fn(dst[:, k, :], hT[:, k, :], ACT.Identity, bias=pcol[:, at + k:at + k + 1])

                if not last:
                    for k in range(KT):
                        offset(h_hi, k).then_inc(hi_part, 1)
                for k in range(KT):
                    offset(xT, k).then_inc(y_ready, 1)
                if late:
                    refill(late.pop())

            def mix(l):
                it = items["m", l]
                us = iter(it["units"])
                b0 = ROW["b_in", l]

                def offset(dst, x, row, tiles=2, func=ACT.Identity):
                    done(x)
                    for m in range(tiles):
                        ins = fn(dst(m), banks[x.bank][:, m * T:(m + 1) * T], func, bias=pcol[:, b0 + row + m:b0 + row + m + 1])
                    free(ins, x)
                    refill(next(us))

                offset(lambda m: pool_u[:, m, PADW:], it["pool"], B_POOL)
                offset(lambda m: conv_a[:, m, :], it["conv_a"], B_CONV)
                offset(lambda m: conv_y[:, m, :], it["conv_g"], B_CONV + 2, func=ACT.Sigmoid)
                for n, (x, row) in enumerate(zip(it["qk"], (B_KI, B_QI, B_QI + 2, B_K, B_Q, B_Q + 2))):
                    if n >= 3:
                        freed(it["rot"][n - 3])
                    offset(lambda m: pre[x.pre][:, m * T:(m + 1) * T], x, row, tiles=2 if n else 1)
                v = it["v"]
                done(v)
                b = banks[v.bank][:, 0:272].rearrange("p (t n) -> p t n", t=NT)
                nc.scalar.copy(vD[:], b[:, :, 0:128])
                free(nc.scalar.mul(wi[:], b[:, :, 128:136], float(np.float32(IDX_HEADS ** -0.5))), v)
                refill(next(us))
                for n, s in enumerate(it["idx"]):
                    done(s)
                    if n >= 2:
                        act.wait_ge(score_step, NT * IDX_HEADS * l + 2 * (n - 1))
                    free(fn(relu[n % 2], banks[s.bank][:], ACT.Relu, scale=HD ** -0.5), s)
                with act.Fori(0, 4) as i:
                    for n, (u, x) in enumerate(it["gates"]):
                        done(x, i)
                        for m in range(2):
                            ins = fn(gates[:, bass.ds(i * 6 + (2 * n + m), 1), :], banks[x.bank][:, m * T:(m + 1) * T].unsqueeze(1),
                                     ACT.Sigmoid, bias=pcol[:, bass.ds(i * 6 + (b0 + B_GATE + 2 * n + m), 1)])
                        free(ins, x)
                        refill(u, i)
                s, m_, v, b = it["cln"]
                act.wait_ge(centred, count(centred))
                fn(sq[:, 0:2, :], conv_y[:], ACT.Square).then_inc(squares_ready, 1)
                deviation(v, ((0, 2, 256),), 1)
                at = ROW["conv_ln_b_2"] + 2 * l
                for m in range(2):
                    act.wait_ge(ln_ready, count(ln_ready))
                    ins = fn(conv_y[:, m, :], conv_y[:, m, :], ACT.Silu, bias=pcol[:, at + m:at + m + 1])
                ins.then_inc(act_step, 1)
                act.wait_ge(act_step, l + 1)
                nc.scalar.copy(conv_hi[:], conv_y[:]).then_inc(hi_part, 1)
                tag = ("m", l)
                attn_64(tag, N_HEADS, True, dst=attn_hi)
                for branch in ("pool", "conv", "attn"):
                    refills((tag, branch), branch == "attn")
                round_parts(4, 2)
                refill(late.pop())
                refills((tag, "wo"), True)

            def ffn2(tag, l, before):
                head, body, tail = items[tag, "up"]
                w, b = ROW["ffn_dw_w_2"] + l * FCW * 44 + 2 * 44, ROW["ffn_dw_b_2"] + l * 44

                def step(n, j, u, x, i=None):
                    def col(at):
                        return pcol[:, at:at + 1] if i is None else pcol[:, bass.ds(i * 3 + at, 1)]

                    k = before + n + 1
                    act.wait_ge(hidden_ready, k if i is None else i * 3 + k)
                    done(x, i)
                    for m, tile in ((0, 0), (1, 22)):
                        ins = fn(pre[j][:, m * T:(m + 1) * T], banks[x.bank][:, m * T:(m + 1) * T], ACT.Identity,
                                 scale=col(w + tile + n), bias=col(b + tile + n))
                    ins.then_inc(taps_started, 1)
                    refill(u, i)
                    act.wait_ge(bank_free[x.bank], x.free if i is None else i + x.free)
                    fn(pre[j][:, 0:T], pre[j][:, 0:T], ACT.Silu).then_inc(gate_ready, 1)

                for j, (u, x) in enumerate(head):
                    step(j, j, u, x)
                with act.Fori(1, 7) as i:
                    for j, (u, x) in enumerate(body):
                        step(j, j, u, x, i)
                for u, x in tail:
                    step(FT - 1, 0, u, x)
                refills((tag, "down"), True)

            source = [items["start"][0]]
            n_ffn = 0
            for kind, arg in phases():
                if kind == "lambda":
                    act.wait_ge(lam_sums, 1)
                    fn(lame[:], lams[:], ACT.Exp).then_inc(lam_exps, 1)
                elif kind == "second":
                    second()
                elif kind == "rms":
                    c = arg[1] == "attn_norm" and arg[0] % 3 == 2
                    rms(source[0], ROW[arg[1]] + arg[2], by_class if c else lambda x, natural: x)
                    norm[0] = arg
                elif kind in "ABC":
                    (attn_a if kind == "A" else attn_b if kind == "B" else attn_c)(arg)
                    source[0] = items[arg, "wo"]
                elif kind == "ffn":
                    ffn(("ffn", arg), FT * n_ffn)
                    n_ffn += 1
                    source[0] = items[("ffn", arg), "down"]
                elif kind == "final":
                    for j, x in enumerate(source[0]):
                        freed(x)
                        fn(sq[:, 2 * j:2 * j + 2, :], xT[:, 2 * j:2 * j + 2, :], ACT.Square).then_inc(squares_ready, 1)
                    refill(late.pop())
                    whole_deviation(items["final"][0], D, 0, hT[:, 6, :])
                elif kind in ("ln", "ln_last"):
                    ln(arg, kind == "ln_last")
                elif kind == "mix":
                    mix(arg)
                elif kind == "ffn2":
                    ffn2(("ffn2", arg), arg, FT * n_ffn)
                    n_ffn += 1

        @block.vector
        def _(dve):
            v_ = nc.vector
            tally = {}
            steps = [0]
            source = [None, None]

            def count(s, n=1):
                tally[s.name] = tally.get(s.name, 0) + n
                return tally[s.name]

            def done(x, i=None):
                dve.wait_ge(pe_done, x.done if i is None else i * x.step_done + x.done)

            def freed(x, i=None):
                dve.wait_ge(bank_free[x.bank], x.free if i is None else i * x.step_free + x.free)

            def free(ins, x):
                ins.then_inc(bank_free[x.bank], 1)

            def link(ins, behind=0):
                steps[0] += 1
                ins.then_inc(dve_step, 1)
                if steps[0] > behind:
                    dve.wait_ge(dve_step, steps[0] - behind)

            def rest(slot, nth, i=None, step=0):
                dve.wait_ge(hi_ready, nth if i is None else i * step + nth)
                v_.tensor_tensor(w_lo[slot][:], raw[slot][:], w_hi[slot][:].bitcast(F32), ALU.subtract).then_inc(lo_ready, 1)

            def refill(u, i=None):
                if i is None and u.index + SLOTS >= total[0]:
                    return
                rest(u.slot, u.index + SLOTS + 1, i, u.span)

            late = []

            def refills(tag, hold=False):
                head, loop, tail = items[tag, "units"]
                if hold:
                    late.append((tail or head)[-1])
                    head, tail = (head, tail[:-1]) if tail else (head[:-1], tail)
                for u in head:
                    refill(u)
                if loop and loop[-1].at(2).index + SLOTS < total[0]:
                    with dve.Fori(1, 3) as i:
                        for u in loop:
                            refill(u, i)
                elif loop:
                    for u in [u.at(i) for i in (1, 2) for u in loop]:
                        refill(u)
                for u in tail:
                    refill(u)

            def start():
                v_.memset(eps[:, 0:1], EPS)
                v_.memset(eps[:, 1:2], LN_EPS)
                v_.memset(eps[:, 3:4], 0.0)
                link(v_.memset(eps[:, 2:3], math.pi / 2))
                xs, r = items["start"]
                for j, x in enumerate(xs):
                    done(x)
                    free(v_.tensor_copy(xT[:, 2 * j:2 * j + 2, :], banks[x.bank][:].rearrange("p (m n) -> p m n", m=2)), x)
                done(r)
                free(v_.tensor_copy(pcol[:, 0:P], banks[r.bank][:, 0:P]), r)
                freed(r)
                for b in (5, 6):
                    x = items["idle", b]
                    done(x)
                    free(v_.tensor_copy(rot[b - 5][:, 0:P], banks[b][:, 0:P]), x)
                rest(0, 1)

            def lambdas():
                dve.wait_ge(lam_landed, 16 * 8)
                for n in range(2):
                    ins = v_.tensor_tensor(lamp[:, 2 * n:2 * n + 2, :], lamv[:, 4 * n:4 * n + 2, :],
                                           lamv[:, 4 * n + 2:4 * n + 4, :], ALU.mult)
                link(ins)
                v_.tensor_reduce(lams[:], lamp[:], AX.X, ALU.add).then_inc(lam_sums, 1)
                dve.wait_ge(lam_exps, 1)
                link(v_.tensor_tensor(neglam[:], lame[:, 2:4], lame[:, 0:2], ALU.subtract))
                for l in range(2):
                    v_.tensor_scalar(neglam[:, l:l + 1], neglam[:, l:l + 1], -lambda_init(3 * l), None, ALU.add)
                    ins = v_.tensor_scalar(subg[:, l:l + 1], pcol[:, ROW["a_subln"] + l:ROW["a_subln"] + l + 1],
                                           1.0 - lambda_init(3 * l), None, ALU.mult)
                link(ins)
                dve.wait_ge(consts_landed, 16 * 3)

            def second():
                dve.wait_ge(consts_landed, 16 * 5)
                dve.wait_ge(pos_landed, 16)
                v_.tensor_copy(ang, pos_i).then_inc(area_free, 1)
                dve.wait_ge(area_free, 1)
                link(v_.tensor_scalar(ang, ang, invf[:, 0:1], None, ALU.mult))
                link(v_.tensor_scalar(turns, ang, 1.0 / (2 * math.pi), MAGIC, ALU.mult, ALU.add))
                link(v_.tensor_scalar(turns, turns, -MAGIC, None, ALU.add))
                for part in TWO_PI:
                    link(v_.scalar_tensor_tensor(ang, turns, -part, ang, ALU.mult, ALU.add))
                link(v_.tensor_scalar(red, ang, PI_IN, -PI_IN, ALU.min, ALU.max))
                v_.tensor_scalar(turns, red, -1.0, None, ALU.mult).then_inc(angles_ready, 1)
                dve.wait_ge(angles_ready, 1)
                v_.tensor_tensor(scr, turns, red, ALU.max).then_inc(angles_ready, 1)

            def rows2():
                dve.wait_ge(sines_ready, 1)
                dve.wait_ge(consts2_landed, 16)
                for n, x in enumerate(items["rows2"]):
                    done(x)
                    w = min(512, N_ROWS - P - 512 * n)
                    free(v_.tensor_copy(pcol[:, P + 512 * n:P + 512 * n + w], banks[x.bank][:, 0:w]), x)
                for x in items["rows2"]:
                    freed(x)

            def split_rest(n, width, k):
                dve.wait_ge(hi_part, count(hi_part))
                s = slice(width * k, width * (k + 1))
                v_.tensor_tensor(h_lo[:, s, :], hT[:, s, :], h_hi[:, s, :].bitcast(F32), ALU.subtract).then_inc(h_ready, 1)

            def add_pair(j):
                if source[0]:
                    x, xs = source[0][j], xT[:, 2 * j:2 * j + 2, :]
                    done(x)
                    b = banks[x.bank][:].rearrange("p (m n) -> p m n", m=2)
                    if source[1] is None:
                        free(v_.tensor_tensor(xs, xs, b, ALU.add), x)
                    else:
                        free(v_.scalar_tensor_tensor(xs, xs, source[1], b, ALU.mult, ALU.add), x)

            def rms(tag, at, kind):
                ordered = by_class if kind == "C" else lambda x, natural: x
                for j in range(5):
                    if j < 4:
                        add_pair(j)
                    if j:
                        for k in (2 * j - 2, 2 * j - 1):
                            dve.wait_ge(hi_part, count(hi_part))
                            v_.scalar_tensor_tensor(ordered(h_lo[:, k, :], False), ordered(xT[:, k, :], True),
                                                    pcol[:, at + k:at + k + 1], ordered(h_hi[:, k, :].bitcast(F32), False),
                                                    ALU.mult, ALU.subtract).then_inc(h_ready, 1)
                if late:
                    refill(late.pop())
                else:
                    rest(1, 2)
                    rest(2, 3)
                norm[0] = tag

            norm = [None]

            def deviations():
                freed(items[norm[0]][0])
                v_.reciprocal(rs[:, 0:2], std[:, 0:2]).then_inc(rs_ready, 1)

            def spread_out(dst, table=None):
                b = items[norm[0]][1]
                done(b)
                r = banks[b.bank][:, 0:T]
                if table is None:
                    free(v_.tensor_copy(dst, r), b)
                else:
                    free(v_.tensor_tensor(dst, table, r.unsqueeze(1).to_broadcast([P, 2, T]), ALU.mult), b)
                freed(b)

            def final():
                for j in range(4):
                    add_pair(j)
                if late:
                    refill(late.pop())
                x = items["final"][0]
                freed(x)
                link(v_.reciprocal(hT[:, 7, :], hT[:, 6, :]))
                at = ROW["final_norm"]
                for k in range(KT):
                    v_.scalar_tensor_tensor(xT[:, k, :], xT[:, k, :], pcol[:, at + k:at + k + 1], hT[:, 7, :],
                                            ALU.mult, ALU.mult).then_inc(y_ready, 1)

            def rotate(n, x, r, dst, cos, sin, i=None, lo=0, hi=P, tiles=2, ready=rot_ready):
                w = tiles * T
                done(r, i)
                shape = [hi - lo, tiles, T]

                def wide(tb):
                    return tb[lo:hi, :].unsqueeze(1).to_broadcast(shape)

                p3 = pre[x.pre][lo:hi, 0:w].rearrange("p (m n) -> p m n", m=tiles)
                r3 = rot[n % 2][lo:hi, 0:w].rearrange("p (m n) -> p m n", m=tiles)
                v_.tensor_tensor(dst, p3, wide(cos), ALU.mult)
                free(v_.tensor_tensor(r3, banks[r.bank][lo:hi, 0:w].rearrange("p (m n) -> p m n", m=tiles), wide(sin),
                                      ALU.mult), r)
                freed(r, i)
                v_.tensor_tensor(dst, dst, r3, ALU.add).then_inc(ready, 1)

            def attn_a(i):
                l = i // 3
                us, xs, rr = items[i, "units"], items[i, "qk"], items[i, "rot"]
                deviations()
                for n, u in enumerate(us):
                    refill(u)
                    if n == 1:
                        spread_out(hT[:, 0:2, :], tab[:, 0:2, :])
                    if 1 <= n <= 8:
                        rotate(n, xs[n - 1], rr[n - 1], qT[:, 2 * n - 2:2 * n, :], hT[:, 0, :], hT[:, 1, :])
                S = items[i, "S"]
                for hd in range(A_HEADS + 1):
                    if hd < A_HEADS:
                        for sub in range(2):
                            n = 2 * hd + sub
                            done(S[n])
                            v_.tensor_reduce(negmax[n % 4][:], banks[S[n].bank][:].rearrange("p (m n) -> p m n", m=2), AX.X,
                                             ALU.max, negate=True).then_inc(negmax_ready, 1)
                    if hd >= 1:
                        n = 2 * (hd - 1)
                        e = expoA[(hd - 1) % 3]
                        rec = [erec[(n + sub) % 4] for sub in range(2)]
                        for sub in range(2):
                            freed(S[n + sub])
                            link(v_.reciprocal(rec[sub][:], esum[(n + sub) % 4][:]))
                        link(v_.tensor_scalar(rec[1][:], rec[1][:], neglam[:, l:l + 1], None, ALU.mult))
                        for tt in range(NT):
                            e0 = e[:, tt * T:(tt + 1) * T]
                            ins = v_.tensor_scalar(e0, e0, rec[0][:, tt:tt + 1], None, ALU.mult)
                        link(ins)
                        for tt in range(NT):
                            e0, e1 = e[:, tt * T:(tt + 1) * T], e[:, 512 + tt * T:512 + (tt + 1) * T]
                            ins = v_.scalar_tensor_tensor(e0, e1, rec[1][:, tt:tt + 1], e0, ALU.mult, ALU.add)
                        ins.then_inc(probs_ready, 1)
                s, sp_items = items[i, "subln"]
                freed(s)
                v_.reciprocal(rs[:, 0:16], std[:, 0:16]).then_inc(rs_ready, 1)
                for g in range(5):
                    if g < 4:
                        b = sp_items[g]
                        done(b)
                        m = slice(2 * g, 2 * g + 2)
                        free(v_.scalar_tensor_tensor(hT[:, m, :], oT[:, m, :], subg[:, l:l + 1],
                                                     banks[b.bank][:].rearrange("p (m n) -> p m n", m=2), ALU.mult, ALU.mult), b)
                    if g:
                        split_rest(4, 2, g - 1)
                refills((i, "wo"), True)
                source[:] = items[i, "wo"], None

            def attn_64(tag, heads, mask=None, dst=None, scale=None, natural=lambda x: x):
                S, TT, O = items[tag, "S"], items[tag, "T"], items[tag, "O"]
                w = T * len(TT[0])
                for hd in range(heads + 5):
                    if hd < heads:
                        if mask is None:
                            done(S[hd][0])
                            v_.tensor_reduce(negmax[hd % 4][:], banks[S[hd][0].bank][:].rearrange("p (m n) -> p m n", m=2),
                                             AX.X, ALU.max, negate=True).then_inc(negmax_ready, 1)
                        else:
                            e = expo[hd % 3]
                            if hd >= 3:
                                for it in TT[hd - 3]:
                                    done(it)
                            for n, s in enumerate(S[hd]):
                                done(s)
                                c = slice(512 * n, 512 * (n + 1))
                                if scale is None:
                                    free(v_.tensor_tensor(e[:, c], banks[s.bank][:], mask[:, c], ALU.add), s)
                                else:
                                    free(v_.scalar_tensor_tensor(e[:, c], banks[s.bank][:], scale, mask[:, c], ALU.mult,
                                                                 ALU.add), s)
                            for s in S[hd]:
                                freed(s)
                            v_.tensor_reduce(negmax[hd % 4][:], e[:, 0:NT * w].rearrange("p (t n) -> p t n", t=NT), AX.X,
                                             ALU.max, negate=True).then_inc(negmax_ready, 1)
                    if 1 <= hd <= heads:
                        g = hd - 1
                        if mask is None:
                            freed(S[g][0])
                        else:
                            dve.wait_ge(exp_ready, count(exp_ready))
                        link(v_.reciprocal(erec[g % 4][:], esum[g % 4][:]))
                        for tt in range(NT):
                            e = expo[g % 3][:, w * tt:w * (tt + 1)]
                            ins = v_.tensor_scalar(e, e, erec[g % 4][:, tt:tt + 1], None, ALU.mult)
                        ins.then_inc(probs_ready, 1)
                    if hd >= 5 and hd % 4 == 0:
                        g = (hd - 5) // 4
                        dve.wait_ge(hi_part, count(hi_part))
                        a, b = dst or (h_hi, h_lo)
                        hi, lo = (natural(x[:, 2 * g:2 * g + 2, :]) for x in (a, b))
                        src = banks[O[g].bank][:].rearrange("p (m n) -> p m n", m=2)
                        if len(hi.shape) == 4:
                            src = src.rearrange("p m (c u) -> p m c u", c=4)
                        free(v_.tensor_tensor(lo, src, hi.bitcast(F32), ALU.subtract), O[g])

            def attn_b(i):
                us = items[i, "units"]
                deviations()
                refill(us[0])
                spread_out(hT[:, 7, :])
                for n, x in enumerate(items[i, "raw"]):
                    done(x)
                    if n < 2:
                        free(v_.tensor_tensor(latT[:, 2 * n:2 * n + 2, :], banks[x.bank][:].rearrange("p (m n) -> p m n", m=2),
                                              hT[:, 7, :].unsqueeze(1).to_broadcast([P, 2, T]), ALU.mult), x)
                        if n == 1:
                            refill(us[1])
                    else:
                        v_.tensor_tensor(latT[:, 4, :], banks[x.bank][:, 0:T], hT[:, 7, :], ALU.mult)
                        free(v_.tensor_tensor(pre[2][64:96, 0:T], banks[x.bank][64:96, T:2 * T], hT[64:96, 7, :], ALU.mult), x)
                s, b = items[i, "stat"]
                freed(s)
                v_.reciprocal(rs[:, 0:4], std[:, 0:4]).then_inc(rs_ready, 1)
                done(b)
                for k in range(7):
                    if k < 5:
                        at = ROW["b_q_norm"] + k
                        a = 0 if k < 3 else T
                        v_.scalar_tensor_tensor(hT[:, k, :], latT[:, k, :], pcol[:, at:at + 1], banks[b.bank][:, a:a + T],
                                                ALU.mult, ALU.mult).then_inc(to_split, 1)
                    if k >= 2:
                        split_rest(5, 1, k - 2)
                refill(us[2])
                rotate(0, items[i, "raw"][2], items[i, "krot"], kr[64:96, :].unsqueeze(1), tab[:, 2, :], tab[:, 3, :],
                       lo=64, hi=96, tiles=1, ready=kr_ready)
                for n, (x, r) in enumerate(zip(items[i, "qk"], items[i, "rot"])):
                    if n % 2 == 0:
                        if n:
                            refill(us[2 + n // 2])
                    rotate(n + 1, x, r, qT[0:96, 2 * n:2 * n + 2, :], tab[:, 2, :], tab[:, 3, :], hi=96)
                for u in us[6:9]:
                    refill(u)
                attn_64(i, B_HEADS)
                refills((i, "wo"), True)
                source[:] = items[i, "wo"], None

            def attn_c(i):
                us, xs, rr = items[i, "units"], items[i, "qk"], items[i, "rot"]
                deviations()
                spread_out(hT[:, 0:2, :], tab[:, 4:6, :])
                with dve.Fori(0, C_GROUPS) as g:
                    for n, u in enumerate(us):
                        refill(u, g)
                        if 1 <= n <= 8:
                            m = n - 1
                            dst = (qT if m < 4 else kT)[:, bass.ds(g * 8 + 2 * (m % 4), 2), :]
                            rotate(m, xs[m], rr[m], dst, hT[:, 0, :], hT[:, 1, :], i=g)
                dve.wait_ge(cmask_landed, 16)
                attn_64(i, C_HEADS, mask=cmask, natural=lambda x: x.rearrange("p m (u c) -> p m c u", c=4))
                refills((i, "wo"), True)
                source[:] = items[i, "wo"], None

            def ffn(tag, before):
                head, body, tail = items[tag, "up"]
                g0 = count(gate_ready, FT) - FT

                def step(j, n, u, x, i=None):
                    done(x, i)
                    free(v_.tensor_tensor(pre[j].rearrange("p (m n) -> p m n", m=2),
                                          banks[x.bank][:].rearrange("p (m n) -> p m n", m=2),
                                          hT[:, 4, :].unsqueeze(1).to_broadcast([P, 2, T]), ALU.mult), x)
                    refill(u, i)
                    k = g0 + n + 1
                    dve.wait_ge(gate_ready, k if i is None else i * 3 + k)
                    k = before + n + 1
                    dve.wait_ge(hidden_ready, k if i is None else i * 3 + k)
                    v_.tensor_tensor(hT[:, j, :], pre[j][:, T:2 * T], pre[j][:, 0:T], ALU.mult).then_inc(product_ready, 1)

                deviations()
                spread_out(hT[:, 4, :])

                for j, (u, x) in enumerate(head):
                    step(j, j, u, x)
                with dve.Fori(1, 7) as i:
                    for j, (u, x) in enumerate(body):
                        step(j, j, u, x, i)
                for u, x in tail:
                    step(0, FT - 1, u, x)
                refills((tag, "down"), True)
                source[:] = items[tag, "down"], None

            def ln(tag, last):
                m, v = items[tag]
                for j in range(4):
                    add_pair(j)
                done(m)
                for j in range(4):
                    xs = xT[:, 2 * j:2 * j + 2, :]
                    ins = v_.scalar_tensor_tensor(xs, banks[m.bank][:, 0:T].unsqueeze(1).to_broadcast([P, 2, T]), -1.0 / D,
                                                  xs, ALU.mult, ALU.add)
                    if j < 3:
                        ins.then_inc(centred, 1)
                    else:
                        free(ins, m)
                freed(v)
                link(v_.reciprocal(sq[:, 1, :], sq[:, 0, :]))
                at, ab = ROW[tag[0]] + tag[2], ROW[tag[1]] + tag[2]
                count(ln_ready, KT)
                for k in range(KT + 2):
                    if k < KT:
                        v_.scalar_tensor_tensor(hT[:, k, :], xT[:, k, :], pcol[:, at + k:at + k + 1], sq[:, 1, :],
                                                ALU.mult, ALU.mult).then_inc(ln_ready, 1)
                    if k >= 2 and not last:
                        dve.wait_ge(hi_part, count(hi_part))
                        v_.scalar_tensor_tensor(h_lo[:, k - 2, :], hT[:, k - 2, :], pcol[:, ab + k - 2:ab + k - 1],
                                                h_hi[:, k - 2, :].bitcast(F32), ALU.add, ALU.subtract).then_inc(h_ready, 1)
                source[0] = None
                if late:
                    refill(late.pop())

            def mix(l):
                it = items["m", l]
                us = it["units"]
                link(v_.memset(pool_u[:, :, 0:PADW], 0.0))
                taps = None
                def convolve():
                    dve.wait_ge(glu_ready, l + 1)
                    cw, cb = ROW["conv_dw_w_2"] + l * CONV_W * 2 + 1, ROW["conv_dw_b_2"] + 2 * l + 1
                    y = conv_y[:, 1, :]
                    for j in range(CONV_W):
                        hh = conv_h[:, 1, PADW - CONV_W + 1 + j:PADW - CONV_W + 1 + j + T]
                        wj = pcol[:, cw + 2 * j:cw + 2 * j + 1]
                        if j == 0:
                            link(v_.tensor_scalar(y, hh, wj, pcol[:, cb:cb + 1], ALU.mult, ALU.add))
                        elif j < CONV_W - 1:
                            link(v_.scalar_tensor_tensor(y, hh, wj, y, ALU.mult, ALU.add))
                        else:
                            v_.scalar_tensor_tensor(y, hh, wj, y, ALU.mult, ALU.add).then_inc(conv_out, 1)
                        if j % 2:
                            yield

                def pools():
                    end = T + PADW
                    freed(it["pool"])
                    dve.wait_ge(glu_ready, l + 1)
                    link(v_.tensor_tensor(pool_w2[:, :, 1:], pool_u[:, :, 1:], pool_u[:, :, :end - 1], ALU.add))
                    link(v_.tensor_tensor(pool_w4[:, :, 3:], pool_w2[:, :, 3:], pool_w2[:, :, 1:end - 2], ALU.add))
                    v_.tensor_tensor(mixed[0:64, 0, :], pool_w2[0:64, 0, PADW:], inv_cnt[0:64, 0, :], ALU.mult)
                    link(v_.tensor_tensor(pool_w2[:, 1, 7:], pool_w4[:, 1, 7:], pool_w4[:, 1, 3:end - 4], ALU.add))
                    v_.tensor_tensor(mixed[64:128, 0, :], pool_w4[64:128, 0, PADW:], inv_cnt[64:128, 0, :], ALU.mult)
                    v_.tensor_tensor(mixed[0:64, 1, :], pool_w2[0:64, 1, PADW:], inv_cnt[0:64, 1, :], ALU.mult)
                    link(v_.tensor_tensor(pool_w4[64:128, 1, 15:], pool_w2[64:128, 1, 15:], pool_w2[64:128, 1, 7:end - 8], ALU.add))
                    link(v_.tensor_tensor(mixed[64:128, 1, :], pool_w4[64:128, 1, PADW:], inv_cnt[64:128, 1, :], ALU.mult))
                    v_.tensor_tensor(mixed[:], mixed[:], pool_u[:, :, PADW:], ALU.subtract).then_inc(mixed_ready, 1)

                for u in us[0:4]:
                    refill(u)
                dsts = (kidT.unsqueeze(1), qiT[:, 0:2, :], qiT[:, 2:4, :], kdT, qD[:, 0:2, :], qD[:, 2:4, :])
                for n, (x, r, dst) in enumerate(zip(it["qk"], it["rot"], dsts)):
                    refill(us[4 + n])
                    rotate(n, x, r, dst, tabd[:, 0, :], tabd[:, 1, :], tiles=2 if n else 1)
                    taps = taps or convolve()
                    next(taps, None)
                freed(it["v"])
                base = NT * IDX_HEADS * l
                for n, s in enumerate(it["idx"]):
                    freed(s)
                    for tt in range(NT):
                        src, wh = relu[n % 2][:, tt * T:(tt + 1) * T], wi[:, tt, n:n + 1]
                        if n == 0:
                            v_.tensor_scalar(score[:, tt, :], src, wh, None, ALU.mult).then_inc(score_step, 1)
                        else:
                            dve.wait_ge(score_step, base + 2 * n + tt - 1)
                            v_.scalar_tensor_tensor(score[:, tt, :], src, wh, score[:, tt, :], ALU.mult,
                                                    ALU.add).then_inc(score_step, 1)

                def topk():
                    for tt in range(NT):
                        dve.wait_ge(score_masked, count(score_masked))
                        src = score[:, tt, :]
                        for _ in range(TOPK // 8):
                            link(v_.max(m8[:], src))
                            link(v_.match_replace(work[:, tt, :], m8[:], src, TAKEN))
                            src = work[:, tt, :]
                            yield
                        link(v_.tensor_scalar(src, src, TAKEN, 1.0, ALU.is_equal, ALU.subtract))
                        v_.tensor_scalar(src, src, -NEG, None, ALU.mult).then_inc(picked, 1)
                        yield

                search = topk()
                def rest_of(j):
                    u = it["gates"][j % 3][0]
                    rest(u.slot, u.index + 3 * (j // 3) + SLOTS + 1)

                for j in range(11):
                    rest_of(j)
                    for _ in range(2):
                        next(search, None)
                    if j == 8:
                        pools()
                    next(taps, None)
                for part in (search, taps):
                    for _ in part:
                        pass
                x = it["poolmix"]
                done(x)
                at = ROW["pool_scale_2"] + 2 * l
                for m in range(2):
                    ins = v_.tensor_scalar(mixed[:, m, :], banks[x.bank][:, m * T:(m + 1) * T], pcol[:, at + m:at + m + 1],
                                           None, ALU.mult)
                free(ins, x)
                freed(x)
                link(v_.tensor_copy(pool_hi[:], mixed[:]))
                v_.tensor_tensor(pool_lo[:], mixed[:], pool_hi[:].bitcast(F32), ALU.subtract).then_inc(branch_ready, 1)
                s, m_, v, b = it["cln"]
                done(s)
                free(v_.tensor_scalar(rs[:, 0:2], banks[s.bank][:, 0:2], -1.0 / 256, None, ALU.mult), s)
                done(m_)
                v_.tensor_tensor(conv_y[:], conv_y[:], banks[m_.bank][:, 0:T].unsqueeze(1).to_broadcast([P, 2, T]),
                                 ALU.add).then_inc(centred, 1)
                rest_of(11)
                freed(v)
                v_.reciprocal(rs[:, 0:2], std[:, 0:2]).then_inc(rs_ready, 1)
                done(b)
                at = ROW["conv_ln_g_2"] + 2 * l
                count(ln_ready, 2)
                for m in range(2):
                    v_.scalar_tensor_tensor(conv_y[:, m, :], conv_y[:, m, :], pcol[:, at + m:at + m + 1],
                                            banks[b.bank][:, 0:T], ALU.mult, ALU.mult).then_inc(ln_ready, 1)
                dve.wait_ge(hi_part, count(hi_part))
                v_.tensor_tensor(conv_lo[:], conv_y[:], conv_hi[:].bitcast(F32), ALU.subtract).then_inc(branch_ready, 1)
                dve.wait_ge(keep_ready, count(keep_ready, NT))
                tag = ("m", l)
                attn_64(tag, N_HEADS, mask=work.rearrange("p t n -> p (t n)"), dst=(attn_hi, attn_lo),
                        scale=HD ** -0.5)
                for br, name in enumerate(("pool", "conv", "attn")):
                    refills((tag, name), name == "attn")
                    for m, x in enumerate(items[tag, name]):
                        done(x)
                        dst = hT[:, 2 * m:2 * m + 2, :]
                        tmp = rot[m % 2][:].rearrange("p (m n) -> p m n", m=2)
                        b = banks[x.bank][:].rearrange("p (m n) -> p m n", m=2)
                        g = gates[:, 8 * br + 2 * m:8 * br + 2 * m + 2, :]
                        free(v_.tensor_tensor(dst if br == 0 else tmp, b, g, ALU.mult), x)
                        if br:
                            freed(x)
                            ins = v_.tensor_tensor(dst, dst, tmp, ALU.add)
                            if br == 2:
                                ins.then_inc(to_split, 1)
                            else:
                                link(ins)
                        if br == 2 and m:
                            split_rest(4, 2, m - 1)
                split_rest(4, 2, 3)
                refill(late.pop())
                refills((tag, "wo"), True)
                source[:] = items[tag, "wo"], ALPHA

            def ffn2(tag, l, before):
                head, body, tail = items[tag, "up"]
                w = ROW["ffn_dw_w_2"] + l * FCW * 44
                started0 = 22 * l
                g0 = count(gate_ready, FT) - FT
                chain0 = steps[0]

                def step(n, j, u, x, i=None):
                    def col(at):
                        return pcol[:, at:at + 1] if i is None else pcol[:, bass.ds(i * 3 + at, 1)]

                    if i is not None or n:
                        make((j - 1) % 3, n - 1, i)
                    done(x, i)
                    at = started0 + n + 1
                    dve.wait_ge(taps_started, at if i is None else i * 3 + at)
                    for m, tile in ((0, 0), (1, 22)):
                        o, b = pre[j][:, m * T:(m + 1) * T], banks[x.bank][:, m * T:(m + 1) * T]
                        v_.scalar_tensor_tensor(o[:, 1:], b[:, :T - 1], col(w + 44 + tile + n), o[:, 1:], ALU.mult,
                                                ALU.add).then_inc(dve_step, 1)
                    for m, tile in ((0, 0), (1, 22)):
                        o, b = pre[j][:, m * T:(m + 1) * T], banks[x.bank][:, m * T:(m + 1) * T]
                        at = chain0 + 2 * n + m + 1
                        dve.wait_ge(dve_step, at if i is None else i * 6 + at)
                        ins = v_.scalar_tensor_tensor(o[:, 2:], b[:, :T - 2], col(w + tile + n), o[:, 2:], ALU.mult, ALU.add)
                    free(ins, x)
                    refill(u, i)

                def make(j, n, i):
                    at = g0 + n + 1
                    dve.wait_ge(gate_ready, at if i is None else i * 3 + at)
                    at = before + n + 1
                    dve.wait_ge(hidden_ready, at if i is None else i * 3 + at)
                    v_.tensor_tensor(hT[:, j, :], pre[j][:, 0:T], pre[j][:, T:2 * T], ALU.mult).then_inc(product_ready, 1)

                for j, (u, x) in enumerate(head):
                    step(j, j, u, x)
                with dve.Fori(1, 7) as i:
                    for j, (u, x) in enumerate(body):
                        step(j, j, u, x, i)
                for u, x in tail:
                    step(FT - 1, 0, u, x)
                make(0, FT - 1, None)
                steps[0] += 44
                refills((tag, "down"), True)
                source[:] = items[tag, "down"], ALPHA

            n_ffn = 0
            for kind, arg in phases():
                if kind == "start":
                    start()
                elif kind == "lambda":
                    lambdas()
                elif kind == "second":
                    second()
                elif kind == "rms":
                    c = "ABC"[arg[0] % 3] if arg[1] == "attn_norm" else None
                    rms(arg, ROW[arg[1]] + arg[2], c)
                elif kind == "A":
                    attn_a(arg)
                elif kind == "B":
                    attn_b(arg)
                elif kind == "C":
                    attn_c(arg)
                elif kind == "ffn":
                    ffn(("ffn", arg), FT * n_ffn)
                    n_ffn += 1
                elif kind == "rows2":
                    rows2()
                elif kind == "final":
                    final()
                    source[0] = None
                elif kind in ("ln", "ln_last"):
                    ln(arg, kind == "ln_last")
                elif kind == "mix":
                    mix(arg)
                elif kind == "ffn2":
                    ffn2(("ffn2", arg), arg, FT * n_ffn)
                    n_ffn += 1
                elif kind == "end":
                    if source[0]:
                        for j in range(4):
                            add_pair(j)
                    for n, x in enumerate(items["end"]):
                        done(x)
                        free(v_.tensor_copy(xrows[:, n % 2, (n // 2) * 512:(n // 2 + 1) * 512], banks[x.bank][:]), x)


def lambda_init(i):
    return 0.8 - 0.6 * math.exp(-0.3 * i)


TWO_PI = (6.28125, float(np.float32(0.0019340515136718750)),
          2 * math.pi - 6.28125 - float(np.float32(0.0019340515136718750)))
MAGIC = 12582912.0
PI_IN = 3.1415925


def constants():
    f = np.float32

    def rope(rot_dim):
        pos = np.arange(T, dtype=f)
        inv = (f(500000.0) ** (-np.arange(0, rot_dim, 2, dtype=f) / f(rot_dim))).astype(f)
        ang = (pos[:, None] * inv[None, :]).astype(f)
        return np.cos(ang).astype(f), np.sin(ang).astype(f)

    def tables(cos, sin, starts, rows):
        r = cos.shape[1]
        c, s = np.ones((P, T), f), np.zeros((P, T), f)
        for a in starts:
            for z in range(2):
                c[a + z * r:a + (z + 1) * r] = cos.T
                s[a + z * r:a + (z + 1) * r] = sin.T
        return c, s

    def swap(starts, r):
        w = np.zeros((P, P), f)
        for a in starts:
            for d in range(r):
                w[a + r + d, a + d] = -1.0
                w[a + d, a + r + d] = 1.0
        return w

    ca, sa = tables(*rope(16), (0, 64), P)
    cb, sb_ = tables(*rope(32), (64,), P)
    order = np.arange(T).reshape(T // 4, 4).T.reshape(T)
    tab = np.stack([ca, sa, cb, sb_, ca[:, order], sa[:, order]], 1)
    rotm = np.stack([swap((0, 64), 8), swap((64,), 16), swap((0, 64), 32)], 1)
    cmask = np.empty((P, NT, 4 * P), f)
    for tt in range(NT):
        own = order[tt * P:(tt + 1) * P]
        near = np.abs(own[:, None] - order[None, :]) <= 64
        apart = own[:, None] - own[None, :]
        cmask[:, tt] = np.where(np.concatenate([near, apart % 4 == 0, apart % 16 == 0], 1), f(0), f(NEG))
    cnt = np.zeros((P, 2, T), f)
    for g, win in enumerate(POOL_WINDOWS):
        cnt[HD * (g % 2):HD * (g % 2) + HD, g // 2] = 1.0 / np.minimum(np.arange(T) + 1, win)
    invf = f(10000.0) ** (-np.arange(32, dtype=f) / f(32))
    return {"c_tab": tab, "c_rotm": rotm, "c_cmask": cmask.reshape(P, NT * 4 * P), "c_inv_cnt": cnt,
            "c_invf": np.tile(invf.astype(f), 4)[:, None]}


_INS = ["x", "attn_norm", "ffn_norm", "final_norm", "a_w_qkv", "a_lambda_q1", "a_lambda_k1", "a_lambda_q2",
        "a_lambda_k2", "a_subln", "a_w_o", "b_w_a", "b_q_norm", "b_kv_norm", "b_w_qb", "b_w_kvb", "b_w_o",
        "c_w_qkv", "c_w_o", "f_w_gu", "f_w_out", "positions_2", "ln_in_g_2", "ln_in_b_2", "w_in_2", "b_in_2",
        "pool_w_2", "pool_scale_2", "w_pool_out_2", "conv_dw_w_2", "conv_dw_b_2", "conv_ln_g_2", "conv_ln_b_2",
        "w_conv_out_2", "w_attn_out_2", "w_o_2", "ln1_g_2", "ln1_b_2", "w_up_2", "ffn_dw_w_2", "ffn_dw_b_2",
        "w_down_2", "ln2_g_2", "ln2_b_2"]


def kernel(**inputs):
    import concourse.bacc as bacc
    from concourse.bass_utils import run_bass_kernel_spmd

    nc = bacc.Bacc("TRN2", target_bir_lowering=False, num_devices=1)
    arrays, t = {}, {}
    for name, a in [*((n, inputs[n]) for n in _INS), *constants().items()]:
        a = np.ascontiguousarray(a)
        arrays[f"in_{name}"] = a
        t[name] = nc.dram_tensor(f"in_{name}", a.shape, mybir.dt.from_np(a.dtype), kind="ExternalInput").ap()
    t["out"] = nc.dram_tensor("out", (1, T, D), F32, kind="ExternalOutput").ap()
    build(nc, t)
    r = run_bass_kernel_spmd(nc, [arrays], core_ids=[0])
    return r.results[0]["out"]
```
